# Optimizing a Trainium2 kernel written in Bass

```python
import jax, jax.numpy as jnp
from jax import lax
import numpy as np

D_MODEL = 1024
BATCH = 1
SEQ = 512
DEPTH = 1
DEC_BATCH = 8
DEC_SEQ = 4
PAST_LEN = 2048
PAGE_SIZE = 128

LRU_WIDTH = D_MODEL // 2
LRU_BLOCKS = 8
LRU_BLOCK_W = LRU_WIDTH // LRU_BLOCKS
CONV_W = 4
RG_C = 8.0
ATTN_WIDTH = D_MODEL - LRU_WIDTH
HEAD_DIM = 64
N_HEADS = ATTN_WIDTH // HEAD_DIM
IDX_HEADS = 8
IDX_DIM = 64
TOPK_MAX = 256
QBLOCK = 128
D_FF = 4 * D_MODEL
ROPE_THETA = 10000.0
EPS = 1e-6
PROJ_SIZES = (LRU_WIDTH, LRU_WIDTH, ATTN_WIDTH, ATTN_WIDTH, ATTN_WIDTH, IDX_HEADS * IDX_DIM, IDX_DIM, IDX_HEADS)
D_IN_PROJ = sum(PROJ_SIZES)

kernel_name = 'hymba_rglru_dsa_step'

def _rmsnorm(x, g):
    xf = x.astype(jnp.float32)
    y = xf * lax.rsqrt(jnp.mean(xf * xf, axis=-1, keepdims=True) + EPS)
    return (y * g.astype(jnp.float32)).astype(x.dtype)

def _rope(x, pos):
    half = x.shape[-1] // 2
    freq = ROPE_THETA ** (-jnp.arange(half, dtype=jnp.float32) / half)
    ang = pos.astype(jnp.float32)[:, None] * freq[None, :]
    cos = jnp.cos(ang)[:, None, :]
    sin = jnp.sin(ang)[:, None, :]
    xf = x.astype(jnp.float32)
    x1, x2 = xf[..., :half], xf[..., half:]
    return jnp.concatenate([x1 * cos - x2 * sin, x2 * cos + x1 * sin], axis=-1).astype(x.dtype)

def _split_proj(z):
    out = []
    s = 0
    for n in PROJ_SIZES:
        out.append(z[..., s:s + n])
        s += n
    return out

def _rglru(xb, conv_buf, h0, conv_w, conv_b, w_a, b_a, w_i, b_i, lam):
    B, T, W = xb.shape
    xp = jnp.concatenate([conv_buf.astype(xb.dtype), xb], axis=1)
    xc = conv_b + xp[:, 0:T] * conv_w[0]
    for j in range(1, CONV_W):
        xc = xc + xp[:, j:j + T] * conv_w[j]
    new_buf = xp[:, T:]
    xblk = xc.reshape(B, T, LRU_BLOCKS, LRU_BLOCK_W)
    r = jax.nn.sigmoid(jnp.einsum('btnc,ncd->btnd', xblk, w_a).reshape(B, T, W) + b_a)
    i = jax.nn.sigmoid(jnp.einsum('btnc,ncd->btnd', xblk, w_i).reshape(B, T, W) + b_i)
    log_a = -RG_C * jax.nn.softplus(-lam.astype(jnp.float32)) * r.astype(jnp.float32)
    a = jnp.exp(log_a)
    u = jnp.sqrt(-jnp.expm1(2.0 * log_a)) * (i * xc).astype(jnp.float32)

    def step(h, au):
        a_t, u_t = au
        h = a_t * h + u_t
        return h, h

    hT, hs = lax.scan(step, h0.astype(jnp.float32), (jnp.swapaxes(a, 0, 1), jnp.swapaxes(u, 0, 1)))
    return jnp.swapaxes(hs, 0, 1).astype(xb.dtype), hT.astype(xb.dtype), new_buf

def _index_scores(qi, wi, ki):
    dots = jnp.einsum('...thd,...sd->...ths', qi.astype(jnp.float32), ki.astype(jnp.float32)) * (IDX_DIM ** -0.5)
    return jnp.einsum('...ths,...th->...ts', jax.nn.relu(dots), wi.astype(jnp.float32)) * (IDX_HEADS ** -0.5)

def _sparse_attend(q, kg, vg, valid):
    s = jnp.einsum('...thd,...tkhd->...thk', q.astype(jnp.float32), kg.astype(jnp.float32)) * (HEAD_DIM ** -0.5)
    s = jnp.where(valid[..., :, None, :], s, -jnp.inf)
    p = jax.nn.softmax(s, axis=-1)
    return jnp.einsum('...thk,...tkhd->...thd', p.astype(vg.dtype), vg)

def _dsa_prompt(q, k, v, qi, ki, wi):
    B, S = q.shape[0], q.shape[1]
    nb = S // QBLOCK
    kk = min(TOPK_MAX, S // 4)
    qb = q.reshape(B, nb, QBLOCK, N_HEADS, HEAD_DIM)
    qib = qi.reshape(B, nb, QBLOCK, IDX_HEADS, IDX_DIM)
    wib = wi.reshape(B, nb, QBLOCK, IDX_HEADS)
    kpos = jnp.arange(S)

    def block(n):
        b = n // nb
        j = n % nb
        qpos = j * QBLOCK + jnp.arange(QBLOCK)
        sc = _index_scores(qib[b, j], wib[b, j], ki[b])
        sc = jnp.where(kpos[None, :] <= qpos[:, None], sc, -jnp.inf)
        _, idx = lax.top_k(sc, kk)
        valid = idx <= qpos[:, None]
        return _sparse_attend(qb[b, j], k[b][idx], v[b][idx], valid)

    o = lax.map(block, jnp.arange(B * nb))
    return o.reshape(B, S, N_HEADS, HEAD_DIM)

def _dsa_sample(q, k_new, v_new, qi, ki_new, wi, cache_k, cache_v, cache_kidx, page_table):
    DB, T = q.shape[0], q.shape[1]
    L = PAST_LEN + T
    kk = min(TOPK_MAX, L // 4)
    ki_past = cache_kidx[page_table].reshape(DB, PAST_LEN, IDX_DIM)
    ki_all = jnp.concatenate([ki_past.astype(ki_new.dtype), ki_new], axis=1)
    qpos = PAST_LEN + jnp.arange(T)
    kpos = jnp.arange(L)
    sc = _index_scores(qi, wi, ki_all)
    sc = jnp.where(kpos[None, None, :] <= qpos[None, :, None], sc, -jnp.inf)
    _, idx = lax.top_k(sc, kk)
    valid = idx <= qpos[None, :, None]
    is_past = (idx < PAST_LEN)[..., None, None]
    pidx = jnp.minimum(idx, PAST_LEN - 1)
    bidx = jnp.arange(DB)[:, None, None]
    phys = page_table[bidx, pidx // PAGE_SIZE]
    off = pidx % PAGE_SIZE
    nidx = jnp.clip(idx - PAST_LEN, 0, T - 1)
    kg = jnp.where(is_past, cache_k[phys, off].astype(q.dtype), k_new[bidx, nidx])
    vg = jnp.where(is_past, cache_v[phys, off].astype(q.dtype), v_new[bidx, nidx])
    return _sparse_attend(q, kg, vg, valid)

def _layer(x, pos, conv_buf, h0, attend, g_pre_mix, w_in, conv_w, conv_b, w_a, b_a, w_i, b_i, lam,
           w_out, g_post_mix, g_pre_ffn, w_ff1, w_ff2, g_post_ffn):
    B, T, _ = x.shape
    hn = _rmsnorm(x, g_pre_mix)
    xl, gate, q, k, v, qi, ki, wi = _split_proj(hn @ w_in)
    q = _rope(q.reshape(B, T, N_HEADS, HEAD_DIM), pos)
    k = _rope(k.reshape(B, T, N_HEADS, HEAD_DIM), pos)
    v = v.reshape(B, T, N_HEADS, HEAD_DIM)
    qi = _rope(qi.reshape(B, T, IDX_HEADS, IDX_DIM), pos)
    ki = _rope(ki[:, :, None, :], pos)[:, :, 0, :]
    lru, hT, new_buf = _rglru(xl, conv_buf, h0, conv_w, conv_b, w_a, b_a, w_i, b_i, lam)
    att = attend(q, k, v, qi, ki, wi)
    mix = jnp.concatenate([lru * jax.nn.gelu(gate), att.reshape(B, T, ATTN_WIDTH)], axis=-1) @ w_out
    x = x + _rmsnorm(mix, g_post_mix)
    f = jnp.square(jax.nn.relu(_rmsnorm(x, g_pre_ffn) @ w_ff1)) @ w_ff2
    x = x + _rmsnorm(f, g_post_ffn)
    return x, (k, v, ki, hT, new_buf)

def setup_inputs(seed: int = 0) -> dict:
    key = jax.random.key(seed)
    ks = jax.random.split(key, 24)
    n_pages = PAST_LEN // PAGE_SIZE
    n_pool = (DEC_BATCH * n_pages * 5) // 4
    nrm = lambda k, shape, s: jax.random.normal(k, shape, jnp.float32) * s
    page_table = jax.random.permutation(ks[0], n_pool)[:DEC_BATCH * n_pages].reshape(DEC_BATCH, n_pages).astype(jnp.int32)
    u = jax.random.uniform(ks[1], (DEPTH, LRU_WIDTH), jnp.float32, 0.9, 0.999)
    a0 = u ** (1.0 / RG_C)
    lam = jnp.log(a0 / (1.0 - a0))
    return {
        'x_prompt': nrm(ks[2], (BATCH, SEQ, D_MODEL), 1.0),
        'x_sample': nrm(ks[3], (DEC_BATCH, DEC_SEQ, D_MODEL), 1.0),
        'cache_k': nrm(ks[4], (DEPTH, n_pool, PAGE_SIZE, N_HEADS, HEAD_DIM), 1.0),
        'cache_v': nrm(ks[5], (DEPTH, n_pool, PAGE_SIZE, N_HEADS, HEAD_DIM), 1.0),
        'cache_kidx': nrm(ks[6], (DEPTH, n_pool, PAGE_SIZE, IDX_DIM), 1.0),
        'state_h': nrm(ks[7], (DEPTH, DEC_BATCH, LRU_WIDTH), 0.5),
        'state_conv': nrm(ks[8], (DEPTH, DEC_BATCH, CONV_W - 1, LRU_WIDTH), 1.0),
        'page_table': page_table,
        'g_pre_mix': 1.0 + nrm(ks[9], (DEPTH, D_MODEL), 0.02),
        'w_in': nrm(ks[10], (DEPTH, D_MODEL, D_IN_PROJ), D_MODEL ** -0.5),
        'conv_w': nrm(ks[11], (DEPTH, CONV_W, LRU_WIDTH), CONV_W ** -0.5),
        'conv_b': nrm(ks[12], (DEPTH, LRU_WIDTH), 0.01),
        'w_a': nrm(ks[13], (DEPTH, LRU_BLOCKS, LRU_BLOCK_W, LRU_BLOCK_W), LRU_BLOCK_W ** -0.5),
        'b_a': nrm(ks[14], (DEPTH, LRU_WIDTH), 0.01),
        'w_i': nrm(ks[15], (DEPTH, LRU_BLOCKS, LRU_BLOCK_W, LRU_BLOCK_W), LRU_BLOCK_W ** -0.5),
        'b_i': nrm(ks[16], (DEPTH, LRU_WIDTH), 0.01),
        'lam': lam,
        'w_out': nrm(ks[17], (DEPTH, D_MODEL, D_MODEL), D_MODEL ** -0.5),
        'g_post_mix': 1.0 + nrm(ks[18], (DEPTH, D_MODEL), 0.02),
        'g_pre_ffn': 1.0 + nrm(ks[19], (DEPTH, D_MODEL), 0.02),
        'w_ff1': nrm(ks[20], (DEPTH, D_MODEL, D_FF), D_MODEL ** -0.5),
        'w_ff2': nrm(ks[21], (DEPTH, D_FF, D_MODEL), D_FF ** -0.5),
        'g_post_ffn': 1.0 + nrm(ks[22], (DEPTH, D_MODEL), 0.02),
    }

def reference(x_prompt, x_sample, cache_k, cache_v, cache_kidx, state_h, state_conv, page_table,
              g_pre_mix, w_in, conv_w, conv_b, w_a, b_a, w_i, b_i, lam, w_out, g_post_mix,
              g_pre_ffn, w_ff1, w_ff2, g_post_ffn):
    B, S, _ = x_prompt.shape
    DB, T, _ = x_sample.shape
    pos_p = jnp.arange(S)
    pos_s = PAST_LEN + jnp.arange(T)
    xp, xs = x_prompt, x_sample
    p_states, s_states = [], []
    for l in range(DEPTH):
        lw = (g_pre_mix[l], w_in[l], conv_w[l], conv_b[l], w_a[l], b_a[l], w_i[l], b_i[l], lam[l],
              w_out[l], g_post_mix[l], g_pre_ffn[l], w_ff1[l], w_ff2[l], g_post_ffn[l])
        xp, sp = _layer(xp, pos_p, jnp.zeros((B, CONV_W - 1, LRU_WIDTH), xp.dtype),
                        jnp.zeros((B, LRU_WIDTH), xp.dtype), _dsa_prompt, *lw)
        ck, cv, ci = cache_k[l], cache_v[l], cache_kidx[l]
        attend_s = lambda q, k, v, qi, ki, wi: _dsa_sample(q, k, v, qi, ki, wi, ck, cv, ci, page_table)
        xs, ss = _layer(xs, pos_s, state_conv[l], state_h[l], attend_s, *lw)
        p_states.append(sp)
        s_states.append(ss)
    k_prompt = jnp.stack([s[0] for s in p_states])
    v_prompt = jnp.stack([s[1] for s in p_states])
    kidx_prompt = jnp.stack([s[2] for s in p_states])
    h_prompt = jnp.stack([s[3] for s in p_states])
    conv_prompt = jnp.stack([s[4] for s in p_states])
    k_sample = jnp.stack([s[0] for s in s_states])
    v_sample = jnp.stack([s[1] for s in s_states])
    kidx_sample = jnp.stack([s[2] for s in s_states])
    h_sample = jnp.stack([s[3] for s in s_states])
    conv_sample = jnp.stack([s[4] for s in s_states])
    return (xp, xs, k_prompt, v_prompt, kidx_prompt, h_prompt, conv_prompt,
            k_sample, v_sample, kidx_sample, h_sample, conv_sample)


_drawn_inputs = setup_inputs


def setup_inputs(seed=0):
    import zlib

    import numpy as np

    out = dict(_drawn_inputs(seed))
    spreads = {}
    factors = {'b_a': 22.439, 'b_i': 8.0, 'g_post_mix': 10.704, 'g_pre_ffn': 39.181, 'g_post_ffn': 58.803}
    for name, (base, spread) in spreads.items():
        noise = np.random.default_rng([zlib.crc32(name.encode()), seed]).standard_normal(out[name].shape)
        drawn = base * np.exp(spread * noise) if base else spread * noise
        out[name] = __import__('jax').numpy.asarray(drawn.astype(out[name].dtype))
    for name, factor in factors.items():
        out[name] = (out[name] * factor).astype(out[name].dtype)
    return out
```

```python
from contextlib import ExitStack

import concourse.bass as bass
from concourse import mybir

P = 128
F32 = mybir.dt.float32
I32 = mybir.dt.int32
ALU = mybir.AluOpType
ACT = mybir.ActivationFunctionType
AX_X = mybir.AxisListType.X

D_MODEL = 1024
SEQ = 512
DEC_BATCH = 8
DEC_SEQ = 4
NS = DEC_BATCH * DEC_SEQ
NT = SEQ + NS
HALF = NT // 2
PAST = 2048
PAGE = 128
NPG = PAST // PAGE
NPOOL = DEC_BATCH * NPG * 5 // 4
WIDTH = 512
CT = WIDTH // P
NH = 8
HD = 64
KT = D_MODEL // P
D_FF = 4 * D_MODEL
FT = D_FF // P
QB = SEQ // P
TOPK_P = min(256, SEQ // 4)
TOPK_S = min(256, (PAST + DEC_SEQ) // 4)
NKEY = PAST + NS
GRP = DEC_BATCH // 4
EPS = 1e-6
RG_C = 8.0
OUT_OF_REACH = -1e30
TAKEN = -3e38
XW = 3 + SEQ + DEC_BATCH * (3 + DEC_SEQ)
SCALE = HD ** -0.5
IDX_SCALE = (HD ** -0.5) * (NH ** -0.5)

G_PRE_MIX, G_POST_MIX, G_PRE_FFN, G_POST_FFN = 0, 8, 16, 24
CONV_W0, CONV_B, B_A, B_I, LAM, H0, CONV0 = 32, 48, 52, 56, 60, 64, 96
NPAR = 192

BLOCKS = ["qi", "q", "k", "xl", "gate", "v", "wo0", "wo1"] + [f"f1_{i}" for i in range(8)] + [f"f2_{i}" for i in range(8)]
E_QI, E_KW, E_Q, E_K, E_XL, E_GATE, E_V, E_WO, E_F1, E_F2, E_END = 0, 8, 10, 18, 26, 34, 42, 47, 63, 127, 143
BLOCK_END = [E_KW, E_K, E_XL, E_GATE, E_V, E_WO, E_WO + 8, E_F1]
SCP_AT = {1: 0, 2: 256, 3: 640}
KSTEPS = GRP * NPG
ATT_UNITS = QB * NH
LRU_STEPS = 3


def build(nc, xT_d, par_d, w_in_d, w_kw_d, w_out_d, w_ff1_d, w_ff2_d, wgate_d, ck_d, cv_d, ci_d, steps_d, ptT_d,
          ident_d, rope_d, causal_d, ind_d, newmask_d, keyoff_d, yT_d, kT_d, v_d, kiT_d, lru_d):
    with ExitStack() as ctx:
        def sb(name, shape, dt=F32):
            return ctx.enter_context(nc.sbuf_tensor(name, shape, dt))

        def sem(name):
            return ctx.enter_context(nc.semaphore(name))

        bank = [ctx.enter_context(nc.psum_tensor(f"bank{i}", [P, 512], F32)) for i in range(8)]

        regX = sb("regX", [P, KT * NT])
        regR = sb("regR", [P, KT * NT])
        regM = sb("regM", [P, KT * NT])
        regQ = sb("regQ", [P, KT * NT])
        wring = sb("wring", [P, 2, 4096])
        arena = sb("arena", [P, 17872])
        lx = sb("lx", [P, 6 * NT])
        scp = sb("scp", [P, 1152])
        qbd = sb("qbd", [P, DEC_BATCH, CT, 32])
        kwrow = sb("kwrow", [P, 5, 72])
        wgate = sb("wgate", [P, 2, CT, P])
        ident = sb("ident", [P, P])
        ones = sb("ones", [P, P])
        causal = sb("causal", [P, P])
        ind = sb("ind", [NS, GRP, P])
        wT = sb("wT", [NS, GRP, P])
        wm = sb("wm", [P, GRP, NS])
        newmask = sb("newmask", [NS, NS])
        par = sb("par", [P, NPAR])
        keyoff = sb("keyoff", [P, 1])
        pt_own = sb("pt_own", [P, DEC_BATCH], I32)
        row_i = sb("row_i", [P, DEC_BATCH], I32)
        kw_diag = sb("kw_diag", [P, KT * 72])
        wkw = kw_diag[:, :].rearrange("p (k c) -> p k c", k=KT)
        diag = kw_diag[:, 0:4 * P].rearrange("p (s c) -> p s c", s=4)
        qi_s = sb("qi_s", [P, CT, NS])
        q_s = sb("q_s", [P, CT, NS])
        m8 = sb("m8", [P, 3, 8])
        pack = sb("pack", [P, CT, 36])
        sp = sb("sp", [P, 8 * CT])
        eps = sb("eps", [P, 1])
        steps = sb("steps", [1, KSTEPS * 4], I32)
        stat = sb("stat", [P, 4, 4])
        sstat = sb("sstat", [P, GRP, 8])

        def tiles(region, n=KT):
            return region[:, 0:n * NT].rearrange("p (k t) -> p k t", t=NT)

        xT = tiles(regX)
        hnT = tiles(regR)
        mixT = tiles(regM)
        sqT = tiles(regQ)
        oT = tiles(regR)
        fT = tiles(regM)
        hT = tiles(arena, FT)
        qz = regQ[:, 0:NH * SEQ].rearrange("p (h t) -> p h t", t=SEQ)
        kidxT = regX[:, 0:4096].rearrange("p (b c) -> p b c", b=4)
        S = regX[:, 0:GRP * NKEY].rearrange("p (g c) -> p g c", g=GRP)
        R = regM[:, 0:GRP * NKEY].rearrange("p (g c) -> p g c", g=GRP)
        work_s = regM[0:NS, 4 * NT:4 * NT + NKEY]
        work_p = regM[:, 4 * NT:4 * NT + 1152]
        pT = regR[:, 0:GRP * 17 * P].rearrange("p (g r c) -> p g r c", g=GRP, r=17)
        at = 0

        def carve(n):
            nonlocal at
            at += n
            return arena[:, at - n:at]

        kv = carve(3 * 2048).rearrange("p (s b c) -> p s b c", s=3, b=4)
        kidx_in_sb = arena[:, 0:4096].rearrange("p (b c) -> p b c", b=4)
        scs = carve(NKEY)[0:NS, :]
        kT = carve(CT * NT).rearrange("p (k t) -> p k t", t=NT)
        v = carve(5 * 512).rearrange("p (j c) -> p j c", j=5)
        xl = carve(CT * XW).rearrange("p (k t) -> p k t", t=XW)
        kiT = carve(NT)
        pTp_at = carve(1056)
        pTp = pTp_at[:, 0:1024].rearrange("p (s c) -> p s c", s=2)
        qis = pTp_at[:, 0:512].rearrange("p (b e c) -> p b e c", b=DEC_BATCH, e=2)
        kw = pTp_at[:, 512:1056]
        sm = carve(1024).rearrange("p (s c) -> p s c", s=2)
        probs = [sm[:, 0, :], sm[:, 1, :], lx[:, 0:512], lx[:, 512:1024]]
        probsT = [pTp[:, 0, :], pTp[:, 1, :], lx[:, 1024:1536], lx[:, 1536:2048]]
        so = lx[:, 2048:3072].rearrange("p (g c) -> p g c", g=GRP)
        raw = lx[:, 0:2 * NT].rearrange("p (s t) -> p s t", s=2)
        swp = lx[:, 2 * NT:4 * NT].rearrange("p (s t) -> p s t", s=2)
        cosT = lx[:, 4 * NT:5 * NT]
        sinT = lx[:, 5 * NT:6 * NT]
        xc, gi, ga, dd, aa = (lx[:, i * NT:(i + 1) * NT] for i in range(5))
        rms = lx[:, 0:NT]

        wslot = [wring[:, s, :].rearrange("p (k c) -> p k c", k=KT) for s in range(2)]
        wslot2 = [wring[:, s, :].rearrange("p (k c) -> p k c", k=FT) for s in range(2)]

        const_in = sem("const_in")
        steps_in = sem("steps_in")
        x_in = sem("x_in")
        kw_in = sem("kw_in")
        w_in = [sem("w_in_even"), sem("w_in_odd")]
        kidx_in = sem("kidx_in")
        q_placed = sem("q_placed")
        kv_in = [sem(f"kv_in{i}") for i in range(3)]
        x_again = sem("x_again")
        stored = sem("stored")
        state_stored = sem("state_stored")
        gemm_mm = sem("gemm_mm")
        gemm_ev = sem("gemm_ev")
        sq_rd = sem("sq_rd")
        ssq_mm = sem("ssq_mm")
        rms_rd = sem("rms_rd")
        rstd_rd = sem("rstd_rd")
        hn_rd = sem("hn_rd")
        x1_rd = sem("x1_rd")
        y_rd = sem("y_rd")
        rows_rd = sem("rows_rd")
        zero_rd = sem("zero_rd")
        lam_rd = sem("lam_rd")
        explam_rd = sem("explam_rd")
        rope_out = sem("rope_out")
        ki_dup = sem("ki_dup")
        wi_tr = sem("wi_tr")
        wi_rd = sem("wi_rd")
        wT_rd = sem("wT_rd")
        wT_tr = sem("wT_tr")
        wm_rd = sem("wm_rd")
        pi_mm = sem("pi_mm")
        pi_ev = sem("pi_ev")
        pi_acc = sem("pi_acc")
        qis_rd = sem("qis_rd")
        kx_tr = sem("kx_tr")
        kx_ev = sem("kx_ev")
        kd_mm = sem("kd_mm")
        kd_ev = sem("kd_ev")
        ks_mm = sem("ks_mm")
        ks_ev = sem("ks_ev")
        pmask_rd = sem("pmask_rd")
        smask_rd = sem("smask_rd")
        tk_p = sem("tk_p")
        tk_s = sem("tk_s")
        qbd_rd = sem("qbd_rd")
        k_mm = sem("k_mm")
        k_ev = sem("k_ev")
        kn_mm = sem("kn_mm")
        kn_ev = sem("kn_ev")
        sp_rd = sem("sp_rd")
        xc_rd = sem("xc_rd")
        lg_mm = sem("lg_mm")
        lg_ev = sem("lg_ev")
        tanh_rd = sem("tanh_rd")
        dd_rd = sem("dd_rd")
        root_rd = sem("root_rd")
        pk_rd = sem("pk_rd")
        pa_s = sem("pa_s")
        pa_m = sem("pa_m")
        pa_e = sem("pa_e")
        pa_n = sem("pa_n")
        pa_r = sem("pa_r")
        pa_t = sem("pa_t")
        pa_te = sem("pa_te")
        pa_o = sem("pa_o")
        pa_oe = sem("pa_oe")
        sm_mm = sem("sm_mm")
        sm_ev = sem("sm_ev")
        smax_rd = sem("smax_rd")
        se_rd = sem("se_rd")
        st_tr = sem("st_tr")
        st_ev = sem("st_ev")
        v_mm = sem("v_mm")
        so_rd = sem("so_rd")
        so_tr = sem("so_tr")
        so_ev = sem("so_ev")
        h_rd = sem("h_rd")
        dve_step = sem("dve_step")
        act_step = sem("act_step")
        pool_step = sem("pool_step")

        block = ctx.enter_context(nc.Block())

        N_CONST = 9
        w_src = [w_in_d[i] for i in range(6)] + [w_out_d[i] for i in range(2)]

        @block.sync
        def _(eng):
            for hf in range(2):
                eng.dma_start(regX[:, hf * 4 * NT:(hf + 1) * 4 * NT], xT_d[:, hf * 4 * NT:(hf + 1) * 4 * NT]).then_inc(x_in, 16)
            eng.dma_start(steps[:, :], steps_d).then_inc(steps_in, 16)
            eng.dma_start(par[:, :], par_d).then_inc(const_in, 16)
            eng.dma_start(pt_own[:, :], bass.AP(tensor=ptT_d.tensor, offset=0, ap=[[DEC_BATCH, NPG], [0, 8], [1, DEC_BATCH]])).then_inc(const_in, 16)
            eng.dma_start(keyoff[:, :], keyoff_d).then_inc(const_in, 16)
            eng.dma_start(wring[:, 0, :], w_src[0]).then_inc(w_in[0], 16)
            eng.dma_start(wkw, w_kw_d).then_inc(kw_in, 16)
            eng.dma_start(lx[:, 4 * NT:6 * NT], rope_d).then_inc(const_in, 16)
            eng.dma_start(ident[:, :], ident_d).then_inc(const_in, 16)
            eng.dma_start(causal[:, :], causal_d).then_inc(const_in, 16)
            eng.dma_start(ind[:, :, :], ind_d).then_inc(const_in, 16)
            eng.dma_start(newmask[:, :], newmask_d).then_inc(const_in, 16)
            eng.dma_start(wgate[:, :, :, :], wgate_d).then_inc(const_in, 16)
            eng.dma_start(wring[:, 1, :], w_src[1]).then_inc(w_in[1], 16)

            page_regs = [eng.alloc_register(f"page{b4}") for b4 in range(4)]

            def stream(s, slot, table, freed, uses):
                eng.load(page_regs, steps[0:1, bass.ds(s * 4, 4)])
                page = [eng.snap(r, min_val=0, max_val=NPOOL - 1) for r in page_regs]
                if freed is not None:
                    eng.wait_ge(freed, uses)
                for b4 in range(4):
                    eng.dma_start(kv[:, slot, b4, :], table[bass.ds(page[b4], 1), :, :].rearrange("a p c -> p (a c)")).then_inc(kv_in[slot], 16)

            eng.wait_ge(steps_in, 16)
            stream(0, 2, ck_d, None, 0)
            stream(1, 0, ck_d, kx_tr, 16)
            stream(2, 1, ck_d, kx_tr, 16)
            with eng.Fori(0, 9) as i:
                for j in range(3):
                    stream(i * 3 + (3 + j), (j + 2) % 3, ck_d, k_mm, i * 3 + (j + 1))
            for s in (30, 31):
                stream(s, (s + 2) % 3, ck_d, k_mm, s - 2)
            for s in range(3):
                stream(s, (s + KSTEPS + 2) % 3, cv_d, k_mm, KSTEPS - 2 + s)
            with eng.Fori(0, 9) as i:
                for j in range(3):
                    stream(i * 3 + (3 + j), (j + KSTEPS + 2) % 3, cv_d, v_mm, i * 3 + (j + 1))
            for s in (30, 31):
                stream(s, (s + KSTEPS + 2) % 3, cv_d, v_mm, s - 2)
            with eng.Fori(0, 4) as i:
                for s in range(2):
                    eng.wait_ge(gemm_mm, i * 16 + (E_WO + 8 + 8 * s))
                    eng.dma_start(wring[:, s, :], w_ff1_d[bass.ds(i * 2 + s, 1), :, :].rearrange("a p c -> p (a c)")).then_inc(w_in[s], 16)
            for s in range(2):
                eng.wait_ge(gemm_mm, E_F1 + 48 + 8 * (s + 1))
                eng.dma_start(wring[:, s, :], w_ff2_d[s]).then_inc(w_in[s], 16)
            with eng.Fori(0, 3) as i:
                for s in range(2):
                    eng.wait_ge(gemm_mm, i * 4 + (E_F2 + 2 * (s + 1)))
                    eng.dma_start(wring[:, s, :], w_ff2_d[bass.ds(i * 2 + (2 + s), 1), :, :].rearrange("a p c -> p (a c)")).then_inc(w_in[s], 16)
            for k in range(KT):
                eng.wait_ge(y_rd, k + 1)
                eng.dma_start(yT_d[:, k, :], xT[:, k, :]).then_inc(stored, 16)
            eng.wait_ge(state_stored, 16 * 5)
            eng.wait_ge(stored, 16 * KT)

        ci_rows = ci_d.rearrange("n (s r) d -> (n s) (r d)", r=16)

        @block.gpsimd
        def _(eng):
            steps = [0]

            def link(ins):
                steps[0] += 1
                ins.then_inc(pool_step, 1)
                eng.wait_ge(pool_step, steps[0])

            def gather(dst, rows, index, landed):
                eng.indirect_dma_start(dst, None, rows, bass.IndirectOffsetOnAxis(ap=index, axis=0)).then_inc(landed, 16)

            eng.wait_ge(rows_rd, 1)
            for b in range(4):
                gather(kidx_in_sb[:, b, :], ci_rows, row_i[:, b:b + 1], kidx_in)

            def rope(t, out, parts=P):
                r, w = raw[0:parts, t % 2, :], swp[0:parts, t % 2, :]
                eng.wait_ge(gemm_ev, 2 * t + 2)
                nc.gpsimd.tensor_tensor(r, r, cosT[0:parts, :], ALU.mult)
                link(nc.gpsimd.tensor_tensor(w, w, sinT[0:parts, :], ALU.mult))
                nc.gpsimd.tensor_tensor(out, r, w, ALU.add).then_inc(rope_out, 1)

            eng.wait_ge(const_in, 16 * N_CONST)
            for t in range(CT):
                rope(t, raw[:, t % 2, :])
            rope(4, kiT[0:HD, :], HD)
            eng.wait_ge(kx_tr, 8)
            for b in range(4):
                gather(kidx_in_sb[:, b, :], ci_rows, row_i[:, 4 + b:5 + b], kidx_in)
            for t in range(5, 9):
                rope(t, raw[:, t % 2, :])
            for m in range(CT):
                rope(9 + m, kT[:, m, :])
            eng.wait_ge(rope_out, 13)
            eng.dma_start(kT_d, kT).then_inc(state_stored, 16)
            eng.dma_start(kiT_d, kiT[0:HD, :]).then_inc(state_stored, 16)
            eng.wait_ge(gemm_ev, E_WO)
            eng.dma_start(v_d[0:SEQ, :].rearrange("(j p) c -> p j c", p=P), v[:, 0:4, :]).then_inc(state_stored, 16)
            eng.dma_start(v_d[SEQ:NT, :], v[0:NS, 4, :]).then_inc(state_stored, 16)
            eng.wait_ge(st_tr, 10)
            eng.dma_start(regX[:, :], xT_d).then_inc(x_again, 16)
            eng.wait_ge(pk_rd, 4)
            eng.dma_start(lru_d, pack[:, :, :]).then_inc(state_stored, 16)
            for u in range(ATT_UNITS):
                eng.wait_ge(pa_r, u + 1)
                if u >= 4:
                    eng.wait_ge(pa_t, u - 3)
                nc.gpsimd.tensor_scalar(diag[:, u % 4, :], ident[:, :], stat[:, u % 4, 3:4], None, ALU.mult).then_inc(pa_n, 1)

        @block.scalar
        def _(eng):
            steps = [0]

            def link(ins):
                steps[0] += 1
                ins.then_inc(act_step, 1)
                eng.wait_ge(act_step, steps[0])

            def gemm_out(e):
                eng.wait_ge(gemm_mm, e + 1)
                return bank[e % 4]

            eng.wait_ge(lam_rd, 1)
            nc.scalar.activation(sp[:, 4 * CT:5 * CT], sp[:, 2 * CT:3 * CT], ACT.Exp).then_inc(explam_rd, 1)
            for k in range(KT):
                if k % 4 == 0:
                    eng.wait_ge(x_in, 32)
                nc.scalar.activation(hnT[:, k, :], xT[:, k, :], ACT.Square).then_inc(sq_rd, 1)

            def root_mean_square(n, zero=0):
                eng.wait_ge(ssq_mm, n)
                eng.wait_ge(zero_rd, 1)
                for hf in range(2):
                    ins = nc.scalar.activation(rms[:, hf * HALF:(hf + 1) * HALF], bank[4 + hf][:, 0:HALF], ACT.Sqrt,
                                               bias=eps[:, 0:1], scale=1.0 / D_MODEL)
                ins.then_inc(rms_rd, 1)

            root_mean_square(1)

            def rotary_tile(t, e, parts=P):
                if 2 <= t <= 5:
                    eng.wait_ge(q_placed, t - 1)
                elif 7 <= t <= 10:
                    eng.wait_ge(q_placed, t - 2)
                elif t in (6, 11, 12):
                    eng.wait_ge(rope_out, t - 1)
                elif t == 0:
                    eng.wait_ge(hn_rd, KT)
                for hf in range(2):
                    src = gemm_out(e + hf)
                    c = slice(hf * HALF, (hf + 1) * HALF)
                    nc.scalar.copy(raw[0:parts, t % 2, c], src[0:parts, 0:HALF])
                    for q in range(parts // 32):
                        last = nc.scalar.copy(swp[32 * q:32 * q + 32, t % 2, c], src[32 * (q ^ 1):32 * (q ^ 1) + 32, 0:HALF])
                    if parts == HD:
                        last = nc.scalar.copy(kw[HD:HD + NH, c], src[HD:HD + NH, 0:HALF])
                    last.then_inc(gemm_ev, 1)

            def load_block(n):
                eng.dma_start(wring[:, n % 2, :], w_src[n]).then_inc(w_in[n % 2], 16)

            def place_queries(t, m, compact):
                eng.wait_ge(rope_out, t + 1)
                nc.scalar.copy(qz[0:HD, 2 * m, :], raw[0:HD, t % 2, 0:SEQ])
                nc.scalar.copy(qz[HD:P, 2 * m + 1, :], raw[HD:P, t % 2, 0:SEQ])
                nc.scalar.copy(compact[:, m, :], raw[:, t % 2, SEQ:NT]).then_inc(q_placed, 1)

            eng.wait_ge(zero_rd, 2)
            for t in range(5):
                if t < CT:
                    rotary_tile(t, 2 * t)
                else:
                    rotary_tile(t, E_KW, HD)
                if t >= 1:
                    place_queries(t - 1, t - 1, qi_s)
            load_block(2)
            eng.wait_ge(rope_out, 5)
            nc.scalar.copy(kw[0:HD, :], kiT[0:HD, :])
            nc.scalar.copy(kiT[HD:P, :], kiT[0:HD, :]).then_inc(ki_dup, 1)
            eng.wait_ge(q_placed, CT)
            for e in range(2):
                for hh in range(2):
                    for m in range(CT):
                        dst = qis[HD * e:HD * e + HD, :, e, (2 * m + hh) * DEC_SEQ:(2 * m + hh + 1) * DEC_SEQ]
                        last = nc.scalar.copy(dst, qi_s[HD * hh:HD * hh + HD, m, :].rearrange("p (b t) -> p b t", t=DEC_SEQ))
            last.then_inc(qis_rd, 1)
            for u in range(24):
                nk = P * (u // NH + 2)
                eng.wait_ge(pi_mm, u + 1)
                if u >= 2:
                    eng.wait_ge(pi_acc, u - 1)
                nc.scalar.activation(sm[:, u % 2, 0:nk], bank[6 + u % 2][:, 0:nk], ACT.Relu, scale=IDX_SCALE).then_inc(pi_ev, 1)
            for g in range(GRP):
                for u in range(8):
                    eng.wait_ge(kx_tr, 8 * g + u + 1)
                    if g == 1 and u == 0:
                        eng.wait_ge(kd_mm, 5)
                    nc.scalar.copy(kidxT[:, u // 2, (u % 2) * 512:(u % 2) * 512 + 512], bank[4 + u % 2][:, :]).then_inc(kx_ev, 1)
                for d in range(5):
                    eng.wait_ge(kd_mm, 5 * g + d + 1)
                    b_ = bank[6 + (5 * g + d) % 2]
                    if d < 4:
                        e, ch = d // 2, d % 2
                        dst = R[:, g, 0:PAST].rearrange("p (j e k) -> p e j k", e=2, k=P)[:, e, 4 * ch:4 * ch + 4, :]
                        src = b_[:, :].rearrange("p (j k) -> p j k", k=P)
                    else:
                        dst, src = R[:, g, PAST:NKEY], b_[:, 0:NS]
                    nc.scalar.activation(dst, src, ACT.Relu, scale=IDX_SCALE).then_inc(kd_ev, 1)

            for m in range(CT + 1):
                if m < CT:
                    rotary_tile(5 + m, E_Q + 2 * m)
                if m == CT - 1:
                    load_block(3)
                if m >= 1:
                    place_queries(4 + m, m - 1, q_s)
            eng.wait_ge(q_placed, 2 * CT)
            for m in range(CT):
                for hh in range(2):
                    dst = qbd[HD * hh:HD * hh + HD, :, m, (2 * m + hh) * DEC_SEQ:(2 * m + hh + 1) * DEC_SEQ]
                    last = nc.scalar.copy(dst, q_s[HD * hh:HD * hh + HD, m, :].rearrange("p (b t) -> p b t", t=DEC_SEQ))
            last.then_inc(qbd_rd, 1)

            def sample_scores(s):
                eng.wait_ge(k_mm, s + 1)
                nc.scalar.mul(S[:, s // NPG, (s % NPG) * P:(s % NPG + 1) * P], bank[4 + s % 2][:, 0:P], SCALE).then_inc(k_ev, 1)

            for m in range(CT):
                rotary_tile(9 + m, E_K + 2 * m)
                sample_scores(2 * m)
                sample_scores(2 * m + 1)
            load_block(4)
            for m in range(CT):
                for hf in range(2):
                    e = E_XL + 2 * m + hf
                    src = gemm_out(e)
                    if hf == 0:
                        nc.scalar.copy(xl[:, m, 3:3 + HALF], src[:, 0:HALF]).then_inc(gemm_ev, 1)
                    else:
                        n = SEQ - HALF
                        nc.scalar.copy(xl[:, m, 3 + HALF:3 + SEQ], src[:, 0:n])
                        dst = xl[:, m, 3 + SEQ:XW].rearrange("p (b w) -> p b w", w=3 + DEC_SEQ)[:, :, 3:3 + DEC_SEQ]
                        nc.scalar.copy(dst, src[:, n:n + NS].rearrange("p (b t) -> p b t", t=DEC_SEQ)).then_inc(gemm_ev, 1)
                sample_scores(8 + 2 * m)
                sample_scores(8 + 2 * m + 1)
            load_block(5)
            for m in range(CT):
                for hf in range(2):
                    src = gemm_out(E_GATE + 2 * m + hf)
                    if m == 0 and hf == 0:
                        eng.wait_ge(ks_mm, 5)
                    nc.scalar.activation(mixT[:, m, hf * HALF:(hf + 1) * HALF], src[:, 0:HALF], ACT.Gelu_apprx_tanh).then_inc(gemm_ev, 1)
                sample_scores(16 + 2 * m)
                sample_scores(16 + 2 * m + 1)
            load_block(6)
            for j in range(5):
                src = gemm_out(E_V + j)
                n = P if j < 4 else NS
                nc.scalar.copy(v[0:n, j, :], src[0:n, :]).then_inc(gemm_ev, 1)
                if j < 4:
                    sample_scores(24 + 2 * j)
                    sample_scores(24 + 2 * j + 1)
            load_block(7)
            for g in range(GRP):
                eng.wait_ge(kn_mm, g + 1)
                nc.scalar.mul(S[:, g, PAST:NKEY], bank[4 + g][:, 0:NS], SCALE).then_inc(kn_ev, 1)

            for g in range(GRP):
                eng.wait_ge(smax_rd, g + 1)
                nc.scalar.activation(S[:, g, :], S[:, g, :], ACT.Exp, bias=sstat[:, g, 6:7], accum_out=sstat[:, g, 7:8]).then_inc(se_rd, 1)
            for g in range(GRP):
                for q in range(5):
                    n = 5 * g + q
                    eng.wait_ge(st_tr, n + 1)
                    if q < 4:
                        ins = nc.scalar.copy(pT[:, g, 4 * q:4 * q + 4, :], bank[2 + n % 2][:, :].rearrange("p (r c) -> p r c", r=4))
                    else:
                        ins = nc.scalar.copy(pT[0:NS, g, 16, :], bank[2 + n % 2][0:NS, 0:P])
                    ins.then_inc(st_ev, 1)
            eng.wait_ge(sp_rd, 1)
            for c in range(CT):
                for u in range(4):
                    gate, hf = u // 2, u % 2
                    eng.wait_ge(lg_mm, 4 * c + u + 1)
                    if u == 0 and c > 0:
                        eng.wait_ge(pk_rd, c)
                    bias = par[:, (B_A, B_I)[gate] + c:(B_A, B_I)[gate] + c + 1]
                    nc.scalar.activation((ga, gi)[gate][:, hf * HALF:(hf + 1) * HALF], bank[6 + u % 2][:, 0:HALF],
                                         ACT.Sigmoid, bias=bias).then_inc(lg_ev, 1)
                eng.wait_ge(lg_ev, 4 * c + 4)
                link(nc.scalar.activation(aa, ga, ACT.Exp, scale=sp[:, c:c + 1]))
                nc.scalar.activation(dd, aa, ACT.Square)
                nc.scalar.activation(ga, ga, ACT.Tanh, scale=sp[:, c:c + 1]).then_inc(tanh_rd, 1)
                eng.wait_ge(dd_rd, c + 1)
                nc.scalar.activation(dd, dd, ACT.Sqrt, scale=-1.0).then_inc(root_rd, 1)

            def exponentials(u):
                nk = P * (u // NH + 1)
                eng.wait_ge(pa_m, u + 1)
                nc.scalar.activation(probs[u % 4][:, 0:nk], probs[u % 4][:, 0:nk], ACT.Exp, bias=stat[:, u % 4, 1:2],
                                     accum_out=stat[:, u % 4, 2:3]).then_inc(pa_e, 1)

            def transposed_out(u):
                nk = P * (u // NH + 1)
                eng.wait_ge(pa_t, u + 1)
                if u == 0:
                    eng.wait_ge(kd_mm, 10)
                nc.scalar.copy(probsT[u % 4][:, 0:nk], bank[6 + u % 2][:, 0:nk]).then_inc(pa_te, 1)

            for u in range(ATT_UNITS + 2):
                if u < ATT_UNITS:
                    exponentials(u)
                if u >= 2:
                    transposed_out(u - 2)

            for g in range(GRP):
                eng.wait_ge(so_tr, g + 1)
                for m in range(CT):
                    for hh in range(2):
                        h = 2 * m + hh
                        src = bank[6 + g][HD * hh:HD * hh + HD, m * P:(m + 1) * P].rearrange("p (b h t) -> p b h t", b=4, h=NH)[:, :, h, :]
                        dst = mixT[HD * hh:HD * hh + HD, 4 + m, SEQ + 16 * g:SEQ + 16 * g + 16].rearrange("p (b t) -> p b t", b=4)
                        last = nc.scalar.copy(dst, src)
                last.then_inc(so_ev, 1)

            def with_squares(dst, e0, m, hf):
                src = gemm_out(e0 + 2 * m + hf)
                c = slice(hf * HALF, (hf + 1) * HALF)
                nc.scalar.copy(dst[:, m, c], src[:, 0:HALF])
                nc.scalar.activation(sqT[:, m, c], src[:, 0:HALF], ACT.Square).then_inc(gemm_ev, 1)

            for m in range(KT):
                for hf in range(2):
                    with_squares(oT, E_WO, m, hf)
            root_mean_square(2)
            for k in range(KT):
                eng.wait_ge(x1_rd, k + 1)
                if k == 0:
                    eng.wait_ge(ssq_mm, 2)
                nc.scalar.activation(sqT[:, k, :], xT[:, k, :], ACT.Square).then_inc(sq_rd, 1)
            root_mean_square(3)
            eng.wait_ge(state_stored, 16 * 5)
            with eng.Fori(0, 8) as i:
                for u in range(8):
                    e = E_F1 + u
                    eng.wait_ge(gemm_mm, i * 8 + (e + 1))
                    nc.scalar.activation(arena[:, bass.ds(i * (4 * NT) + ((u // 2) * NT + (u % 2) * HALF), HALF)],
                                         bank[e % 4][:, 0:HALF], ACT.Relu).then_inc(gemm_ev, 1)
            with eng.Fori(0, 4) as i:
                for u in range(4):
                    e = E_F2 + u
                    c = i * (2 * NT) + ((u // 2) * NT + (u % 2) * HALF)
                    eng.wait_ge(gemm_mm, i * 4 + (e + 1))
                    nc.scalar.copy(regM[:, bass.ds(c, HALF)], bank[e % 4][:, 0:HALF])
                    nc.scalar.activation(regQ[:, bass.ds(c, HALF)], bank[e % 4][:, 0:HALF], ACT.Square).then_inc(gemm_ev, 1)
            root_mean_square(4)

        @block.vector
        def _(eng):
            steps = [0]
            vec = nc.vector

            def link(ins):
                steps[0] += 1
                ins.then_inc(dve_step, 1)
                eng.wait_ge(dve_step, steps[0])

            vec.memset(eps[:, :], EPS)
            vec.memset(ones[:, :], 1.0).then_inc(zero_rd, 1)
            vec.memset(regQ[:, :], 0.0)
            vec.memset(pTp_at[:, 0:512], 0.0)
            vec.memset(qbd[:, :, :, :], 0.0)
            vec.memset(xl[:, :, 0:3], 0.0).then_inc(zero_rd, 1)
            eng.wait_ge(const_in, 16 * N_CONST)
            vec.tensor_scalar(row_i[:, :], pt_own[:, :], float(PAGE // 16), keyoff[:, 0:1], ALU.mult, ALU.add).then_inc(rows_rd, 1)
            for c in range(CT):
                dst = xl[:, c, 3 + SEQ:XW].rearrange("p (b w) -> p b w", w=3 + DEC_SEQ)[:, :, 0:3]
                src = par[:, CONV0 + 24 * c:CONV0 + 24 * c + 24].rearrange("p (b w) -> p b w", w=3)
                vec.tensor_copy(dst, src)

            lam, z = par[:, LAM:LAM + CT], sp[:, CT:2 * CT]
            link(vec.tensor_scalar(z, lam, -1.0, None, ALU.mult))
            link(vec.tensor_tensor(sp[:, 2 * CT:3 * CT], lam, z, ALU.min))
            vec.tensor_scalar(sp[:, 3 * CT:4 * CT], z, 0.0, None, ALU.max).then_inc(lam_rd, 1)
            eng.wait_ge(explam_rd, 1)
            ez, s1, s2, acc = (sp[:, i * CT:(i + 1) * CT] for i in (4, 5, 6, 7))
            link(vec.tensor_scalar(s1, ez, 2.0, None, ALU.add))
            link(vec.reciprocal(s1, s1))
            link(vec.tensor_tensor(s1, s1, ez, ALU.mult))
            link(vec.tensor_tensor(s2, s1, s1, ALU.mult))
            link(vec.tensor_scalar(acc, s2, 1.0 / 17, None, ALU.mult))
            for odd in range(15, 1, -2):
                link(vec.scalar_tensor_tensor(out=acc, in0=acc, scalar=1.0 / odd, in1=s2, op0=ALU.add, op1=ALU.mult))
            link(vec.scalar_tensor_tensor(out=acc, in0=acc, scalar=1.0, in1=s1, op0=ALU.add, op1=ALU.mult))
            link(vec.scalar_tensor_tensor(out=acc, in0=acc, scalar=2.0, in1=sp[:, 3 * CT:4 * CT], op0=ALU.mult, op1=ALU.add))
            vec.tensor_scalar(sp[:, 0:CT], acc, -RG_C, None, ALU.mult).then_inc(sp_rd, 1)


            def recip_rms(n):
                eng.wait_ge(rms_rd, n)
                vec.reciprocal(rms, rms).then_inc(rstd_rd, 1)
                eng.wait_ge(rstd_rd, n)

            recip_rms(1)
            for k in range(KT):
                vec.scalar_tensor_tensor(out=hnT[:, k, :], in0=xT[:, k, :], scalar=par[:, G_PRE_MIX + k:G_PRE_MIX + k + 1],
                                         in1=rms, op0=ALU.mult, op1=ALU.mult).then_inc(hn_rd, 1)

            eng.wait_ge(wi_tr, 1)
            vec.tensor_copy(kwrow[:, 0:4, :], bank[6][:, 0:288].rearrange("p (j c) -> p j c", j=4))
            vec.tensor_copy(kwrow[0:NS, 4, :], bank[6][0:NS, 288:360]).then_inc(wi_rd, 1)
            eng.wait_ge(wi_rd, 1)
            for g in range(GRP):
                wi = kwrow[0:NS, 4, HD:HD + NH].unsqueeze(1).unsqueeze(3).to_broadcast([NS, 4, NH, DEC_SEQ])
                ins = vec.tensor_tensor(wT[:, g, :].rearrange("p (b h t) -> p b h t", b=4, h=NH),
                                        ind[:, g, :].rearrange("p (b h t) -> p b h t", b=4, h=NH), wi, ALU.mult)
            ins.then_inc(wT_rd, 1)
            eng.wait_ge(wT_tr, 1)
            vec.tensor_copy(wm[:, :, :], bank[7][:, 0:GRP * NS].rearrange("p (g c) -> p g c", g=GRP)).then_inc(wm_rd, 1)
            for u in range(24):
                n, h = u // NH + 1, u % NH
                nk = P * (n + 1)
                acc = scp[:, SCP_AT[n]:SCP_AT[n] + nk]
                w = kwrow[:, n, HD + h:HD + h + 1]
                eng.wait_ge(pi_ev, u + 1)
                if h == 0:
                    ins = vec.tensor_scalar(acc, sm[:, u % 2, 0:nk], w, None, ALU.mult)
                else:
                    ins = vec.scalar_tensor_tensor(out=acc, in0=sm[:, u % 2, 0:nk], scalar=w, in1=acc, op0=ALU.mult, op1=ALU.add)
                ins.then_inc(pi_acc, 1)
                eng.wait_ge(pi_acc, u + 1)
            for n in range(1, QB):
                last = scp[:, SCP_AT[n] + n * P:SCP_AT[n] + (n + 1) * P]
                link(vec.tensor_tensor(last, last, causal[:, :], ALU.add))
            for c in range(5):
                eng.wait_ge(ks_mm, c + 1)
                if c < 4:
                    dst = scs[:, 0:PAST].rearrange("q (p r) -> q r p", r=16)[:, 4 * c:4 * c + 4, :]
                    ins = vec.tensor_copy(dst, bank[4 + c % 2][0:NS, :].rearrange("q (r p) -> q r p", r=4))
                else:
                    ins = vec.tensor_tensor(scs[:, PAST:NKEY], bank[4][0:NS, 0:NS], newmask[:, :], ALU.add)
                ins.then_inc(ks_ev, 1)
            eng.wait_ge(ks_ev, 5)

            link(vec.tensor_copy(work_p, scp[:, :]))
            wp = {n: work_p[:, SCP_AT[n]:SCP_AT[n] + P * (n + 1)] for n in range(1, QB)}
            for i in range(TOPK_P // 8):
                for n in range(1, QB):
                    vec.max(m8[:, n - 1, :], wp[n]).then_inc(tk_p, 1)
                for n in range(1, QB):
                    eng.wait_ge(tk_p, 6 * i + n)
                    vec.match_replace(wp[n], m8[:, n - 1, :], wp[n], TAKEN).then_inc(tk_p, 1)
                eng.wait_ge(tk_p, 6 * i + 6)
            link(vec.tensor_tensor(work_p, work_p, scp[:, :], ALU.not_equal))
            link(vec.tensor_scalar(scp[:, :], work_p, -OUT_OF_REACH, OUT_OF_REACH, ALU.mult, ALU.add))
            link(vec.tensor_copy(work_s, scs))
            for i in range(TOPK_S // 8):
                vec.max(m8[0:NS, 0, :], work_s).then_inc(tk_s, 1)
                eng.wait_ge(tk_s, 2 * i + 1)
                vec.match_replace(work_s, m8[0:NS, 0, :], work_s, TAKEN).then_inc(tk_s, 1)
                eng.wait_ge(tk_s, 2 * i + 2)
            link(vec.tensor_tensor(work_s, work_s, scs, ALU.not_equal))
            vec.tensor_scalar(scs, work_s, -OUT_OF_REACH, OUT_OF_REACH, ALU.mult, ALU.add).then_inc(smask_rd, 1)

            for g in range(GRP):
                for c in range(5):
                    n = 5 * g + c
                    cols = slice(c * 512, min((c + 1) * 512, NKEY))
                    w = cols.stop - cols.start
                    eng.wait_ge(sm_mm, n + 1)
                    eng.wait_ge(kn_ev, g + 1)
                    vec.tensor_tensor_reduce(out=S[:, g, cols], in0=S[:, g, cols], in1=bank[2 + n % 2][:, 0:w], scale=1.0, scalar=TAKEN,
                                             op0=ALU.add, op1=ALU.max, accum_out=sstat[:, g, c:c + 1]).then_inc(sm_ev, 1)
                eng.wait_ge(sm_ev, 5 * g + 5)
                link(vec.tensor_reduce(sstat[:, g, 5:6], sstat[:, g, 0:5], AX_X, ALU.max))
                vec.tensor_scalar(sstat[:, g, 6:7], sstat[:, g, 5:6], -1.0, None, ALU.mult).then_inc(smax_rd, 1)
            eng.wait_ge(gemm_ev, E_V)
            eng.wait_ge(rope_out, 13)
            for c in range(CT):
                def window(j):
                    prompt = xl[:, c, j:j + SEQ]
                    sample = xl[:, c, 3 + SEQ:XW].rearrange("p (b w) -> p b w", w=3 + DEC_SEQ)[:, :, j:j + DEC_SEQ]
                    return prompt, sample

                outs = (xc[:, 0:SEQ], xc[:, SEQ:NT].rearrange("p (b t) -> p b t", t=DEC_SEQ))
                for j in range(4):
                    w = par[:, CONV_W0 + 4 * j + c:CONV_W0 + 4 * j + c + 1]
                    for o, x in zip(outs, window(j)):
                        if j == 0:
                            ins = vec.tensor_scalar(o, x, w, par[:, CONV_B + c:CONV_B + c + 1], ALU.mult, ALU.add)
                        else:
                            ins = vec.scalar_tensor_tensor(out=o, in0=x, scalar=w, in1=o, op0=ALU.mult, op1=ALU.add)
                    if j < 3:
                        link(ins)
                ins.then_inc(xc_rd, 1)
                eng.wait_ge(lg_ev, 4 * c + 4)
                link(vec.tensor_tensor(gi, gi, xc, ALU.mult))
                eng.wait_ge(tanh_rd, c + 1)
                vec.scalar_tensor_tensor(out=dd, in0=dd, scalar=1.0, in1=ga, op0=ALU.add, op1=ALU.mult).then_inc(dd_rd, 1)
                eng.wait_ge(root_rd, c + 1)
                link(vec.tensor_tensor(gi, gi, dd, ALU.mult))
                a0 = aa[:, SEQ:NT].rearrange("p (b t) -> p b t", t=DEC_SEQ)[:, :, 0]
                u0 = gi[:, SEQ:NT].rearrange("p (b t) -> p b t", t=DEC_SEQ)[:, :, 0]
                link(vec.tensor_tensor(ga[:, 0:DEC_BATCH], a0, par[:, H0 + 8 * c:H0 + 8 * c + 8], ALU.mult))
                vec.tensor_tensor(u0, u0, ga[:, 0:DEC_BATCH], ALU.add)
                link(vec.memset(a0, 0.0))
                link(vec.tensor_tensor_scan(dd, aa, gi, 0.0, ALU.mult, ALU.add))
                vec.tensor_tensor(mixT[:, c, :], mixT[:, c, :], dd, ALU.mult)
                vec.tensor_copy(pack[:, c, 0:3], xl[:, c, SEQ:SEQ + 3])
                vec.tensor_copy(pack[:, c, 3:27].rearrange("p (b t) -> p b t", t=3),
                                xl[:, c, 3 + SEQ:XW].rearrange("p (b w) -> p b w", w=3 + DEC_SEQ)[:, :, DEC_SEQ:DEC_SEQ + 3])
                vec.tensor_copy(pack[:, c, 27:28], dd[:, SEQ - 1:SEQ])
                vec.tensor_copy(pack[:, c, 28:36], dd[:, SEQ:NT].rearrange("p (b t) -> p b t", t=DEC_SEQ)[:, :, DEC_SEQ - 1]).then_inc(pk_rd, 1)
                eng.wait_ge(pk_rd, c + 1)

            def masked(u):
                n, h = u // NH, u % NH
                nk = P * (n + 1)
                mask = causal[:, :] if n == 0 else scp[:, SCP_AT[n]:SCP_AT[n] + nk]
                eng.wait_ge(pa_s, u + 1)
                if u >= 4:
                    eng.wait_ge(pa_t, u - 3)
                link(vec.tensor_tensor_reduce(out=probs[u % 4][:, 0:nk], in0=bank[4 + u % 2][:, 0:nk], in1=mask, scale=SCALE, scalar=TAKEN,
                                              op0=ALU.add, op1=ALU.max, accum_out=stat[:, u % 4, 0:1]))
                vec.tensor_scalar(stat[:, u % 4, 1:2], stat[:, u % 4, 0:1], -1.0, None, ALU.mult).then_inc(pa_m, 1)

            def row_sum(u):
                eng.wait_ge(pa_e, u + 1)
                vec.reciprocal(stat[:, u % 4, 3:4], stat[:, u % 4, 2:3]).then_inc(pa_r, 1)

            def pair_out(w):
                eng.wait_ge(pa_o, w + 1)
                n, m = w // CT, w % CT
                vec.tensor_copy(mixT[:, 4 + m, n * P:(n + 1) * P], bank[w % 2][:, 0:P]).then_inc(pa_oe, 1)

            for u in range(ATT_UNITS + 5):
                if u < ATT_UNITS:
                    masked(u)
                if 1 <= u <= ATT_UNITS:
                    row_sum(u - 1)
                if u >= 6 and u % 2 == 0:
                    pair_out((u - 6) // 2)

            for g in range(GRP):
                eng.wait_ge(se_rd, g + 1)
                link(vec.reciprocal(sstat[:, g, 0:1], sstat[:, g, 7:8]))
            for g in range(GRP):
                eng.wait_ge(v_mm, 16 * (g + 1))
                vec.tensor_scalar(so[:, g, :], bank[2 + g][:, :], sstat[:, g, 0:1], None, ALU.mult).then_inc(so_rd, 1)

            eng.wait_ge(x_again, 16)
            recip_rms(2)
            for k in range(KT):
                link(vec.scalar_tensor_tensor(out=oT[:, k, :], in0=oT[:, k, :], scalar=par[:, G_POST_MIX + k:G_POST_MIX + k + 1],
                                              in1=rms, op0=ALU.mult, op1=ALU.mult))
                vec.tensor_tensor(xT[:, k, :], xT[:, k, :], oT[:, k, :], ALU.add).then_inc(x1_rd, 1)
            recip_rms(3)
            eng.wait_ge(x1_rd, KT)
            for k in range(KT):
                vec.scalar_tensor_tensor(out=hnT[:, k, :], in0=xT[:, k, :], scalar=par[:, G_PRE_FFN + k:G_PRE_FFN + k + 1],
                                         in1=rms, op0=ALU.mult, op1=ALU.mult).then_inc(hn_rd, 1)
            with eng.Fori(0, 32) as i:
                eng.wait_ge(gemm_ev, i * 2 + (E_F1 + 2))
                h = arena[:, bass.ds(i * NT, NT)]
                vec.tensor_tensor(h, h, h, ALU.mult).then_inc(h_rd, 1)
            recip_rms(4)
            for k in range(KT):
                link(vec.scalar_tensor_tensor(out=fT[:, k, :], in0=fT[:, k, :], scalar=par[:, G_POST_FFN + k:G_POST_FFN + k + 1],
                                              in1=rms, op0=ALU.mult, op1=ALU.mult))
                vec.tensor_tensor(xT[:, k, :], xT[:, k, :], fT[:, k, :], ALU.add).then_inc(y_rd, 1)

        @block.tensor
        def _(eng):
            pe = nc.tensor

            def ssq(squares, ready):
                for k in range(KT):
                    ready(k)
                    for hf in range(2):
                        ins = pe.matmul(bank[4 + hf][:, 0:HALF], ones[:, :], squares[:, k, hf * HALF:(hf + 1) * HALF],
                                        start=(k == 0), stop=(k == KT - 1))
                ins.then_inc(ssq_mm, 1)

            def slot_free(e):
                if e >= 4:
                    eng.wait_ge(gemm_ev, e - 3)

            def product(e, hf, lhs, rhs, parts=P):
                slot_free(e)
                for k in range(KT):
                    ins = pe.matmul(bank[e % 4][0:parts, 0:HALF], lhs(k), rhs[:, k, hf * HALF:(hf + 1) * HALF],
                                    start=(k == 0), stop=(k == KT - 1))
                ins.then_inc(gemm_mm, 1)

            def tile_product(e, w, m, rhs):
                for hf in range(2):
                    product(e + hf, hf, lambda k: w[:, k, m * P:(m + 1) * P], rhs)

            def weights(n):
                eng.wait_ge(w_in[n % 2], 16 * (n // 2 + 1))
                return wslot[n % 2]

            eng.wait_ge(zero_rd, 1)
            ssq(hnT, lambda k: eng.wait_ge(sq_rd, k + 1))
            eng.wait_ge(hn_rd, KT)
            w = weights(0)
            for m in range(CT):
                tile_product(E_QI + 2 * m, w, m, hnT)
            eng.wait_ge(kw_in, 16)
            for hf in range(2):
                product(E_KW + hf, hf, lambda k: wkw[:, k, :], hnT, 72)
            eng.wait_ge(ki_dup, 1)
            eng.wait_ge(const_in, 16 * N_CONST)
            for j in range(5):
                n = P if j < 4 else NS
                ins = pe.transpose(bank[6][0:n, 72 * j:72 * j + 72], kw[0:72, j * P:j * P + n], ident[0:72, 0:72])
            ins.then_inc(wi_tr, 1)
            eng.wait_ge(wT_rd, 1)
            for g in range(GRP):
                ins = pe.transpose(bank[7][:, g * NS:(g + 1) * NS], wT[:, g, :], ident[0:NS, 0:NS])
            ins.then_inc(wT_tr, 1)
            eng.wait_ge(zero_rd, 2)
            eng.wait_ge(q_placed, CT)
            for u in range(24):
                n, h = u // NH + 1, u % NH
                nk = P * (n + 1)
                if u >= 2:
                    eng.wait_ge(pi_ev, u - 1)
                elif u == 1:
                    eng.wait_ge(wm_rd, 1)
                pe.matmul(bank[6 + u % 2][:, 0:nk], qz[:, h, n * P:(n + 1) * P], kiT[:, 0:nk], start=True, stop=True).then_inc(pi_mm, 1)
            eng.wait_ge(qis_rd, 1)
            for g in range(GRP):
                eng.wait_ge(kidx_in, 64 * (g + 1))
                for u in range(8):
                    n = 8 * g + u
                    if n >= 2:
                        eng.wait_ge(kx_ev, n - 1)
                    for j in range(4):
                        ins = pe.transpose(bank[4 + u % 2][:, j * P:(j + 1) * P],
                                           kidx_in_sb[:, u // 2, ((u % 2) * 4 + j) * P:((u % 2) * 4 + j + 1) * P], ident[:, :])
                    ins.then_inc(kx_tr, 1)
                eng.wait_ge(kx_ev, 8 * g + 8)
                for d in range(5):
                    n = 5 * g + d
                    if n >= 2:
                        eng.wait_ge(kd_ev, n - 1)
                    else:
                        eng.wait_ge(pi_ev, 24)
                    for b4 in range(4):
                        e, ch = (d // 2, d % 2) if d < 4 else (0, 0)
                        rhs = kidxT[:, b4, ch * 512:ch * 512 + 512] if d < 4 else kiT[:, SEQ:NT]
                        w_ = 512 if d < 4 else NS
                        ins = pe.matmul(bank[6 + n % 2][32 * b4:32 * b4 + 32, 0:w_], qis[:, 4 * g + b4, e, :], rhs, start=True, stop=True)
                    ins.then_inc(kd_mm, 1)
            eng.wait_ge(kd_ev, 10)
            eng.wait_ge(wm_rd, 1)
            for c in range(5):
                cols = slice(c * 512, min((c + 1) * 512, NKEY))
                if c >= 2:
                    eng.wait_ge(ks_ev, c - 1)
                for g in range(GRP):
                    ins = pe.matmul(bank[4 + c % 2][0:NS, 0:cols.stop - cols.start], wm[:, g, :], R[:, g, cols],
                                    start=(g == 0), stop=(g == GRP - 1))
                ins.then_inc(ks_mm, 1)

            w = weights(1)
            for m in range(CT):
                tile_product(E_Q + 2 * m, w, m, hnT)

            def key_scores(s):
                slot = (s + 2) % 3
                eng.wait_ge(kv_in[slot], 64 * (s // 3 + 1))
                if s >= 2:
                    eng.wait_ge(k_ev, s - 1)
                elif s == 0:
                    eng.wait_ge(qbd_rd, 1)
                    eng.wait_ge(ks_ev, 5)
                for m in range(CT):
                    for b4 in range(4):
                        ins = pe.matmul(bank[4 + s % 2][32 * b4:32 * b4 + 32, 0:P], qbd[:, 4 * (s // NPG) + b4, m, :],
                                        kv[:, slot, b4, m * P:(m + 1) * P], start=(m == 0), stop=(m == CT - 1))
                ins.then_inc(k_mm, 1)

            step = 0
            for n, e0 in ((2, E_K), (3, E_XL), (4, E_GATE)):
                w = weights(n)
                for m in range(CT):
                    tile_product(e0 + 2 * m, w, m, hnT)
                    key_scores(step)
                    key_scores(step + 1)
                    step += 2
            w = weights(5)
            for j in range(5):
                n = P if j < 4 else NS
                e = E_V + j
                slot_free(e)
                for k in range(KT):
                    ins = pe.matmul(bank[e % 4][0:n, :], hnT[:, k, j * P:j * P + n], w[:, k, :], start=(k == 0), stop=(k == KT - 1))
                ins.then_inc(gemm_mm, 1)
                if j < 4:
                    key_scores(step)
                    key_scores(step + 1)
                    step += 2
            eng.wait_ge(rope_out, 13)
            for g in range(GRP):
                eng.wait_ge(k_ev, KSTEPS)
                for m in range(CT):
                    for b4 in range(4):
                        ins = pe.matmul(bank[4 + g][32 * b4:32 * b4 + 32, 0:NS], qbd[:, 4 * g + b4, m, :], kT[:, m, SEQ:NT],
                                        start=(m == 0), stop=(m == CT - 1))
                ins.then_inc(kn_mm, 1)
            eng.wait_ge(smask_rd, 1)
            eng.wait_ge(gemm_ev, E_WO)
            for g in range(GRP):
                for c in range(5):
                    n = 5 * g + c
                    cols = slice(c * 512, min((c + 1) * 512, NKEY))
                    if n >= 2:
                        eng.wait_ge(sm_ev, n - 1)
                    pe.matmul(bank[2 + n % 2][:, 0:cols.stop - cols.start], ind[:, g, :], scs[:, cols], start=True, stop=True).then_inc(sm_mm, 1)
            eng.wait_ge(sm_ev, 10)
            for g in range(GRP):
                eng.wait_ge(se_rd, g + 1)
                for q in range(5):
                    n = 5 * g + q
                    if n >= 2:
                        eng.wait_ge(st_ev, n - 1)
                    if q < 4:
                        for r in range(4 * q, 4 * q + 4):
                            ins = pe.transpose(bank[2 + n % 2][:, (r % 4) * P:(r % 4 + 1) * P], S[:, g, r * P:(r + 1) * P], ident[:, :])
                    else:
                        ins = pe.transpose(bank[2 + n % 2][0:NS, 0:P], S[:, g, PAST:NKEY], ident[:, :])
                    ins.then_inc(st_tr, 1)
            def value_products(s):
                g, r = s // NPG, s % NPG
                t = s + KSTEPS
                slot = (t + 2) % 3
                eng.wait_ge(kv_in[slot], 64 * (t // 3 + 1))
                for b4 in range(4):
                    ins = pe.matmul(bank[2 + g][32 * b4:32 * b4 + 32, :], pT[:, g, r, 32 * b4:32 * b4 + 32], kv[:, slot, b4, :],
                                    start=(r == 0), stop=False)
                if r == NPG - 1:
                    for b4 in range(4):
                        ins = pe.matmul(bank[2 + g][32 * b4:32 * b4 + 32, :], pT[0:NS, g, 16, 32 * b4:32 * b4 + 32], v[0:NS, 4, :],
                                        start=False, stop=True)
                ins.then_inc(v_mm, 1)

            eng.wait_ge(st_ev, 10)
            step = 0
            for c in range(CT):
                eng.wait_ge(xc_rd, c + 1)
                for u in range(4):
                    n = 4 * c + u
                    if n >= 2:
                        eng.wait_ge(lg_ev, n - 1)
                    hf = u % 2
                    pe.matmul(bank[6 + n % 2][:, 0:HALF], wgate[:, u // 2, c, :], xc[:, hf * HALF:(hf + 1) * HALF],
                              start=True, stop=True).then_inc(lg_mm, 1)
                for _ in range(LRU_STEPS):
                    value_products(step)
                    step += 1

            def att_scores(u):
                n, h = u // NH, u % NH
                if u >= 2:
                    eng.wait_ge(pa_m, u - 1)
                else:
                    eng.wait_ge(kn_ev, GRP)
                pe.matmul(bank[4 + u % 2][:, 0:P * (n + 1)], qz[:, h, n * P:(n + 1) * P], kT[:, h // 2, 0:P * (n + 1)],
                          start=True, stop=True).then_inc(pa_s, 1)

            def att_transposes(u):
                n = u // NH
                eng.wait_ge(pa_n, u + 1)
                if u >= 2:
                    eng.wait_ge(pa_te, u - 1)
                else:
                    eng.wait_ge(lg_ev, 16)
                for j in range(n + 1):
                    ins = pe.matmul(bank[6 + u % 2][:, j * P:(j + 1) * P], probs[u % 4][:, j * P:(j + 1) * P], diag[:, u % 4, :],
                                    start=True, stop=True)
                ins.then_inc(pa_t, 1)

            def att_values(u):
                n, h = u // NH, u % NH
                w_ = u // 2
                eng.wait_ge(pa_te, u + 1)
                if w_ >= 2:
                    eng.wait_ge(pa_oe, w_ - 1)
                else:
                    eng.wait_ge(gemm_ev, E_WO)
                p0 = HD * (h % 2)
                for j in range(n + 1):
                    ins = pe.matmul(bank[w_ % 2][p0:p0 + HD, 0:P], v[:, j, h * HD:(h + 1) * HD], probsT[u % 4][:, j * P:(j + 1) * P],
                                    start=(j == 0), stop=(j == n))
                if h % 2:
                    ins.then_inc(pa_o, 1)

            for u in range(ATT_UNITS + 3):
                if u < ATT_UNITS:
                    att_scores(u)
                if 2 <= u < ATT_UNITS + 2:
                    att_transposes(u - 2)
                if u >= 3:
                    att_values(u - 3)
                while step < KSTEPS and step - CT * LRU_STEPS < (u + 1) * (KSTEPS - CT * LRU_STEPS) // ATT_UNITS:
                    value_products(step)
                    step += 1

            for g in range(GRP):
                eng.wait_ge(so_rd, g + 1)
                if g == 0:
                    eng.wait_ge(pa_te, ATT_UNITS)
                for m in range(CT):
                    ins = pe.transpose(bank[6 + g][:, m * P:(m + 1) * P], so[:, g, m * P:(m + 1) * P], ident[:, :])
                ins.then_inc(so_tr, 1)

            eng.wait_ge(so_ev, GRP)
            eng.wait_ge(pa_oe, ATT_UNITS // 2)
            eng.wait_ge(pk_rd, CT)
            eng.wait_ge(st_ev, 10)
            for n in (6, 7):
                w = weights(n)
                for m in range(CT):
                    tile_product(E_WO + 8 * (n - 6) + 2 * m, w, m, mixT)
            ssq(sqT, lambda k: eng.wait_ge(gemm_ev, E_WO + 2 * k + 2))
            eng.wait_ge(rms_rd, 2)
            ssq(sqT, lambda k: eng.wait_ge(sq_rd, KT + k + 1))
            eng.wait_ge(hn_rd, 2 * KT)
            with eng.Fori(0, 4) as i:
                for s in range(2):
                    eng.wait_ge(w_in[s], i * 16 + 16 * 5)
                    for m in range(CT):
                        for hf in range(2):
                            e = E_F1 + 8 * s + 2 * m + hf
                            eng.wait_ge(gemm_ev, i * 16 + (e - 3))
                            for k in range(KT):
                                ins = pe.matmul(bank[e % 4][:, 0:HALF], wslot[s][:, k, m * P:(m + 1) * P],
                                                hnT[:, k, hf * HALF:(hf + 1) * HALF], start=(k == 0), stop=(k == KT - 1))
                            ins.then_inc(gemm_mm, 1)
            eng.wait_ge(h_rd, FT)
            with eng.Fori(0, 4) as i:
                for s in range(2):
                    eng.wait_ge(w_in[s], i * 16 + 16 * 9)
                    for hf in range(2):
                        e = E_F2 + 2 * s + hf
                        eng.wait_ge(gemm_ev, i * 4 + (e - 3))
                        for k in range(FT):
                            ins = pe.matmul(bank[e % 4][:, 0:HALF], wslot2[s][:, k, :], hT[:, k, hf * HALF:(hf + 1) * HALF],
                                            start=(k == 0), stop=(k == FT - 1))
                        ins.then_inc(gemm_mm, 1)
            eng.wait_ge(rms_rd, 3)
            ssq(sqT, lambda k: eng.wait_ge(gemm_ev, E_F2 + 2 * k + 2))


def kernel(x_prompt, x_sample, cache_k, cache_v, cache_kidx, state_h, state_conv, page_table, g_pre_mix, w_in, conv_w,
           conv_b, w_a, b_a, w_i, b_i, lam, w_out, g_post_mix, g_pre_ffn, w_ff1, w_ff2, g_post_ffn):
    import numpy as np
    import concourse.bacc as bacc
    from concourse.bass_utils import run_bass_kernel_spmd as run

    f4 = np.float32
    a = {k: np.asarray(x) for k, x in dict(
        x_prompt=x_prompt, x_sample=x_sample, ck=cache_k, cv=cache_v, ci=cache_kidx, sh=state_h, sc=state_conv,
        w_in=w_in, w_out=w_out, w1=w_ff1, w2=w_ff2, conv_w=conv_w, w_a=w_a, w_i=w_i).items()}

    tokens = np.concatenate([a["x_prompt"].reshape(SEQ, D_MODEL), a["x_sample"].reshape(NS, D_MODEL)])
    xT = tokens.T.reshape(KT, P, NT).transpose(1, 0, 2).reshape(P, KT * NT)

    def by_channel(x, *rest):
        return np.asarray(x).reshape(-1, P).T

    par = np.concatenate(
        [by_channel(g) for g in (g_pre_mix, g_post_mix, g_pre_ffn, g_post_ffn, conv_w, conv_b, b_a, b_i, lam)]
        + [a["sh"].reshape(DEC_BATCH, CT, P).transpose(2, 1, 0).reshape(P, -1),
           a["sc"].reshape(DEC_BATCH, 3, CT, P).transpose(3, 2, 0, 1).reshape(P, -1)], axis=1)

    def blocks(w, cols):
        k, n = w.shape
        return w.reshape(k // P, P, n // cols, cols).transpose(2, 1, 0, 3).reshape(n // cols, P, -1)

    wi = a["w_in"][0]
    part = {n: wi[:, 512 * i:512 * (i + 1)] for i, n in enumerate(["xl", "gate", "q", "k", "v", "qi"])}
    w_in_blocks = np.concatenate([blocks(part[n], 512) for n in ("qi", "q", "k", "xl", "gate", "v")])
    w_kw = wi[:, 3072:3144].reshape(KT, P, 72).transpose(1, 0, 2)
    wgate = np.zeros((P, 2, CT, P), f4)
    for n, w in enumerate((a["w_a"][0], a["w_i"][0])):
        for j in range(8):
            o = HD * (j % 2)
            wgate[o:o + HD, n, j // 2, o:o + HD] = w[j]
    ck = a["ck"][0].reshape(NPOOL, PAGE, CT, P).transpose(0, 3, 2, 1).reshape(NPOOL, P, CT * PAGE)

    half = HD // 2
    freq = f4(10000.0) ** (-np.arange(half, dtype=f4) / f4(half))
    pos = np.concatenate([np.arange(SEQ), np.tile(PAST + np.arange(DEC_SEQ), DEC_BATCH)]).astype(f4)
    ang = (pos[None, :] * freq[:, None]).astype(f4)
    cos, sin = np.cos(ang), np.sin(ang)
    rope = np.concatenate([np.tile(cos, (4, 1)), np.tile(np.concatenate([-sin, sin]), (2, 1))], axis=1).astype(f4)
    q = np.arange(P)
    causal = np.where(q[None, :] > q[:, None], OUT_OF_REACH, 0.0).astype(f4)
    qb, qt = np.arange(NS) // DEC_SEQ, np.arange(NS) % DEC_SEQ
    rb, rt = np.arange(P) // 32, np.arange(P) % DEC_SEQ
    ind = np.stack([(qb[:, None] == rb[None, :] + 4 * g) & (qt[:, None] == rt[None, :]) for g in range(GRP)], axis=1).astype(f4)
    newmask = np.where((qb[:, None] == qb[None, :]) & (qt[None, :] <= qt[:, None]), 0.0, OUT_OF_REACH).astype(f4)
    keyoff = (q[:, None] % 8).astype(f4)

    steps = np.asarray(page_table).reshape(GRP, 4, NPG).transpose(0, 2, 1).reshape(1, KSTEPS * 4)

    arrays = {
        "xT": xT, "par": par, "w_in": w_in_blocks, "w_kw": w_kw, "w_out": blocks(a["w_out"][0], 512),
        "w_ff1": blocks(a["w1"][0], 512), "w_ff2": blocks(a["w2"][0], P), "wgate": wgate,
        "ck": ck, "cv": a["cv"][0].reshape(NPOOL, PAGE, WIDTH), "ci": a["ci"][0], "steps": steps, "ptT": np.asarray(page_table).T,
        "ident": np.eye(P, dtype=f4), "rope": rope, "causal": causal, "ind": ind, "newmask": newmask, "keyoff": keyoff,
    }
    arrays = {f"in_{k}": np.ascontiguousarray(x) for k, x in arrays.items()}
    nc = bacc.Bacc("TRN2", target_bir_lowering=False, num_devices=1)
    args = [nc.dram_tensor(k, x.shape, mybir.dt.from_np(x.dtype), kind="ExternalInput").ap() for k, x in arrays.items()]
    outs = [(P, KT, NT), (P, CT, NT), (NT, WIDTH), (HD, NT), (P, CT, 36)]
    for i, shape in enumerate(outs):
        args.append(nc.dram_tensor(f"out_{i}", shape, F32, kind="ExternalOutput").ap())
    build(nc, *args)
    r = run(nc, [arrays], core_ids=[0]).results[0]
    yT, kT, v, kiT, lru = (r[f"out_{i}"] for i in range(len(outs)))

    y = yT.transpose(2, 1, 0).reshape(NT, D_MODEL)
    k = kT.transpose(2, 1, 0).reshape(NT, WIDTH)
    ki = kiT.T
    st = lru.transpose(2, 1, 0).reshape(36, WIDTH)
    return (y[:SEQ].reshape(1, SEQ, D_MODEL), y[SEQ:].reshape(DEC_BATCH, DEC_SEQ, D_MODEL),
            k[:SEQ].reshape(1, 1, SEQ, NH, HD), v[:SEQ].reshape(1, 1, SEQ, NH, HD), ki[:SEQ].reshape(1, 1, SEQ, HD),
            st[27].reshape(1, 1, WIDTH), st[0:3].reshape(1, 1, 3, WIDTH),
            k[SEQ:].reshape(1, DEC_BATCH, DEC_SEQ, NH, HD), v[SEQ:].reshape(1, DEC_BATCH, DEC_SEQ, NH, HD),
            ki[SEQ:].reshape(1, DEC_BATCH, DEC_SEQ, HD),
            st[28:36].reshape(1, DEC_BATCH, WIDTH), st[3:27].reshape(1, DEC_BATCH, 3, WIDTH))
```

```python
from contextlib import ExitStack

import concourse.bass as bass
from concourse import mybir

P = 128
F32 = mybir.dt.float32
F32R = mybir.dt.float32r
I32 = mybir.dt.int32
ALU = mybir.AluOpType
ACT = mybir.ActivationFunctionType
AX_X = mybir.AxisListType.X

D_MODEL = 1024
SEQ = 512
DEC_BATCH = 8
DEC_SEQ = 4
NS = DEC_BATCH * DEC_SEQ
NT = SEQ + NS
HALF = NT // 2
PAST = 2048
PAGE = 128
NPG = PAST // PAGE
NPOOL = DEC_BATCH * NPG * 5 // 4
WIDTH = 512
CT = WIDTH // P
NH = 8
HD = 64
KT = D_MODEL // P
D_FF = 4 * D_MODEL
FT = D_FF // P
QB = SEQ // P
TOPK_P = min(256, SEQ // 4)
TOPK_S = min(256, (PAST + DEC_SEQ) // 4)
NKEY = PAST + NS
GRP = DEC_BATCH // 4
EPS = 1e-6
RG_C = 8.0
OUT_OF_REACH = -1e30
TAKEN = -3e38
XW = 3 + SEQ + DEC_BATCH * (3 + DEC_SEQ)
SCALE = HD ** -0.5
IDX_SCALE = (HD ** -0.5) * (NH ** -0.5)

G_PRE_MIX, G_POST_MIX, G_PRE_FFN, G_POST_FFN = 0, 8, 16, 24
CONV_W0, CONV_B, B_A, B_I, LAM, H0, CONV0 = 32, 48, 52, 56, 60, 64, 96
NPAR = 192

E_QI, E_KW, E_Q, E_K, E_XL, E_GATE, E_V, E_WO, E_MIX = 0, 8, 10, 18, 26, 34, 42, 47, 63
HT = FT // 2
PIECE = KT * P
PIECES = 2 * (HT + 2 * KT)
SCP_AT = {1: 0, 2: 256, 3: 640}
KSTEPS = GRP * NPG
ATT_UNITS = QB * NH
LRU_STEPS = 3


def build(nc, xT_d, par_d, w_in_d, w_kw_d, w_out_d, w_mlp_d, wgate_d, ck_d, cv_d, ci_d, steps_d, ptT_d,
          ident_d, rope_d, causal_d, ind_d, newmask_d, keyoff_d, yT_d, kT_d, v_d, kiT_d, lru_d):
    with ExitStack() as ctx:
        def sb(name, shape, dt=F32):
            return ctx.enter_context(nc.sbuf_tensor(name, shape, dt))

        def sem(name):
            return ctx.enter_context(nc.semaphore(name))

        bank = [ctx.enter_context(nc.psum_tensor(f"bank{i}", [P, 512], F32)) for i in range(8)]

        start = {}

        def region(name, shape):
            start[name] = nc.sbuf_base
            return sb(name, shape)

        def over(name, shape, place, offset, dt=F32R):
            return nc.alloc_sbuf_tensor_at(name, shape, dt, offset=start[place] + 4 * offset)

        regX = region("regX", [P, KT * NT])
        regR = region("regR", [P, KT * NT])
        regM = region("regM", [P, KT * NT])
        regQ = region("regQ", [P, KT * NT])
        wring = region("wring", [P, 2, 4096])
        arena = region("arena", [P, 17872])
        hn_hi = over("hn_hi", [P, KT, NT], "regR", 0)
        hn_lo = over("hn_lo", [P, KT, NT], "regQ", 0)
        h_hi = over("h_hi", [P, HT * NT], "arena", 0)
        h_lo = over("h_lo", [P, HT * NT], "arena", HT * NT)
        w_raw = wring[:, 0, 0:2 * PIECE].rearrange("p (s c) -> p s c", s=2)
        w_hi = over("w_hi", [P, 2, PIECE], "wring", 4096)
        w_lo = over("w_lo", [P, 2, PIECE], "wring", 4096 + 2 * PIECE)
        lx = sb("lx", [P, 6 * NT])
        scp = sb("scp", [P, 1152])
        qbd = sb("qbd", [P, DEC_BATCH, CT, 32])
        kwrow = sb("kwrow", [P, 5, 72])
        wgate = sb("wgate", [P, 2, CT, P])
        ident = sb("ident", [P, P])
        ones = sb("ones", [P, P])
        causal = sb("causal", [P, P])
        ind = sb("ind", [NS, GRP, P])
        wT = sb("wT", [NS, GRP, P])
        wm = sb("wm", [P, GRP, NS])
        newmask = sb("newmask", [NS, NS])
        par = sb("par", [P, NPAR])
        keyoff = sb("keyoff", [P, 1])
        pt_own = sb("pt_own", [P, DEC_BATCH], I32)
        row_i = sb("row_i", [P, DEC_BATCH], I32)
        kw_diag = sb("kw_diag", [P, KT * 72])
        wkw = kw_diag[:, :].rearrange("p (k c) -> p k c", k=KT)
        diag = kw_diag[:, 0:4 * P].rearrange("p (s c) -> p s c", s=4)
        qi_s = sb("qi_s", [P, CT, NS])
        q_s = sb("q_s", [P, CT, NS])
        m8 = sb("m8", [P, 3, 8])
        pack = sb("pack", [P, CT, 36])
        sp = sb("sp", [P, 8 * CT])
        eps = sb("eps", [P, 1])
        steps = sb("steps", [1, KSTEPS * 4], I32)
        stat = sb("stat", [P, 4, 4])
        sstat = sb("sstat", [P, GRP, 8])

        def tiles(region, n=KT):
            return region[:, 0:n * NT].rearrange("p (k t) -> p k t", t=NT)

        xT = tiles(regX)
        hnT = tiles(regR)
        mixT = tiles(regM)
        sqT = tiles(regQ)
        oT = tiles(regR)
        fT = tiles(regM)
        qz = regQ[:, 0:NH * SEQ].rearrange("p (h t) -> p h t", t=SEQ)
        kidxT = regX[:, 0:4096].rearrange("p (b c) -> p b c", b=4)
        S = regX[:, 0:GRP * NKEY].rearrange("p (g c) -> p g c", g=GRP)
        R = regM[:, 0:GRP * NKEY].rearrange("p (g c) -> p g c", g=GRP)
        work_s = regM[0:NS, 4 * NT:4 * NT + NKEY]
        work_p = regM[:, 4 * NT:4 * NT + 1152]
        pT = regR[:, 0:GRP * 17 * P].rearrange("p (g r c) -> p g r c", g=GRP, r=17)
        at = 0

        def carve(n):
            nonlocal at
            at += n
            return arena[:, at - n:at]

        kv = carve(3 * 2048).rearrange("p (s b c) -> p s b c", s=3, b=4)
        kidx_in_sb = arena[:, 0:4096].rearrange("p (b c) -> p b c", b=4)
        scs = carve(NKEY)[0:NS, :]
        kT = carve(CT * NT).rearrange("p (k t) -> p k t", t=NT)
        v = carve(5 * 512).rearrange("p (j c) -> p j c", j=5)
        xl = carve(CT * XW).rearrange("p (k t) -> p k t", t=XW)
        kiT = carve(NT)
        pTp_at = carve(1056)
        pTp = pTp_at[:, 0:1024].rearrange("p (s c) -> p s c", s=2)
        qis = pTp_at[:, 0:512].rearrange("p (b e c) -> p b e c", b=DEC_BATCH, e=2)
        kw = pTp_at[:, 512:1056]
        sm = carve(1024).rearrange("p (s c) -> p s c", s=2)
        probs = [sm[:, 0, :], sm[:, 1, :], lx[:, 0:512], lx[:, 512:1024]]
        probsT = [pTp[:, 0, :], pTp[:, 1, :], lx[:, 1024:1536], lx[:, 1536:2048]]
        so = lx[:, 2048:3072].rearrange("p (g c) -> p g c", g=GRP)
        raw = lx[:, 0:2 * NT].rearrange("p (s t) -> p s t", s=2)
        swp = lx[:, 2 * NT:4 * NT].rearrange("p (s t) -> p s t", s=2)
        cosT = lx[:, 4 * NT:5 * NT]
        sinT = lx[:, 5 * NT:6 * NT]
        xc, gi, ga, dd, aa = (lx[:, i * NT:(i + 1) * NT] for i in range(5))
        rms = lx[:, 0:NT]
        relu_t = lx[:, NT:3 * NT].rearrange("p (s t) -> p s t", s=2)
        square_t = lx[:, 3 * NT:5 * NT].rearrange("p (s t) -> p s t", s=2)

        wslot = [wring[:, s, :].rearrange("p (k c) -> p k c", k=KT) for s in range(2)]

        const_in = sem("const_in")
        steps_in = sem("steps_in")
        x_in = sem("x_in")
        kw_in = sem("kw_in")
        w_in = [sem("w_in_even"), sem("w_in_odd")]
        kidx_in = sem("kidx_in")
        q_placed = sem("q_placed")
        kv_in = [sem(f"kv_in{i}") for i in range(3)]
        x_again = sem("x_again")
        stored = sem("stored")
        state_stored = sem("state_stored")
        gemm_mm = sem("gemm_mm")
        gemm_ev = sem("gemm_ev")
        sq_rd = sem("sq_rd")
        ssq_mm = sem("ssq_mm")
        rms_rd = sem("rms_rd")
        rstd_rd = sem("rstd_rd")
        hn_rd = sem("hn_rd")
        x1_rd = sem("x1_rd")
        y_rd = sem("y_rd")
        rows_rd = sem("rows_rd")
        zero_rd = sem("zero_rd")
        lam_rd = sem("lam_rd")
        explam_rd = sem("explam_rd")
        rope_out = sem("rope_out")
        ki_dup = sem("ki_dup")
        wi_tr = sem("wi_tr")
        wi_rd = sem("wi_rd")
        wT_rd = sem("wT_rd")
        wT_tr = sem("wT_tr")
        wm_rd = sem("wm_rd")
        pi_mm = sem("pi_mm")
        pi_ev = sem("pi_ev")
        pi_acc = sem("pi_acc")
        qis_rd = sem("qis_rd")
        kx_tr = sem("kx_tr")
        kx_ev = sem("kx_ev")
        kd_mm = sem("kd_mm")
        kd_ev = sem("kd_ev")
        ks_mm = sem("ks_mm")
        ks_ev = sem("ks_ev")
        pmask_rd = sem("pmask_rd")
        smask_rd = sem("smask_rd")
        tk_p = sem("tk_p")
        tk_s = sem("tk_s")
        qbd_rd = sem("qbd_rd")
        k_mm = sem("k_mm")
        k_ev = sem("k_ev")
        kn_mm = sem("kn_mm")
        kn_ev = sem("kn_ev")
        sp_rd = sem("sp_rd")
        xc_rd = sem("xc_rd")
        lg_mm = sem("lg_mm")
        lg_ev = sem("lg_ev")
        tanh_rd = sem("tanh_rd")
        dd_rd = sem("dd_rd")
        root_rd = sem("root_rd")
        pk_rd = sem("pk_rd")
        pa_s = sem("pa_s")
        pa_m = sem("pa_m")
        pa_e = sem("pa_e")
        pa_n = sem("pa_n")
        pa_r = sem("pa_r")
        pa_t = sem("pa_t")
        pa_te = sem("pa_te")
        pa_o = sem("pa_o")
        pa_oe = sem("pa_oe")
        sm_mm = sem("sm_mm")
        sm_ev = sem("sm_ev")
        smax_rd = sem("smax_rd")
        se_rd = sem("se_rd")
        st_tr = sem("st_tr")
        st_ev = sem("st_ev")
        v_mm = sem("v_mm")
        so_rd = sem("so_rd")
        so_tr = sem("so_tr")
        so_ev = sem("so_ev")
        hn_f = sem("hn_f")
        hn_hi_rd = sem("hn_hi_rd")
        hn_lo_rd = sem("hn_lo_rd")
        piece_in = [sem("piece_in_even"), sem("piece_in_odd")]
        w_hi_rd = sem("w_hi_rd")
        w_lo_rd = sem("w_lo_rd")
        h_mm = sem("h_mm")
        h_ev = sem("h_ev")
        h_sq = sem("h_sq")
        h_hi_rd = sem("h_hi_rd")
        h_lo_rd = sem("h_lo_rd")
        half_mm = sem("half_mm")
        f_mm = sem("f_mm")
        f_ev = sem("f_ev")
        f_add = sem("f_add")
        f_sq = sem("f_sq")
        dve_step = sem("dve_step")
        act_step = sem("act_step")
        pool_step = sem("pool_step")

        block = ctx.enter_context(nc.Block())

        N_CONST = 9
        w_src = [w_in_d[i] for i in range(6)] + [w_out_d[i] for i in range(2)]

        @block.sync
        def _(eng):
            for hf in range(2):
                eng.dma_start(regX[:, hf * 4 * NT:(hf + 1) * 4 * NT], xT_d[:, hf * 4 * NT:(hf + 1) * 4 * NT]).then_inc(x_in, 16)
            eng.dma_start(steps[:, :], steps_d).then_inc(steps_in, 16)
            eng.dma_start(par[:, :], par_d).then_inc(const_in, 16)
            eng.dma_start(pt_own[:, :], bass.AP(tensor=ptT_d.tensor, offset=0, ap=[[DEC_BATCH, NPG], [0, 8], [1, DEC_BATCH]])).then_inc(const_in, 16)
            eng.dma_start(keyoff[:, :], keyoff_d).then_inc(const_in, 16)
            eng.dma_start(wring[:, 0, :], w_src[0]).then_inc(w_in[0], 16)
            eng.dma_start(wkw, w_kw_d).then_inc(kw_in, 16)
            eng.dma_start(lx[:, 4 * NT:6 * NT], rope_d).then_inc(const_in, 16)
            eng.dma_start(ident[:, :], ident_d).then_inc(const_in, 16)
            eng.dma_start(causal[:, :], causal_d).then_inc(const_in, 16)
            eng.dma_start(ind[:, :, :], ind_d).then_inc(const_in, 16)
            eng.dma_start(newmask[:, :], newmask_d).then_inc(const_in, 16)
            eng.dma_start(wgate[:, :, :, :], wgate_d).then_inc(const_in, 16)
            eng.dma_start(wring[:, 1, :], w_src[1]).then_inc(w_in[1], 16)

            page_regs = [eng.alloc_register(f"page{b4}") for b4 in range(4)]

            def stream(s, slot, table, freed, uses):
                eng.load(page_regs, steps[0:1, bass.ds(s * 4, 4)])
                page = [eng.snap(r, min_val=0, max_val=NPOOL - 1) for r in page_regs]
                if freed is not None:
                    eng.wait_ge(freed, uses)
                for b4 in range(4):
                    eng.dma_start(kv[:, slot, b4, :], table[bass.ds(page[b4], 1), :, :].rearrange("a p c -> p (a c)")).then_inc(kv_in[slot], 16)

            eng.wait_ge(steps_in, 16)
            stream(0, 2, ck_d, None, 0)
            stream(1, 0, ck_d, kx_tr, 16)
            stream(2, 1, ck_d, kx_tr, 16)
            with eng.Fori(0, 9) as i:
                for j in range(3):
                    stream(i * 3 + (3 + j), (j + 2) % 3, ck_d, k_mm, i * 3 + (j + 1))
            for s in (30, 31):
                stream(s, (s + 2) % 3, ck_d, k_mm, s - 2)
            for s in range(3):
                stream(s, (s + KSTEPS + 2) % 3, cv_d, k_mm, KSTEPS - 2 + s)
            with eng.Fori(0, 9) as i:
                for j in range(3):
                    stream(i * 3 + (3 + j), (j + KSTEPS + 2) % 3, cv_d, v_mm, i * 3 + (j + 1))
            for s in (30, 31):
                stream(s, (s + KSTEPS + 2) % 3, cv_d, v_mm, s - 2)
            eng.wait_ge(gemm_mm, E_WO + 8)
            for s in range(2):
                eng.dma_start(w_raw[:, s, :], w_mlp_d[s]).then_inc(piece_in[s], 16)
            with eng.Fori(0, PIECES // 2 - 1) as i:
                for s in range(2):
                    eng.wait_ge(w_lo_rd, i * 2 + (s + 1))
                    eng.dma_start(w_raw[:, s, :], w_mlp_d[bass.ds(i * 2 + (2 + s), 1), :, :].rearrange("a p c -> p (a c)")).then_inc(piece_in[s], 16)
            for k in range(KT):
                eng.wait_ge(y_rd, k + 1)
                eng.dma_start(yT_d[:, k, :], xT[:, k, :]).then_inc(stored, 16)
            eng.wait_ge(state_stored, 16 * 5)
            eng.wait_ge(stored, 16 * KT)

        ci_rows = ci_d.rearrange("n (s r) d -> (n s) (r d)", r=16)

        @block.gpsimd
        def _(eng):
            steps = [0]

            def link(ins):
                steps[0] += 1
                ins.then_inc(pool_step, 1)
                eng.wait_ge(pool_step, steps[0])

            def gather(dst, rows, index, landed):
                eng.indirect_dma_start(dst, None, rows, bass.IndirectOffsetOnAxis(ap=index, axis=0)).then_inc(landed, 16)

            eng.wait_ge(rows_rd, 1)
            for b in range(4):
                gather(kidx_in_sb[:, b, :], ci_rows, row_i[:, b:b + 1], kidx_in)

            def rope(t, out, parts=P):
                r, w = raw[0:parts, t % 2, :], swp[0:parts, t % 2, :]
                eng.wait_ge(gemm_ev, 2 * t + 2)
                nc.gpsimd.tensor_tensor(r, r, cosT[0:parts, :], ALU.mult)
                link(nc.gpsimd.tensor_tensor(w, w, sinT[0:parts, :], ALU.mult))
                nc.gpsimd.tensor_tensor(out, r, w, ALU.add).then_inc(rope_out, 1)

            eng.wait_ge(const_in, 16 * N_CONST)
            for t in range(CT):
                rope(t, raw[:, t % 2, :])
            rope(4, kiT[0:HD, :], HD)
            eng.wait_ge(kx_tr, 8)
            for b in range(4):
                gather(kidx_in_sb[:, b, :], ci_rows, row_i[:, 4 + b:5 + b], kidx_in)
            for t in range(5, 9):
                rope(t, raw[:, t % 2, :])
            for m in range(CT):
                rope(9 + m, kT[:, m, :])
            eng.wait_ge(rope_out, 13)
            eng.dma_start(kT_d, kT).then_inc(state_stored, 16)
            eng.dma_start(kiT_d, kiT[0:HD, :]).then_inc(state_stored, 16)
            eng.wait_ge(gemm_ev, E_WO)
            eng.dma_start(v_d[0:SEQ, :].rearrange("(j p) c -> p j c", p=P), v[:, 0:4, :]).then_inc(state_stored, 16)
            eng.dma_start(v_d[SEQ:NT, :], v[0:NS, 4, :]).then_inc(state_stored, 16)
            eng.wait_ge(st_tr, 10)
            eng.dma_start(regX[:, :], xT_d).then_inc(x_again, 16)
            eng.wait_ge(pk_rd, 4)
            eng.dma_start(lru_d, pack[:, :, :]).then_inc(state_stored, 16)
            for u in range(ATT_UNITS):
                eng.wait_ge(pa_r, u + 1)
                if u >= 4:
                    eng.wait_ge(pa_t, u - 3)
                nc.gpsimd.tensor_scalar(diag[:, u % 4, :], ident[:, :], stat[:, u % 4, 3:4], None, ALU.mult).then_inc(pa_n, 1)

            for s in range(2):
                eng.wait_ge(h_ev, 2 * s + 2)
                nc.gpsimd.tensor_tensor(square_t[:, s, :], relu_t[:, s, :], relu_t[:, s, :], ALU.mult).then_inc(h_sq, 1)
            with eng.Fori(0, (FT - 2) // 2) as i:
                for s in range(2):
                    eng.wait_ge(h_ev, i * 4 + (2 * s + 6))
                    eng.wait_ge(h_lo_rd, i * 2 + (s + 1))
                    nc.gpsimd.tensor_tensor(square_t[:, s, :], relu_t[:, s, :], relu_t[:, s, :], ALU.mult).then_inc(h_sq, 1)

        @block.scalar
        def _(eng):
            steps = [0]

            def link(ins):
                steps[0] += 1
                ins.then_inc(act_step, 1)
                eng.wait_ge(act_step, steps[0])

            def gemm_out(e):
                eng.wait_ge(gemm_mm, e + 1)
                return bank[e % 4]

            eng.wait_ge(lam_rd, 1)
            nc.scalar.activation(sp[:, 4 * CT:5 * CT], sp[:, 2 * CT:3 * CT], ACT.Exp).then_inc(explam_rd, 1)
            for k in range(KT):
                if k % 4 == 0:
                    eng.wait_ge(x_in, 32)
                nc.scalar.activation(hnT[:, k, :], xT[:, k, :], ACT.Square).then_inc(sq_rd, 1)

            def root_mean_square(n, zero=0):
                eng.wait_ge(ssq_mm, n)
                eng.wait_ge(zero_rd, 1)
                for hf in range(2):
                    ins = nc.scalar.activation(rms[:, hf * HALF:(hf + 1) * HALF], bank[4 + hf][:, 0:HALF], ACT.Sqrt,
                                               bias=eps[:, 0:1], scale=1.0 / D_MODEL)
                ins.then_inc(rms_rd, 1)

            root_mean_square(1)

            def rotary_tile(t, e, parts=P):
                if 2 <= t <= 5:
                    eng.wait_ge(q_placed, t - 1)
                elif 7 <= t <= 10:
                    eng.wait_ge(q_placed, t - 2)
                elif t in (6, 11, 12):
                    eng.wait_ge(rope_out, t - 1)
                elif t == 0:
                    eng.wait_ge(hn_rd, KT)
                for hf in range(2):
                    src = gemm_out(e + hf)
                    c = slice(hf * HALF, (hf + 1) * HALF)
                    nc.scalar.copy(raw[0:parts, t % 2, c], src[0:parts, 0:HALF])
                    for q in range(parts // 32):
                        last = nc.scalar.copy(swp[32 * q:32 * q + 32, t % 2, c], src[32 * (q ^ 1):32 * (q ^ 1) + 32, 0:HALF])
                    if parts == HD:
                        last = nc.scalar.copy(kw[HD:HD + NH, c], src[HD:HD + NH, 0:HALF])
                    last.then_inc(gemm_ev, 1)

            def load_block(n):
                eng.dma_start(wring[:, n % 2, :], w_src[n]).then_inc(w_in[n % 2], 16)

            def place_queries(t, m, compact):
                eng.wait_ge(rope_out, t + 1)
                nc.scalar.copy(qz[0:HD, 2 * m, :], raw[0:HD, t % 2, 0:SEQ])
                nc.scalar.copy(qz[HD:P, 2 * m + 1, :], raw[HD:P, t % 2, 0:SEQ])
                nc.scalar.copy(compact[:, m, :], raw[:, t % 2, SEQ:NT]).then_inc(q_placed, 1)

            eng.wait_ge(zero_rd, 2)
            for t in range(5):
                if t < CT:
                    rotary_tile(t, 2 * t)
                else:
                    rotary_tile(t, E_KW, HD)
                if t >= 1:
                    place_queries(t - 1, t - 1, qi_s)
            load_block(2)
            eng.wait_ge(rope_out, 5)
            nc.scalar.copy(kw[0:HD, :], kiT[0:HD, :])
            nc.scalar.copy(kiT[HD:P, :], kiT[0:HD, :]).then_inc(ki_dup, 1)
            eng.wait_ge(q_placed, CT)
            for e in range(2):
                for hh in range(2):
                    for m in range(CT):
                        dst = qis[HD * e:HD * e + HD, :, e, (2 * m + hh) * DEC_SEQ:(2 * m + hh + 1) * DEC_SEQ]
                        last = nc.scalar.copy(dst, qi_s[HD * hh:HD * hh + HD, m, :].rearrange("p (b t) -> p b t", t=DEC_SEQ))
            last.then_inc(qis_rd, 1)
            for u in range(24):
                nk = P * (u // NH + 2)
                eng.wait_ge(pi_mm, u + 1)
                if u >= 2:
                    eng.wait_ge(pi_acc, u - 1)
                nc.scalar.activation(sm[:, u % 2, 0:nk], bank[6 + u % 2][:, 0:nk], ACT.Relu, scale=IDX_SCALE).then_inc(pi_ev, 1)
            for g in range(GRP):
                for u in range(8):
                    eng.wait_ge(kx_tr, 8 * g + u + 1)
                    if g == 1 and u == 0:
                        eng.wait_ge(kd_mm, 5)
                    nc.scalar.copy(kidxT[:, u // 2, (u % 2) * 512:(u % 2) * 512 + 512], bank[4 + u % 2][:, :]).then_inc(kx_ev, 1)
                for d in range(5):
                    eng.wait_ge(kd_mm, 5 * g + d + 1)
                    b_ = bank[6 + (5 * g + d) % 2]
                    if d < 4:
                        e, ch = d // 2, d % 2
                        dst = R[:, g, 0:PAST].rearrange("p (j e k) -> p e j k", e=2, k=P)[:, e, 4 * ch:4 * ch + 4, :]
                        src = b_[:, :].rearrange("p (j k) -> p j k", k=P)
                    else:
                        dst, src = R[:, g, PAST:NKEY], b_[:, 0:NS]
                    nc.scalar.activation(dst, src, ACT.Relu, scale=IDX_SCALE).then_inc(kd_ev, 1)

            for m in range(CT + 1):
                if m < CT:
                    rotary_tile(5 + m, E_Q + 2 * m)
                if m == CT - 1:
                    load_block(3)
                if m >= 1:
                    place_queries(4 + m, m - 1, q_s)
            eng.wait_ge(q_placed, 2 * CT)
            for m in range(CT):
                for hh in range(2):
                    dst = qbd[HD * hh:HD * hh + HD, :, m, (2 * m + hh) * DEC_SEQ:(2 * m + hh + 1) * DEC_SEQ]
                    last = nc.scalar.copy(dst, q_s[HD * hh:HD * hh + HD, m, :].rearrange("p (b t) -> p b t", t=DEC_SEQ))
            last.then_inc(qbd_rd, 1)

            def sample_scores(s):
                eng.wait_ge(k_mm, s + 1)
                nc.scalar.mul(S[:, s // NPG, (s % NPG) * P:(s % NPG + 1) * P], bank[4 + s % 2][:, 0:P], SCALE).then_inc(k_ev, 1)

            for m in range(CT):
                rotary_tile(9 + m, E_K + 2 * m)
                sample_scores(2 * m)
                sample_scores(2 * m + 1)
            load_block(4)
            for m in range(CT):
                for hf in range(2):
                    e = E_XL + 2 * m + hf
                    src = gemm_out(e)
                    if hf == 0:
                        nc.scalar.copy(xl[:, m, 3:3 + HALF], src[:, 0:HALF]).then_inc(gemm_ev, 1)
                    else:
                        n = SEQ - HALF
                        nc.scalar.copy(xl[:, m, 3 + HALF:3 + SEQ], src[:, 0:n])
                        dst = xl[:, m, 3 + SEQ:XW].rearrange("p (b w) -> p b w", w=3 + DEC_SEQ)[:, :, 3:3 + DEC_SEQ]
                        nc.scalar.copy(dst, src[:, n:n + NS].rearrange("p (b t) -> p b t", t=DEC_SEQ)).then_inc(gemm_ev, 1)
                sample_scores(8 + 2 * m)
                sample_scores(8 + 2 * m + 1)
            load_block(5)
            for m in range(CT):
                for hf in range(2):
                    src = gemm_out(E_GATE + 2 * m + hf)
                    if m == 0 and hf == 0:
                        eng.wait_ge(ks_mm, 5)
                    nc.scalar.activation(mixT[:, m, hf * HALF:(hf + 1) * HALF], src[:, 0:HALF], ACT.Gelu_apprx_tanh).then_inc(gemm_ev, 1)
                sample_scores(16 + 2 * m)
                sample_scores(16 + 2 * m + 1)
            load_block(6)
            for j in range(5):
                src = gemm_out(E_V + j)
                n = P if j < 4 else NS
                nc.scalar.copy(v[0:n, j, :], src[0:n, :]).then_inc(gemm_ev, 1)
                if j < 4:
                    sample_scores(24 + 2 * j)
                    sample_scores(24 + 2 * j + 1)
            load_block(7)
            for g in range(GRP):
                eng.wait_ge(kn_mm, g + 1)
                nc.scalar.mul(S[:, g, PAST:NKEY], bank[4 + g][:, 0:NS], SCALE).then_inc(kn_ev, 1)

            for g in range(GRP):
                eng.wait_ge(smax_rd, g + 1)
                nc.scalar.activation(S[:, g, :], S[:, g, :], ACT.Exp, bias=sstat[:, g, 6:7], accum_out=sstat[:, g, 7:8]).then_inc(se_rd, 1)
            for g in range(GRP):
                for q in range(5):
                    n = 5 * g + q
                    eng.wait_ge(st_tr, n + 1)
                    if q < 4:
                        ins = nc.scalar.copy(pT[:, g, 4 * q:4 * q + 4, :], bank[2 + n % 2][:, :].rearrange("p (r c) -> p r c", r=4))
                    else:
                        ins = nc.scalar.copy(pT[0:NS, g, 16, :], bank[2 + n % 2][0:NS, 0:P])
                    ins.then_inc(st_ev, 1)
            eng.wait_ge(sp_rd, 1)
            for c in range(CT):
                for u in range(4):
                    gate, hf = u // 2, u % 2
                    eng.wait_ge(lg_mm, 4 * c + u + 1)
                    if u == 0 and c > 0:
                        eng.wait_ge(pk_rd, c)
                    bias = par[:, (B_A, B_I)[gate] + c:(B_A, B_I)[gate] + c + 1]
                    nc.scalar.activation((ga, gi)[gate][:, hf * HALF:(hf + 1) * HALF], bank[6 + u % 2][:, 0:HALF],
                                         ACT.Sigmoid, bias=bias).then_inc(lg_ev, 1)
                eng.wait_ge(lg_ev, 4 * c + 4)
                link(nc.scalar.activation(aa, ga, ACT.Exp, scale=sp[:, c:c + 1]))
                nc.scalar.activation(dd, aa, ACT.Square)
                nc.scalar.activation(ga, ga, ACT.Tanh, scale=sp[:, c:c + 1]).then_inc(tanh_rd, 1)
                eng.wait_ge(dd_rd, c + 1)
                nc.scalar.activation(dd, dd, ACT.Sqrt, scale=-1.0).then_inc(root_rd, 1)

            def exponentials(u):
                nk = P * (u // NH + 1)
                eng.wait_ge(pa_m, u + 1)
                nc.scalar.activation(probs[u % 4][:, 0:nk], probs[u % 4][:, 0:nk], ACT.Exp, bias=stat[:, u % 4, 1:2],
                                     accum_out=stat[:, u % 4, 2:3]).then_inc(pa_e, 1)

            def transposed_out(u):
                nk = P * (u // NH + 1)
                eng.wait_ge(pa_t, u + 1)
                if u == 0:
                    eng.wait_ge(kd_mm, 10)
                nc.scalar.copy(probsT[u % 4][:, 0:nk], bank[6 + u % 2][:, 0:nk]).then_inc(pa_te, 1)

            for u in range(ATT_UNITS + 2):
                if u < ATT_UNITS:
                    exponentials(u)
                if u >= 2:
                    transposed_out(u - 2)

            for g in range(GRP):
                eng.wait_ge(so_tr, g + 1)
                for m in range(CT):
                    for hh in range(2):
                        h = 2 * m + hh
                        src = bank[6 + g][HD * hh:HD * hh + HD, m * P:(m + 1) * P].rearrange("p (b h t) -> p b h t", b=4, h=NH)[:, :, h, :]
                        dst = mixT[HD * hh:HD * hh + HD, 4 + m, SEQ + 16 * g:SEQ + 16 * g + 16].rearrange("p (b t) -> p b t", b=4)
                        last = nc.scalar.copy(dst, src)
                last.then_inc(so_ev, 1)

            def with_squares(dst, e0, m, hf):
                src = gemm_out(e0 + 2 * m + hf)
                c = slice(hf * HALF, (hf + 1) * HALF)
                nc.scalar.copy(dst[:, m, c], src[:, 0:HALF])
                nc.scalar.activation(sqT[:, m, c], src[:, 0:HALF], ACT.Square).then_inc(gemm_ev, 1)

            for m in range(KT):
                for hf in range(2):
                    with_squares(oT, E_WO, m, hf)
            root_mean_square(2)
            for k in range(KT):
                eng.wait_ge(x1_rd, k + 1)
                if k == 0:
                    eng.wait_ge(ssq_mm, 2)
                nc.scalar.activation(sqT[:, k, :], xT[:, k, :], ACT.Square).then_inc(sq_rd, 1)
            root_mean_square(3)
            for k in range(KT):
                eng.wait_ge(hn_f, k + 1)
                nc.scalar.copy(hn_hi[:, k, :], relu_t[:, k % 2, :]).then_inc(hn_hi_rd, 1)

            def round_piece(n, parity, freed, uses):
                eng.wait_ge(freed, uses)
                eng.wait_ge(piece_in[parity], (n - parity) * 8 + 16)
                nc.scalar.copy(w_hi[:, parity, :], w_raw[:, parity, :]).then_inc(w_hi_rd, 1)

            def rectify(j, parity, wait=True):
                for hf in range(2):
                    u = j * 2 + hf
                    if hf == 0 and wait:
                        eng.wait_ge(h_sq, j - 1)
                    eng.wait_ge(h_mm, u + 1)
                    nc.scalar.activation(relu_t[:, parity, hf * HALF:(hf + 1) * HALF], bank[(2 * parity + hf) % 4][:, 0:HALF], ACT.Relu).then_inc(h_ev, 1)

            def round_hidden(j, half, parity):
                eng.wait_ge(h_sq, j + 1)
                nc.scalar.copy(h_hi[:, bass.ds((j - half * HT) * NT, NT)], square_t[:, parity, :]).then_inc(h_hi_rd, 1)

            def weighted(v, parity, hf):
                eng.wait_ge(f_mm, v + 1)
                return bank[(2 * parity + hf) % 4][:, 0:HALF]

            eng.wait_ge(state_stored, 16 * 5)
            round_piece(0, 0, gemm_mm, E_MIX)
            for half in range(2):
                j0, n0, v0 = half * HT, half * PIECES // 2, half * 2 * KT
                if half == 0:
                    round_piece(1, 1, gemm_mm, E_MIX)
                else:
                    round_piece(n0 + 1, 1, f_mm, v0)
                rectify(j0, 0, half > 0)
                round_piece(n0 + 2, 0, h_mm, 2 * j0 + 2)
                rectify(j0 + 1, 1, half > 0)
                round_hidden(j0, half, 0)
                with eng.Fori(0, HT // 2 - 1) as i:
                    for s in range(2):
                        j = i * 2 + (j0 + 2 + s)
                        round_piece(i * 2 + (n0 + 3 + s), (1 + s) % 2, h_mm, i * 4 + (2 * j0 + 4 + 2 * s))
                        rectify(j, s)
                        round_hidden(i * 2 + (j0 + 1 + s), half, (1 + s) % 2)
                round_hidden(j0 + HT - 1, half, 1)
                round_piece(n0 + HT + 1, 1, h_mm, 2 * (j0 + HT))
                round_piece(n0 + HT + 2, 0, half_mm, KT * half + 1)

                def output(m, parity, last=False):
                    if half == 0:
                        for hf in range(2):
                            src = weighted(m * 2 + (v0 + hf), parity, hf)
                            nc.scalar.copy(regM[:, bass.ds(m * NT + hf * HALF, HALF)], src).then_inc(f_ev, 1)
                    else:
                        for hf in range(2):
                            eng.wait_ge(f_add, m * 2 + (hf + 1))
                            c = m * NT + hf * HALF
                            nc.scalar.activation(regQ[:, bass.ds(c, HALF)], regM[:, bass.ds(c, HALF)], ACT.Square).then_inc(f_sq, 1)

                output(0, 0)
                with eng.Fori(0, (KT - 2) // 2) as i:
                    for s in range(2):
                        m = i * 2 + (1 + s)
                        round_piece(i * 4 + (n0 + HT + 3 + 2 * s), 1, f_mm, i * 4 + (v0 + 2 + 2 * s))
                        round_piece(i * 4 + (n0 + HT + 4 + 2 * s), 0, half_mm, i * 2 + (KT * half + 2 + s))
                        output(m, (1 + s) % 2)
                round_piece(n0 + HT + 2 * KT - 1, 1, f_mm, v0 + 2 * KT - 2)
                if half == 0:
                    round_piece(n0 + HT + 2 * KT, 0, half_mm, KT)
                output(KT - 1, 1)
            root_mean_square(4)

        @block.vector
        def _(eng):
            steps = [0]
            vec = nc.vector

            def link(ins):
                steps[0] += 1
                ins.then_inc(dve_step, 1)
                eng.wait_ge(dve_step, steps[0])

            vec.memset(eps[:, :], EPS)
            vec.memset(ones[:, :], 1.0).then_inc(zero_rd, 1)
            vec.memset(regQ[:, :], 0.0)
            vec.memset(pTp_at[:, 0:512], 0.0)
            vec.memset(qbd[:, :, :, :], 0.0)
            vec.memset(xl[:, :, 0:3], 0.0).then_inc(zero_rd, 1)
            eng.wait_ge(const_in, 16 * N_CONST)
            vec.tensor_scalar(row_i[:, :], pt_own[:, :], float(PAGE // 16), keyoff[:, 0:1], ALU.mult, ALU.add).then_inc(rows_rd, 1)
            for c in range(CT):
                dst = xl[:, c, 3 + SEQ:XW].rearrange("p (b w) -> p b w", w=3 + DEC_SEQ)[:, :, 0:3]
                src = par[:, CONV0 + 24 * c:CONV0 + 24 * c + 24].rearrange("p (b w) -> p b w", w=3)
                vec.tensor_copy(dst, src)

            lam, z = par[:, LAM:LAM + CT], sp[:, CT:2 * CT]
            link(vec.tensor_scalar(z, lam, -1.0, None, ALU.mult))
            link(vec.tensor_tensor(sp[:, 2 * CT:3 * CT], lam, z, ALU.min))
            vec.tensor_scalar(sp[:, 3 * CT:4 * CT], z, 0.0, None, ALU.max).then_inc(lam_rd, 1)
            eng.wait_ge(explam_rd, 1)
            ez, s1, s2, acc = (sp[:, i * CT:(i + 1) * CT] for i in (4, 5, 6, 7))
            link(vec.tensor_scalar(s1, ez, 2.0, None, ALU.add))
            link(vec.reciprocal(s1, s1))
            link(vec.tensor_tensor(s1, s1, ez, ALU.mult))
            link(vec.tensor_tensor(s2, s1, s1, ALU.mult))
            link(vec.tensor_scalar(acc, s2, 1.0 / 17, None, ALU.mult))
            for odd in range(15, 1, -2):
                link(vec.scalar_tensor_tensor(out=acc, in0=acc, scalar=1.0 / odd, in1=s2, op0=ALU.add, op1=ALU.mult))
            link(vec.scalar_tensor_tensor(out=acc, in0=acc, scalar=1.0, in1=s1, op0=ALU.add, op1=ALU.mult))
            link(vec.scalar_tensor_tensor(out=acc, in0=acc, scalar=2.0, in1=sp[:, 3 * CT:4 * CT], op0=ALU.mult, op1=ALU.add))
            vec.tensor_scalar(sp[:, 0:CT], acc, -RG_C, None, ALU.mult).then_inc(sp_rd, 1)


            def recip_rms(n):
                eng.wait_ge(rms_rd, n)
                vec.reciprocal(rms, rms).then_inc(rstd_rd, 1)
                eng.wait_ge(rstd_rd, n)

            recip_rms(1)
            for k in range(KT):
                vec.scalar_tensor_tensor(out=hnT[:, k, :], in0=xT[:, k, :], scalar=par[:, G_PRE_MIX + k:G_PRE_MIX + k + 1],
                                         in1=rms, op0=ALU.mult, op1=ALU.mult).then_inc(hn_rd, 1)

            eng.wait_ge(wi_tr, 1)
            vec.tensor_copy(kwrow[:, 0:4, :], bank[6][:, 0:288].rearrange("p (j c) -> p j c", j=4))
            vec.tensor_copy(kwrow[0:NS, 4, :], bank[6][0:NS, 288:360]).then_inc(wi_rd, 1)
            eng.wait_ge(wi_rd, 1)
            for g in range(GRP):
                wi = kwrow[0:NS, 4, HD:HD + NH].unsqueeze(1).unsqueeze(3).to_broadcast([NS, 4, NH, DEC_SEQ])
                ins = vec.tensor_tensor(wT[:, g, :].rearrange("p (b h t) -> p b h t", b=4, h=NH),
                                        ind[:, g, :].rearrange("p (b h t) -> p b h t", b=4, h=NH), wi, ALU.mult)
            ins.then_inc(wT_rd, 1)
            eng.wait_ge(wT_tr, 1)
            vec.tensor_copy(wm[:, :, :], bank[7][:, 0:GRP * NS].rearrange("p (g c) -> p g c", g=GRP)).then_inc(wm_rd, 1)
            for u in range(24):
                n, h = u // NH + 1, u % NH
                nk = P * (n + 1)
                acc = scp[:, SCP_AT[n]:SCP_AT[n] + nk]
                w = kwrow[:, n, HD + h:HD + h + 1]
                eng.wait_ge(pi_ev, u + 1)
                if h == 0:
                    ins = vec.tensor_scalar(acc, sm[:, u % 2, 0:nk], w, None, ALU.mult)
                else:
                    ins = vec.scalar_tensor_tensor(out=acc, in0=sm[:, u % 2, 0:nk], scalar=w, in1=acc, op0=ALU.mult, op1=ALU.add)
                ins.then_inc(pi_acc, 1)
                eng.wait_ge(pi_acc, u + 1)
            for n in range(1, QB):
                last = scp[:, SCP_AT[n] + n * P:SCP_AT[n] + (n + 1) * P]
                link(vec.tensor_tensor(last, last, causal[:, :], ALU.add))
            for c in range(5):
                eng.wait_ge(ks_mm, c + 1)
                if c < 4:
                    dst = scs[:, 0:PAST].rearrange("q (p r) -> q r p", r=16)[:, 4 * c:4 * c + 4, :]
                    ins = vec.tensor_copy(dst, bank[4 + c % 2][0:NS, :].rearrange("q (r p) -> q r p", r=4))
                else:
                    ins = vec.tensor_tensor(scs[:, PAST:NKEY], bank[4][0:NS, 0:NS], newmask[:, :], ALU.add)
                ins.then_inc(ks_ev, 1)
            eng.wait_ge(ks_ev, 5)

            link(vec.tensor_copy(work_p, scp[:, :]))
            wp = {n: work_p[:, SCP_AT[n]:SCP_AT[n] + P * (n + 1)] for n in range(1, QB)}
            for i in range(TOPK_P // 8):
                for n in range(1, QB):
                    vec.max(m8[:, n - 1, :], wp[n]).then_inc(tk_p, 1)
                for n in range(1, QB):
                    eng.wait_ge(tk_p, 6 * i + n)
                    vec.match_replace(wp[n], m8[:, n - 1, :], wp[n], TAKEN).then_inc(tk_p, 1)
                eng.wait_ge(tk_p, 6 * i + 6)
            link(vec.tensor_tensor(work_p, work_p, scp[:, :], ALU.not_equal))
            link(vec.tensor_scalar(scp[:, :], work_p, -OUT_OF_REACH, OUT_OF_REACH, ALU.mult, ALU.add))
            link(vec.tensor_copy(work_s, scs))
            for i in range(TOPK_S // 8):
                vec.max(m8[0:NS, 0, :], work_s).then_inc(tk_s, 1)
                eng.wait_ge(tk_s, 2 * i + 1)
                vec.match_replace(work_s, m8[0:NS, 0, :], work_s, TAKEN).then_inc(tk_s, 1)
                eng.wait_ge(tk_s, 2 * i + 2)
            link(vec.tensor_tensor(work_s, work_s, scs, ALU.not_equal))
            vec.tensor_scalar(scs, work_s, -OUT_OF_REACH, OUT_OF_REACH, ALU.mult, ALU.add).then_inc(smask_rd, 1)

            for g in range(GRP):
                for c in range(5):
                    n = 5 * g + c
                    cols = slice(c * 512, min((c + 1) * 512, NKEY))
                    w = cols.stop - cols.start
                    eng.wait_ge(sm_mm, n + 1)
                    eng.wait_ge(kn_ev, g + 1)
                    vec.tensor_tensor_reduce(out=S[:, g, cols], in0=S[:, g, cols], in1=bank[2 + n % 2][:, 0:w], scale=1.0, scalar=TAKEN,
                                             op0=ALU.add, op1=ALU.max, accum_out=sstat[:, g, c:c + 1]).then_inc(sm_ev, 1)
                eng.wait_ge(sm_ev, 5 * g + 5)
                link(vec.tensor_reduce(sstat[:, g, 5:6], sstat[:, g, 0:5], AX_X, ALU.max))
                vec.tensor_scalar(sstat[:, g, 6:7], sstat[:, g, 5:6], -1.0, None, ALU.mult).then_inc(smax_rd, 1)
            eng.wait_ge(gemm_ev, E_V)
            eng.wait_ge(rope_out, 13)
            for c in range(CT):
                def window(j):
                    prompt = xl[:, c, j:j + SEQ]
                    sample = xl[:, c, 3 + SEQ:XW].rearrange("p (b w) -> p b w", w=3 + DEC_SEQ)[:, :, j:j + DEC_SEQ]
                    return prompt, sample

                outs = (xc[:, 0:SEQ], xc[:, SEQ:NT].rearrange("p (b t) -> p b t", t=DEC_SEQ))
                for j in range(4):
                    w = par[:, CONV_W0 + 4 * j + c:CONV_W0 + 4 * j + c + 1]
                    for o, x in zip(outs, window(j)):
                        if j == 0:
                            ins = vec.tensor_scalar(o, x, w, par[:, CONV_B + c:CONV_B + c + 1], ALU.mult, ALU.add)
                        else:
                            ins = vec.scalar_tensor_tensor(out=o, in0=x, scalar=w, in1=o, op0=ALU.mult, op1=ALU.add)
                    if j < 3:
                        link(ins)
                ins.then_inc(xc_rd, 1)
                eng.wait_ge(lg_ev, 4 * c + 4)
                link(vec.tensor_tensor(gi, gi, xc, ALU.mult))
                eng.wait_ge(tanh_rd, c + 1)
                vec.scalar_tensor_tensor(out=dd, in0=dd, scalar=1.0, in1=ga, op0=ALU.add, op1=ALU.mult).then_inc(dd_rd, 1)
                eng.wait_ge(root_rd, c + 1)
                link(vec.tensor_tensor(gi, gi, dd, ALU.mult))
                a0 = aa[:, SEQ:NT].rearrange("p (b t) -> p b t", t=DEC_SEQ)[:, :, 0]
                u0 = gi[:, SEQ:NT].rearrange("p (b t) -> p b t", t=DEC_SEQ)[:, :, 0]
                link(vec.tensor_tensor(ga[:, 0:DEC_BATCH], a0, par[:, H0 + 8 * c:H0 + 8 * c + 8], ALU.mult))
                vec.tensor_tensor(u0, u0, ga[:, 0:DEC_BATCH], ALU.add)
                link(vec.memset(a0, 0.0))
                link(vec.tensor_tensor_scan(dd, aa, gi, 0.0, ALU.mult, ALU.add))
                vec.tensor_tensor(mixT[:, c, :], mixT[:, c, :], dd, ALU.mult)
                vec.tensor_copy(pack[:, c, 0:3], xl[:, c, SEQ:SEQ + 3])
                vec.tensor_copy(pack[:, c, 3:27].rearrange("p (b t) -> p b t", t=3),
                                xl[:, c, 3 + SEQ:XW].rearrange("p (b w) -> p b w", w=3 + DEC_SEQ)[:, :, DEC_SEQ:DEC_SEQ + 3])
                vec.tensor_copy(pack[:, c, 27:28], dd[:, SEQ - 1:SEQ])
                vec.tensor_copy(pack[:, c, 28:36], dd[:, SEQ:NT].rearrange("p (b t) -> p b t", t=DEC_SEQ)[:, :, DEC_SEQ - 1]).then_inc(pk_rd, 1)
                eng.wait_ge(pk_rd, c + 1)

            def masked(u):
                n, h = u // NH, u % NH
                nk = P * (n + 1)
                mask = causal[:, :] if n == 0 else scp[:, SCP_AT[n]:SCP_AT[n] + nk]
                eng.wait_ge(pa_s, u + 1)
                if u >= 4:
                    eng.wait_ge(pa_t, u - 3)
                link(vec.tensor_tensor_reduce(out=probs[u % 4][:, 0:nk], in0=bank[4 + u % 2][:, 0:nk], in1=mask, scale=SCALE, scalar=TAKEN,
                                              op0=ALU.add, op1=ALU.max, accum_out=stat[:, u % 4, 0:1]))
                vec.tensor_scalar(stat[:, u % 4, 1:2], stat[:, u % 4, 0:1], -1.0, None, ALU.mult).then_inc(pa_m, 1)

            def row_sum(u):
                eng.wait_ge(pa_e, u + 1)
                vec.reciprocal(stat[:, u % 4, 3:4], stat[:, u % 4, 2:3]).then_inc(pa_r, 1)

            def pair_out(w):
                eng.wait_ge(pa_o, w + 1)
                n, m = w // CT, w % CT
                vec.tensor_copy(mixT[:, 4 + m, n * P:(n + 1) * P], bank[w % 2][:, 0:P]).then_inc(pa_oe, 1)

            for u in range(ATT_UNITS + 5):
                if u < ATT_UNITS:
                    masked(u)
                if 1 <= u <= ATT_UNITS:
                    row_sum(u - 1)
                if u >= 6 and u % 2 == 0:
                    pair_out((u - 6) // 2)

            for g in range(GRP):
                eng.wait_ge(se_rd, g + 1)
                link(vec.reciprocal(sstat[:, g, 0:1], sstat[:, g, 7:8]))
            for g in range(GRP):
                eng.wait_ge(v_mm, 16 * (g + 1))
                vec.tensor_scalar(so[:, g, :], bank[2 + g][:, :], sstat[:, g, 0:1], None, ALU.mult).then_inc(so_rd, 1)

            eng.wait_ge(x_again, 16)
            recip_rms(2)
            for k in range(KT):
                link(vec.scalar_tensor_tensor(out=oT[:, k, :], in0=oT[:, k, :], scalar=par[:, G_POST_MIX + k:G_POST_MIX + k + 1],
                                              in1=rms, op0=ALU.mult, op1=ALU.mult))
                vec.tensor_tensor(xT[:, k, :], xT[:, k, :], oT[:, k, :], ALU.add).then_inc(x1_rd, 1)
            recip_rms(3)
            eng.wait_ge(x1_rd, KT)

            def rest_of_input(k):
                eng.wait_ge(hn_hi_rd, k + 1)
                vec.tensor_tensor(hn_lo[:, k, :], relu_t[:, k % 2, :], hn_hi[:, k, :].bitcast(F32), ALU.subtract).then_inc(hn_lo_rd, 1)

            for k in range(KT):
                if k >= 2:
                    eng.wait_ge(hn_lo_rd, k - 1)
                vec.scalar_tensor_tensor(out=relu_t[:, k % 2, :], in0=xT[:, k, :], scalar=par[:, G_PRE_FFN + k:G_PRE_FFN + k + 1],
                                         in1=rms, op0=ALU.mult, op1=ALU.mult).then_inc(hn_f, 1)
                if k >= 1:
                    rest_of_input(k - 1)
            rest_of_input(KT - 1)

            def rest_of_piece(n, parity):
                eng.wait_ge(w_hi_rd, n + 1)
                vec.tensor_tensor(w_lo[:, parity, :], w_raw[:, parity, :], w_hi[:, parity, :].bitcast(F32), ALU.subtract).then_inc(w_lo_rd, 1)

            def rest_of_hidden(j, half, parity):
                at = bass.ds((j - half * HT) * NT, NT)
                eng.wait_ge(h_hi_rd, j + 1)
                vec.tensor_tensor(h_lo[:, at], square_t[:, parity, :], h_hi[:, at].bitcast(F32), ALU.subtract).then_inc(h_lo_rd, 1)

            rest_of_piece(0, 0)
            for half in range(2):
                j0, n0, v0 = half * HT, half * PIECES // 2, half * 2 * KT
                rest_of_piece(n0 + 1, 1)
                rest_of_piece(n0 + 2, 0)
                rest_of_hidden(j0, half, 0)
                with eng.Fori(0, HT // 2 - 1) as i:
                    for s in range(2):
                        rest_of_piece(i * 2 + (n0 + 3 + s), (1 + s) % 2)
                        rest_of_hidden(i * 2 + (j0 + 1 + s), half, (1 + s) % 2)
                rest_of_hidden(j0 + HT - 1, half, 1)
                rest_of_piece(n0 + HT + 1, 1)
                rest_of_piece(n0 + HT + 2, 0)

                def add_output(m, parity):
                    if half == 1:
                        for hf in range(2):
                            out = regM[:, bass.ds(m * NT + hf * HALF, HALF)]
                            eng.wait_ge(f_mm, m * 2 + (v0 + hf + 1))
                            vec.tensor_tensor(out, out, bank[(2 * parity + hf) % 4][:, 0:HALF], ALU.add).then_inc(f_add, 1)

                add_output(0, 0)
                with eng.Fori(0, (KT - 2) // 2) as i:
                    for s in range(2):
                        rest_of_piece(i * 4 + (n0 + HT + 3 + 2 * s), 1)
                        rest_of_piece(i * 4 + (n0 + HT + 4 + 2 * s), 0)
                        add_output(i * 2 + (1 + s), (1 + s) % 2)
                rest_of_piece(n0 + HT + 2 * KT - 1, 1)
                if half == 0:
                    rest_of_piece(n0 + HT + 2 * KT, 0)
                add_output(KT - 1, 1)
            recip_rms(4)
            for k in range(KT):
                link(vec.scalar_tensor_tensor(out=fT[:, k, :], in0=fT[:, k, :], scalar=par[:, G_POST_FFN + k:G_POST_FFN + k + 1],
                                              in1=rms, op0=ALU.mult, op1=ALU.mult))
                vec.tensor_tensor(xT[:, k, :], xT[:, k, :], fT[:, k, :], ALU.add).then_inc(y_rd, 1)

        @block.tensor
        def _(eng):
            pe = nc.tensor

            def ssq(squares, ready):
                for k in range(KT):
                    ready(k)
                    for hf in range(2):
                        ins = pe.matmul(bank[4 + hf][:, 0:HALF], ones[:, :], squares[:, k, hf * HALF:(hf + 1) * HALF],
                                        start=(k == 0), stop=(k == KT - 1))
                ins.then_inc(ssq_mm, 1)

            def slot_free(e):
                if e >= 4:
                    eng.wait_ge(gemm_ev, e - 3)

            def product(e, hf, lhs, rhs, parts=P):
                slot_free(e)
                for k in range(KT):
                    ins = pe.matmul(bank[e % 4][0:parts, 0:HALF], lhs(k), rhs[:, k, hf * HALF:(hf + 1) * HALF],
                                    start=(k == 0), stop=(k == KT - 1))
                ins.then_inc(gemm_mm, 1)

            def tile_product(e, w, m, rhs):
                for hf in range(2):
                    product(e + hf, hf, lambda k: w[:, k, m * P:(m + 1) * P], rhs)

            def weights(n):
                eng.wait_ge(w_in[n % 2], 16 * (n // 2 + 1))
                return wslot[n % 2]

            eng.wait_ge(zero_rd, 1)
            ssq(hnT, lambda k: eng.wait_ge(sq_rd, k + 1))
            eng.wait_ge(hn_rd, KT)
            w = weights(0)
            for m in range(CT):
                tile_product(E_QI + 2 * m, w, m, hnT)
            eng.wait_ge(kw_in, 16)
            for hf in range(2):
                product(E_KW + hf, hf, lambda k: wkw[:, k, :], hnT, 72)
            eng.wait_ge(ki_dup, 1)
            eng.wait_ge(const_in, 16 * N_CONST)
            for j in range(5):
                n = P if j < 4 else NS
                ins = pe.transpose(bank[6][0:n, 72 * j:72 * j + 72], kw[0:72, j * P:j * P + n], ident[0:72, 0:72])
            ins.then_inc(wi_tr, 1)
            eng.wait_ge(wT_rd, 1)
            for g in range(GRP):
                ins = pe.transpose(bank[7][:, g * NS:(g + 1) * NS], wT[:, g, :], ident[0:NS, 0:NS])
            ins.then_inc(wT_tr, 1)
            eng.wait_ge(zero_rd, 2)
            eng.wait_ge(q_placed, CT)
            for u in range(24):
                n, h = u // NH + 1, u % NH
                nk = P * (n + 1)
                if u >= 2:
                    eng.wait_ge(pi_ev, u - 1)
                elif u == 1:
                    eng.wait_ge(wm_rd, 1)
                pe.matmul(bank[6 + u % 2][:, 0:nk], qz[:, h, n * P:(n + 1) * P], kiT[:, 0:nk], start=True, stop=True).then_inc(pi_mm, 1)
            eng.wait_ge(qis_rd, 1)
            for g in range(GRP):
                eng.wait_ge(kidx_in, 64 * (g + 1))
                for u in range(8):
                    n = 8 * g + u
                    if n >= 2:
                        eng.wait_ge(kx_ev, n - 1)
                    for j in range(4):
                        ins = pe.transpose(bank[4 + u % 2][:, j * P:(j + 1) * P],
                                           kidx_in_sb[:, u // 2, ((u % 2) * 4 + j) * P:((u % 2) * 4 + j + 1) * P], ident[:, :])
                    ins.then_inc(kx_tr, 1)
                eng.wait_ge(kx_ev, 8 * g + 8)
                for d in range(5):
                    n = 5 * g + d
                    if n >= 2:
                        eng.wait_ge(kd_ev, n - 1)
                    else:
                        eng.wait_ge(pi_ev, 24)
                    for b4 in range(4):
                        e, ch = (d // 2, d % 2) if d < 4 else (0, 0)
                        rhs = kidxT[:, b4, ch * 512:ch * 512 + 512] if d < 4 else kiT[:, SEQ:NT]
                        w_ = 512 if d < 4 else NS
                        ins = pe.matmul(bank[6 + n % 2][32 * b4:32 * b4 + 32, 0:w_], qis[:, 4 * g + b4, e, :], rhs, start=True, stop=True)
                    ins.then_inc(kd_mm, 1)
            eng.wait_ge(kd_ev, 10)
            eng.wait_ge(wm_rd, 1)
            for c in range(5):
                cols = slice(c * 512, min((c + 1) * 512, NKEY))
                if c >= 2:
                    eng.wait_ge(ks_ev, c - 1)
                for g in range(GRP):
                    ins = pe.matmul(bank[4 + c % 2][0:NS, 0:cols.stop - cols.start], wm[:, g, :], R[:, g, cols],
                                    start=(g == 0), stop=(g == GRP - 1))
                ins.then_inc(ks_mm, 1)

            w = weights(1)
            for m in range(CT):
                tile_product(E_Q + 2 * m, w, m, hnT)

            def key_scores(s):
                slot = (s + 2) % 3
                eng.wait_ge(kv_in[slot], 64 * (s // 3 + 1))
                if s >= 2:
                    eng.wait_ge(k_ev, s - 1)
                elif s == 0:
                    eng.wait_ge(qbd_rd, 1)
                    eng.wait_ge(ks_ev, 5)
                for m in range(CT):
                    for b4 in range(4):
                        ins = pe.matmul(bank[4 + s % 2][32 * b4:32 * b4 + 32, 0:P], qbd[:, 4 * (s // NPG) + b4, m, :],
                                        kv[:, slot, b4, m * P:(m + 1) * P], start=(m == 0), stop=(m == CT - 1))
                ins.then_inc(k_mm, 1)

            step = 0
            for n, e0 in ((2, E_K), (3, E_XL), (4, E_GATE)):
                w = weights(n)
                for m in range(CT):
                    tile_product(e0 + 2 * m, w, m, hnT)
                    key_scores(step)
                    key_scores(step + 1)
                    step += 2
            w = weights(5)
            for j in range(5):
                n = P if j < 4 else NS
                e = E_V + j
                slot_free(e)
                for k in range(KT):
                    ins = pe.matmul(bank[e % 4][0:n, :], hnT[:, k, j * P:j * P + n], w[:, k, :], start=(k == 0), stop=(k == KT - 1))
                ins.then_inc(gemm_mm, 1)
                if j < 4:
                    key_scores(step)
                    key_scores(step + 1)
                    step += 2
            eng.wait_ge(rope_out, 13)
            for g in range(GRP):
                eng.wait_ge(k_ev, KSTEPS)
                for m in range(CT):
                    for b4 in range(4):
                        ins = pe.matmul(bank[4 + g][32 * b4:32 * b4 + 32, 0:NS], qbd[:, 4 * g + b4, m, :], kT[:, m, SEQ:NT],
                                        start=(m == 0), stop=(m == CT - 1))
                ins.then_inc(kn_mm, 1)
            eng.wait_ge(smask_rd, 1)
            eng.wait_ge(gemm_ev, E_WO)
            for g in range(GRP):
                for c in range(5):
                    n = 5 * g + c
                    cols = slice(c * 512, min((c + 1) * 512, NKEY))
                    if n >= 2:
                        eng.wait_ge(sm_ev, n - 1)
                    pe.matmul(bank[2 + n % 2][:, 0:cols.stop - cols.start], ind[:, g, :], scs[:, cols], start=True, stop=True).then_inc(sm_mm, 1)
            eng.wait_ge(sm_ev, 10)
            for g in range(GRP):
                eng.wait_ge(se_rd, g + 1)
                for q in range(5):
                    n = 5 * g + q
                    if n >= 2:
                        eng.wait_ge(st_ev, n - 1)
                    if q < 4:
                        for r in range(4 * q, 4 * q + 4):
                            ins = pe.transpose(bank[2 + n % 2][:, (r % 4) * P:(r % 4 + 1) * P], S[:, g, r * P:(r + 1) * P], ident[:, :])
                    else:
                        ins = pe.transpose(bank[2 + n % 2][0:NS, 0:P], S[:, g, PAST:NKEY], ident[:, :])
                    ins.then_inc(st_tr, 1)
            def value_products(s):
                g, r = s // NPG, s % NPG
                t = s + KSTEPS
                slot = (t + 2) % 3
                eng.wait_ge(kv_in[slot], 64 * (t // 3 + 1))
                for b4 in range(4):
                    ins = pe.matmul(bank[2 + g][32 * b4:32 * b4 + 32, :], pT[:, g, r, 32 * b4:32 * b4 + 32], kv[:, slot, b4, :],
                                    start=(r == 0), stop=False)
                if r == NPG - 1:
                    for b4 in range(4):
                        ins = pe.matmul(bank[2 + g][32 * b4:32 * b4 + 32, :], pT[0:NS, g, 16, 32 * b4:32 * b4 + 32], v[0:NS, 4, :],
                                        start=False, stop=True)
                ins.then_inc(v_mm, 1)

            eng.wait_ge(st_ev, 10)
            step = 0
            for c in range(CT):
                eng.wait_ge(xc_rd, c + 1)
                for u in range(4):
                    n = 4 * c + u
                    if n >= 2:
                        eng.wait_ge(lg_ev, n - 1)
                    hf = u % 2
                    pe.matmul(bank[6 + n % 2][:, 0:HALF], wgate[:, u // 2, c, :], xc[:, hf * HALF:(hf + 1) * HALF],
                              start=True, stop=True).then_inc(lg_mm, 1)
                for _ in range(LRU_STEPS):
                    value_products(step)
                    step += 1

            def att_scores(u):
                n, h = u // NH, u % NH
                if u >= 2:
                    eng.wait_ge(pa_m, u - 1)
                else:
                    eng.wait_ge(kn_ev, GRP)
                pe.matmul(bank[4 + u % 2][:, 0:P * (n + 1)], qz[:, h, n * P:(n + 1) * P], kT[:, h // 2, 0:P * (n + 1)],
                          start=True, stop=True).then_inc(pa_s, 1)

            def att_transposes(u):
                n = u // NH
                eng.wait_ge(pa_n, u + 1)
                if u >= 2:
                    eng.wait_ge(pa_te, u - 1)
                else:
                    eng.wait_ge(lg_ev, 16)
                for j in range(n + 1):
                    ins = pe.matmul(bank[6 + u % 2][:, j * P:(j + 1) * P], probs[u % 4][:, j * P:(j + 1) * P], diag[:, u % 4, :],
                                    start=True, stop=True)
                ins.then_inc(pa_t, 1)

            def att_values(u):
                n, h = u // NH, u % NH
                w_ = u // 2
                eng.wait_ge(pa_te, u + 1)
                if w_ >= 2:
                    eng.wait_ge(pa_oe, w_ - 1)
                else:
                    eng.wait_ge(gemm_ev, E_WO)
                p0 = HD * (h % 2)
                for j in range(n + 1):
                    ins = pe.matmul(bank[w_ % 2][p0:p0 + HD, 0:P], v[:, j, h * HD:(h + 1) * HD], probsT[u % 4][:, j * P:(j + 1) * P],
                                    start=(j == 0), stop=(j == n))
                if h % 2:
                    ins.then_inc(pa_o, 1)

            for u in range(ATT_UNITS + 3):
                if u < ATT_UNITS:
                    att_scores(u)
                if 2 <= u < ATT_UNITS + 2:
                    att_transposes(u - 2)
                if u >= 3:
                    att_values(u - 3)
                while step < KSTEPS and step - CT * LRU_STEPS < (u + 1) * (KSTEPS - CT * LRU_STEPS) // ATT_UNITS:
                    value_products(step)
                    step += 1

            for g in range(GRP):
                eng.wait_ge(so_rd, g + 1)
                if g == 0:
                    eng.wait_ge(pa_te, ATT_UNITS)
                for m in range(CT):
                    ins = pe.transpose(bank[6 + g][:, m * P:(m + 1) * P], so[:, g, m * P:(m + 1) * P], ident[:, :])
                ins.then_inc(so_tr, 1)

            eng.wait_ge(so_ev, GRP)
            eng.wait_ge(pa_oe, ATT_UNITS // 2)
            eng.wait_ge(pk_rd, CT)
            eng.wait_ge(st_ev, 10)
            for n in (6, 7):
                w = weights(n)
                for m in range(CT):
                    tile_product(E_WO + 8 * (n - 6) + 2 * m, w, m, mixT)
            ssq(sqT, lambda k: eng.wait_ge(gemm_ev, E_WO + 2 * k + 2))
            eng.wait_ge(rms_rd, 2)
            ssq(sqT, lambda k: eng.wait_ge(sq_rd, KT + k + 1))
            def three_passes(out, w, rhs_hi, rhs_lo, first, last):
                passes = ((w_hi, rhs_hi), (w_hi, rhs_lo), (w_lo, rhs_hi))
                for k in range(KT):
                    for i, (lhs, rhs) in enumerate(passes):
                        ins = pe.matmul(out, lhs[:, w, k * P:(k + 1) * P], rhs(k), start=(first and k == 0 and i == 0),
                                        stop=(last and k == KT - 1 and i == 2))
                return ins

            def hidden_tile(j, n, parity, wait=True):
                eng.wait_ge(w_lo_rd, n + 1)
                for hf in range(2):
                    if wait:
                        eng.wait_ge(h_ev, j * 2 + (hf - 3))
                    c = slice(hf * HALF, (hf + 1) * HALF)
                    three_passes(bank[2 * parity + hf][:, 0:HALF], parity, lambda k: hn_hi[:, k, c], lambda k: hn_lo[:, k, c],
                                 True, True).then_inc(h_mm, 1)

            def output_tile(m, n, half, parity, wait=True):
                for piece in range(2):
                    eng.wait_ge(w_lo_rd, n + (piece + 1))
                    for hf in range(2):
                        if wait and piece == 0:
                            eng.wait_ge((f_ev, f_add)[half], m * 2 + (hf - 3))

                        def part(h):
                            return lambda k: h[:, (piece * KT + k) * NT + hf * HALF:(piece * KT + k) * NT + (hf + 1) * HALF]

                        ins = three_passes(bank[2 * parity + hf][:, 0:HALF], piece, part(h_hi), part(h_lo), piece == 0, piece == 1)
                        if piece == 1:
                            ins.then_inc(f_mm, 1)
                    if piece == 0:
                        ins.then_inc(half_mm, 1)

            eng.wait_ge(hn_lo_rd, KT)
            eng.wait_ge(gemm_ev, E_MIX)
            for half in range(2):
                j0, n0 = half * HT, half * PIECES // 2
                if half == 1:
                    eng.wait_ge(f_ev, 2 * KT)
                for s in range(2):
                    hidden_tile(j0 + s, n0 + s, s, False)
                with eng.Fori(0, HT // 2 - 1) as i:
                    for s in range(2):
                        hidden_tile(i * 2 + (j0 + 2 + s), i * 2 + (n0 + 2 + s), s)
                eng.wait_ge(h_lo_rd, j0 + HT)
                for s in range(2):
                    output_tile(s, n0 + HT + 2 * s, half, s, False)
                with eng.Fori(0, KT // 2 - 1) as i:
                    for s in range(2):
                        output_tile(i * 2 + (2 + s), i * 4 + (n0 + HT + 4 + 2 * s), half, s)
            eng.wait_ge(rms_rd, 3)
            ssq(sqT, lambda k: eng.wait_ge(f_sq, 2 * k + 2))


def kernel(x_prompt, x_sample, cache_k, cache_v, cache_kidx, state_h, state_conv, page_table, g_pre_mix, w_in, conv_w,
           conv_b, w_a, b_a, w_i, b_i, lam, w_out, g_post_mix, g_pre_ffn, w_ff1, w_ff2, g_post_ffn):
    import numpy as np
    import concourse.bacc as bacc
    from concourse.bass_utils import run_bass_kernel_spmd as run

    f4 = np.float32
    a = {k: np.asarray(x) for k, x in dict(
        x_prompt=x_prompt, x_sample=x_sample, ck=cache_k, cv=cache_v, ci=cache_kidx, sh=state_h, sc=state_conv,
        w_in=w_in, w_out=w_out, w1=w_ff1, w2=w_ff2, conv_w=conv_w, w_a=w_a, w_i=w_i).items()}

    tokens = np.concatenate([a["x_prompt"].reshape(SEQ, D_MODEL), a["x_sample"].reshape(NS, D_MODEL)])
    xT = tokens.T.reshape(KT, P, NT).transpose(1, 0, 2).reshape(P, KT * NT)

    def by_channel(x, *rest):
        return np.asarray(x).reshape(-1, P).T

    par = np.concatenate(
        [by_channel(g) for g in (g_pre_mix, g_post_mix, g_pre_ffn, g_post_ffn, conv_w, conv_b, b_a, b_i, lam)]
        + [a["sh"].reshape(DEC_BATCH, CT, P).transpose(2, 1, 0).reshape(P, -1),
           a["sc"].reshape(DEC_BATCH, 3, CT, P).transpose(3, 2, 0, 1).reshape(P, -1)], axis=1)

    def blocks(w, cols):
        k, n = w.shape
        return w.reshape(k // P, P, n // cols, cols).transpose(2, 1, 0, 3).reshape(n // cols, P, -1)

    wi = a["w_in"][0]
    part = {n: wi[:, 512 * i:512 * (i + 1)] for i, n in enumerate(["xl", "gate", "q", "k", "v", "qi"])}
    w_in_blocks = np.concatenate([blocks(part[n], 512) for n in ("qi", "q", "k", "xl", "gate", "v")])
    w1 = blocks(a["w1"][0], P).reshape(2, HT, P, PIECE)
    w2 = a["w2"][0].reshape(2, 2, KT, P, KT, P).transpose(0, 4, 1, 3, 2, 5).reshape(2, 2 * KT, P, PIECE)
    w_mlp = np.concatenate([w1, w2], axis=1).reshape(PIECES, P, PIECE)
    w_kw = wi[:, 3072:3144].reshape(KT, P, 72).transpose(1, 0, 2)
    wgate = np.zeros((P, 2, CT, P), f4)
    for n, w in enumerate((a["w_a"][0], a["w_i"][0])):
        for j in range(8):
            o = HD * (j % 2)
            wgate[o:o + HD, n, j // 2, o:o + HD] = w[j]
    ck = a["ck"][0].reshape(NPOOL, PAGE, CT, P).transpose(0, 3, 2, 1).reshape(NPOOL, P, CT * PAGE)

    half = HD // 2
    freq = f4(10000.0) ** (-np.arange(half, dtype=f4) / f4(half))
    pos = np.concatenate([np.arange(SEQ), np.tile(PAST + np.arange(DEC_SEQ), DEC_BATCH)]).astype(f4)
    ang = (pos[None, :] * freq[:, None]).astype(f4)
    cos, sin = np.cos(ang), np.sin(ang)
    rope = np.concatenate([np.tile(cos, (4, 1)), np.tile(np.concatenate([-sin, sin]), (2, 1))], axis=1).astype(f4)
    q = np.arange(P)
    causal = np.where(q[None, :] > q[:, None], OUT_OF_REACH, 0.0).astype(f4)
    qb, qt = np.arange(NS) // DEC_SEQ, np.arange(NS) % DEC_SEQ
    rb, rt = np.arange(P) // 32, np.arange(P) % DEC_SEQ
    ind = np.stack([(qb[:, None] == rb[None, :] + 4 * g) & (qt[:, None] == rt[None, :]) for g in range(GRP)], axis=1).astype(f4)
    newmask = np.where((qb[:, None] == qb[None, :]) & (qt[None, :] <= qt[:, None]), 0.0, OUT_OF_REACH).astype(f4)
    keyoff = (q[:, None] % 8).astype(f4)

    steps = np.asarray(page_table).reshape(GRP, 4, NPG).transpose(0, 2, 1).reshape(1, KSTEPS * 4)

    arrays = {
        "xT": xT, "par": par, "w_in": w_in_blocks, "w_kw": w_kw, "w_out": blocks(a["w_out"][0], 512),
        "w_mlp": w_mlp, "wgate": wgate,
        "ck": ck, "cv": a["cv"][0].reshape(NPOOL, PAGE, WIDTH), "ci": a["ci"][0], "steps": steps, "ptT": np.asarray(page_table).T,
        "ident": np.eye(P, dtype=f4), "rope": rope, "causal": causal, "ind": ind, "newmask": newmask, "keyoff": keyoff,
    }
    arrays = {f"in_{k}": np.ascontiguousarray(x) for k, x in arrays.items()}
    nc = bacc.Bacc("TRN2", target_bir_lowering=False, num_devices=1)
    args = [nc.dram_tensor(k, x.shape, mybir.dt.from_np(x.dtype), kind="ExternalInput").ap() for k, x in arrays.items()]
    outs = [(P, KT, NT), (P, CT, NT), (NT, WIDTH), (HD, NT), (P, CT, 36)]
    for i, shape in enumerate(outs):
        args.append(nc.dram_tensor(f"out_{i}", shape, F32, kind="ExternalOutput").ap())
    build(nc, *args)
    r = run(nc, [arrays], core_ids=[0]).results[0]
    yT, kT, v, kiT, lru = (r[f"out_{i}"] for i in range(len(outs)))

    y = yT.transpose(2, 1, 0).reshape(NT, D_MODEL)
    k = kT.transpose(2, 1, 0).reshape(NT, WIDTH)
    ki = kiT.T
    st = lru.transpose(2, 1, 0).reshape(36, WIDTH)
    return (y[:SEQ].reshape(1, SEQ, D_MODEL), y[SEQ:].reshape(DEC_BATCH, DEC_SEQ, D_MODEL),
            k[:SEQ].reshape(1, 1, SEQ, NH, HD), v[:SEQ].reshape(1, 1, SEQ, NH, HD), ki[:SEQ].reshape(1, 1, SEQ, HD),
            st[27].reshape(1, 1, WIDTH), st[0:3].reshape(1, 1, 3, WIDTH),
            k[SEQ:].reshape(1, DEC_BATCH, DEC_SEQ, NH, HD), v[SEQ:].reshape(1, DEC_BATCH, DEC_SEQ, NH, HD),
            ki[SEQ:].reshape(1, DEC_BATCH, DEC_SEQ, HD),
            st[28:36].reshape(1, DEC_BATCH, WIDTH), st[3:27].reshape(1, DEC_BATCH, 3, WIDTH))
```

```python
from contextlib import ExitStack

import concourse.bass as bass
from concourse import mybir

P = 128
F32 = mybir.dt.float32
F32R = mybir.dt.float32r
I32 = mybir.dt.int32
ALU = mybir.AluOpType
ACT = mybir.ActivationFunctionType
AX_X = mybir.AxisListType.X

D_MODEL = 1024
SEQ = 512
DEC_BATCH = 8
DEC_SEQ = 4
NS = DEC_BATCH * DEC_SEQ
NT = SEQ + NS
HALF = NT // 2
PAST = 2048
PAGE = 128
NPG = PAST // PAGE
NPOOL = DEC_BATCH * NPG * 5 // 4
WIDTH = 512
CT = WIDTH // P
NH = 8
HD = 64
KT = D_MODEL // P
D_FF = 4 * D_MODEL
FT = D_FF // P
QB = SEQ // P
TOPK_P = min(256, SEQ // 4)
TOPK_S = min(256, (PAST + DEC_SEQ) // 4)
NKEY = PAST + NS
GRP = DEC_BATCH // 4
EPS = 1e-6
POOL_TILES = (2, 5)
POOL_RESTS = (1, 4)
NORMS = (("in", (4, 5)), ("mix0", (4, None)), ("x0", (5, None)), ("mix1", (None, 6)), ("x1", (None, 7)), ("mlp", (4, 5)))
NORM = {name: i for i, (name, _) in enumerate(NORMS)}
RG_C = 8.0
BLOCK_SLOT = (0, 1, 0, 1, 0, 1, 1, 0)
OUT_OF_REACH = -2.0 ** 100
TAKEN = -3e38
XW = 3 + SEQ + DEC_BATCH * (3 + DEC_SEQ)
SCALE = HD ** -0.5
IDX_SCALE = (HD ** -0.5) * (NH ** -0.5)

G_PRE_MIX, G_POST_MIX, G_PRE_FFN, G_POST_FFN = 0, 8, 16, 24
CONV_W0, CONV_B, B_A, B_I, LAM, H0, CONV0 = 32, 48, 52, 56, 60, 64, 96
NPAR = 192

E_QI, E_KW, E_Q, E_K, E_XL, E_GATE, E_V, E_WO, E_MIX = 0, 8, 10, 18, 26, 34, 42, 47, 63
HT = FT // 2
PIECE = KT * P
PIECES = 2 * (HT + 2 * KT)
SCP_AT = {1: 0, 2: 256, 3: 640}
KSTEPS = GRP * NPG
ATT_UNITS = QB * NH
V_SLOTS = 5
SCAN_ROUNDS = (15, 21, 28)


def build(nc, xT_d, par_d, w_in_d, w_kw_d, w_out_d, w_mlp_d, wgate_d, ck_d, cv_d, ci_d, steps_d, ptT_d,
          ident_d, rope_d, causal_d, ind_d, newmask_d, keyoff_d, yT_d, kT_d, v_d, kiT_d, lru_d):
    with ExitStack() as ctx:
        def sb(name, shape, dt=F32):
            return ctx.enter_context(nc.sbuf_tensor(name, shape, dt))

        def sem(name):
            return ctx.enter_context(nc.semaphore(name))

        bank = [ctx.enter_context(nc.psum_tensor(f"bank{i}", [P, 512], F32)) for i in range(8)]

        start = {}

        def region(name, shape):
            start[name] = nc.sbuf_base
            return sb(name, shape)

        def over(name, shape, place, offset, dt=F32R):
            return nc.alloc_sbuf_tensor_at(name, shape, dt, offset=start[place] + 4 * offset)

        regX = region("regX", [P, KT * NT])
        regR = region("regR", [P, KT * NT])
        regM = region("regM", [P, KT * NT])
        regQ = region("regQ", [P, KT * NT])
        wring = region("wring", [P, 2, 4096])
        arena = region("arena", [P, 17872])
        scp = region("scp", [P, 1152])
        qbd = region("qbd", [P, DEC_BATCH, CT, 32])
        hn_hi = over("hn_hi", [P, KT, NT], "regR", 0)
        hn_lo = over("hn_lo", [P, KT, NT], "regQ", 0)
        h_hi = over("h_hi", [P, HT * NT], "arena", 0)
        h_lo = over("h_lo", [P, HT * NT], "arena", HT * NT)
        w_raw = wring[:, 1, 0:2 * PIECE].rearrange("p (s c) -> p s c", s=2)
        w_hi = [over("w_hi_even", [P, PIECE], "wring", 4096 + 2 * PIECE), over("w_hi_odd", [P, PIECE], "scp", 0)]
        w_lo = [over("w_lo_even", [P, PIECE], "wring", 4096 + 3 * PIECE), over("w_lo_odd", [P, PIECE], "qbd", 0)]
        smask = over("smask", [NS, NKEY], "arena", 3 * 2048)
        lx = sb("lx", [P, 6 * NT])
        kwrow = sb("kwrow", [P, 5, 72])
        wgate = sb("wgate", [P, 2, CT, P])
        ident = sb("ident", [P, P])
        averager = sb("averager", [P, P])
        causal = sb("causal", [P, P])
        ind = sb("ind", [NS, GRP, P])
        ind_r = sb("ind_r", [NS, GRP, P], F32R)
        wT = sb("wT", [NS, GRP, P])
        wm = sb("wm", [P, GRP, NS])
        newmask = sb("newmask", [NS, NS])
        par = sb("par", [P, NPAR])
        keyoff = sb("keyoff", [P, 1])
        pt_own = sb("pt_own", [P, DEC_BATCH], I32)
        row_i = sb("row_i", [P, DEC_BATCH], I32)
        kw_diag = sb("kw_diag", [P, KT * 72])
        wkw = kw_diag[:, :].rearrange("p (k c) -> p k c", k=KT)
        diag = kw_diag[:, 0:4 * P].rearrange("p (s c) -> p s c", s=4)
        qi_s = sb("qi_s", [P, CT, NS])
        q_s = sb("q_s", [P, CT, NS])
        m8 = sb("m8", [P, 3, 8])
        pack = sb("pack", [P, CT, 36])
        sp = sb("sp", [P, 8 * CT])
        eps = sb("eps", [P, 1])
        steps = sb("steps", [1, KSTEPS * 4], I32)
        stat = sb("stat", [P, 4, 4])
        sstat = sb("sstat", [P, GRP, 8])

        def tiles(region, n=KT):
            return region[:, 0:n * NT].rearrange("p (k t) -> p k t", t=NT)

        xT = tiles(regX)
        hnT = tiles(regR)
        mixT = tiles(regM)
        sqT = tiles(regQ)
        oT = tiles(regR)
        fT = tiles(regM)
        qz = regQ[:, 0:NH * SEQ].rearrange("p (h t) -> p h t", t=SEQ)
        kidxT = regX[:, 0:4096].rearrange("p (b c) -> p b c", b=4)
        S = regX[:, 0:GRP * NKEY].rearrange("p (g c) -> p g c", g=GRP)
        R = regM[:, 0:GRP * NKEY].rearrange("p (g c) -> p g c", g=GRP)
        work_s = regM[0:NS, 4 * NT:4 * NT + NKEY]
        pT = regR[:, 0:GRP * 17 * P].rearrange("p (g r c) -> p g r c", g=GRP, r=17)
        at = 0

        def carve(n):
            nonlocal at
            at += n
            return arena[:, at - n:at]

        kv = carve(3 * 2048).rearrange("p (s b c) -> p s b c", s=3, b=4)
        v_slot = [kv[:, 1], kv[:, 2], kv[:, 0]] + [wring[:, 0, i * 2048:(i + 1) * 2048].rearrange("p (b c) -> p b c", b=4) for i in range(2)]
        kidx_in_sb = arena[:, 0:4096].rearrange("p (b c) -> p b c", b=4)
        scs = carve(NKEY)[0:NS, :]
        kT = carve(CT * NT).rearrange("p (k t) -> p k t", t=NT)
        work_p = arena[:, at:at + 1152]
        v = carve(5 * 512).rearrange("p (j c) -> p j c", j=5)
        xl = carve(CT * XW).rearrange("p (k t) -> p k t", t=XW)
        kiT = carve(NT)
        pTp_at = carve(1056)
        pTp = pTp_at[:, 0:1024].rearrange("p (s c) -> p s c", s=2)
        qis = pTp_at[:, 0:512].rearrange("p (b e c) -> p b e c", b=DEC_BATCH, e=2)
        kw = pTp_at[:, 512:1056]
        sm = carve(1024).rearrange("p (s c) -> p s c", s=2)
        probs = [sm[:, 0, :], sm[:, 1, :], lx[:, 0:512], lx[:, 512:1024]]
        probsT = [pTp[:, 0, :], pTp[:, 1, :], lx[:, 1024:1536], lx[:, 1536:2048]]
        so = lx[:, 2048:3072].rearrange("p (g c) -> p g c", g=GRP)
        raw = lx[:, 0:2 * NT].rearrange("p (s t) -> p s t", s=2)
        swp = lx[:, 2 * NT:4 * NT].rearrange("p (s t) -> p s t", s=2)
        cosT = lx[:, 4 * NT:5 * NT]
        sinT = lx[:, 5 * NT:6 * NT]
        xc, gi, ga, dd, aa = (lx[:, i * NT:(i + 1) * NT] for i in range(5))
        rstd = lx[:, 0:NT]
        normed = lx[:, NT:5 * NT].rearrange("p (s t) -> p s t", s=4)
        relu_t = lx[:, NT:3 * NT].rearrange("p (s t) -> p s t", s=2)
        square_t = lx[:, 3 * NT:5 * NT].rearrange("p (s t) -> p s t", s=2)

        half_cols = [slice(hf * HALF, (hf + 1) * HALF) for hf in range(2)]

        def roots_before(name):
            return sum(b is not None for n, banks in NORMS[:NORM[name]] for b in banks)

        wslot = [wring[:, s, :].rearrange("p (k c) -> p k c", k=KT) for s in range(2)]

        const_in = sem("const_in")
        steps_in = sem("steps_in")
        x_in = [sem(f"x_in{i}") for i in range(4)]
        par_in = sem("par_in")
        kw_in = sem("kw_in")
        w_in = [sem("w_in_even"), sem("w_in_odd")]
        kidx_in = sem("kidx_in")
        q_placed = sem("q_placed")
        kv_in = [sem(f"kv_in{i}") for i in range(3)]
        v_in = [sem(f"v_in{i}") for i in range(V_SLOTS)]
        x_again = sem("x_again")
        stored = sem("stored")
        state_stored = sem("state_stored")
        gemm_mm = sem("gemm_mm")
        gemm_ev = sem("gemm_ev")
        sq_even = sem("sq_even")
        sq_pair = sem("sq_pair")
        sq_rd = sem("sq_rd")
        ssq_mm = sem("ssq_mm")
        first_rstd = sem("first_rstd")
        rstd_rd = sem("rstd_rd")
        hn_rd = sem("hn_rd")
        x1_rd = sem("x1_rd")
        x1_pool = sem("x1_pool")
        y_rd = sem("y_rd")
        y_pool = sem("y_pool")
        rows_rd = sem("rows_rd")
        averager_rd = sem("averager_rd")
        rms_rd = sem("rms_rd")
        zero_rd = sem("zero_rd")
        lam_rd = sem("lam_rd")
        explam_rd = sem("explam_rd")
        rope_out = sem("rope_out")
        ki_dup = sem("ki_dup")
        wi_tr = sem("wi_tr")
        wi_rd = sem("wi_rd")
        wT_rd = sem("wT_rd")
        wT_tr = sem("wT_tr")
        wm_rd = sem("wm_rd")
        pi_mm = sem("pi_mm")
        pi_ev = sem("pi_ev")
        pi_acc = sem("pi_acc")
        qis_rd = sem("qis_rd")
        kx_tr = sem("kx_tr")
        kx_ev = sem("kx_ev")
        kd_mm = sem("kd_mm")
        kd_ev = sem("kd_ev")
        ks_mm = sem("ks_mm")
        ks_ev = sem("ks_ev")
        pmask_rd = sem("pmask_rd")
        smask_rd = sem("smask_rd")
        tk_p = sem("tk_p")
        tk_s = sem("tk_s")
        qbd_rd = sem("qbd_rd")
        k_mm = sem("k_mm")
        k_ev = sem("k_ev")
        kn_mm = sem("kn_mm")
        kn_ev = sem("kn_ev")
        sp_rd = sem("sp_rd")
        taps_rd = sem("taps_rd")
        xc_rd = sem("xc_rd")
        u_rd = sem("u_rd")
        scan_rd = sem("scan_rd")
        lg_mm = sem("lg_mm")
        lg_ev = sem("lg_ev")
        tanh_rd = sem("tanh_rd")
        dd_rd = sem("dd_rd")
        root_rd = sem("root_rd")
        pk_rd = sem("pk_rd")
        pa_s = sem("pa_s")
        pa_m = sem("pa_m")
        pa_e = sem("pa_e")
        pa_n = sem("pa_n")
        pa_r = sem("pa_r")
        pa_t = sem("pa_t")
        pa_te = sem("pa_te")
        pa_o = sem("pa_o")
        pa_oe = sem("pa_oe")
        sm_mm = sem("sm_mm")
        sm_ev = sem("sm_ev")
        smax_rd = sem("smax_rd")
        se_rd = sem("se_rd")
        st_tr = sem("st_tr")
        st_ev = sem("st_ev")
        v_mm = sem("v_mm")
        so_rd = sem("so_rd")
        so_tr = sem("so_tr")
        so_ev = sem("so_ev")
        hn_f = sem("hn_f")
        hn_hi_rd = sem("hn_hi_rd")
        hn_lo_rd = sem("hn_lo_rd")
        hn_lo_pool = sem("hn_lo_pool")
        piece_in = [sem("piece_in_even"), sem("piece_in_odd")]
        w_hi_rd = sem("w_hi_rd")
        w_lo_rd = sem("w_lo_rd")
        h_mm = sem("h_mm")
        h_ev = sem("h_ev")
        h_sq = sem("h_sq")
        h_hi_rd = sem("h_hi_rd")
        h_lo_rd = sem("h_lo_rd")
        half_mm = sem("half_mm")
        f_mm = sem("f_mm")
        f_ev = sem("f_ev")
        f_add = sem("f_add")
        f_sq = sem("f_sq")
        sum_rd = sem("sum_rd")
        sq_sum = sem("sq_sum")
        dve_step = sem("dve_step")
        act_step = sem("act_step")
        pool_step = sem("pool_step")

        block = ctx.enter_context(nc.Block())

        N_CONST = 8
        w_src = [w_in_d[i] for i in range(6)] + [w_out_d[i] for i in range(2)]

        @block.sync
        def _(eng):
            for i in range(4):
                c = slice(i * 2 * NT, (i + 1) * 2 * NT)
                eng.dma_start(regX[:, c], xT_d[:, c]).then_inc(x_in[i], 16)
            eng.dma_start(wring[:, 0, :], w_src[0]).then_inc(w_in[0], 16)
            eng.dma_start(steps[:, :], steps_d).then_inc(steps_in, 16)
            eng.dma_start(pt_own[:, :], bass.AP(tensor=ptT_d.tensor, offset=0, ap=[[DEC_BATCH, NPG], [0, 8], [1, DEC_BATCH]])).then_inc(const_in, 16)
            eng.dma_start(keyoff[:, :], keyoff_d).then_inc(const_in, 16)
            eng.dma_start(wkw, w_kw_d).then_inc(kw_in, 16)
            eng.dma_start(lx[:, 4 * NT:6 * NT], rope_d).then_inc(const_in, 16)
            eng.dma_start(ident[:, :], ident_d).then_inc(const_in, 16)
            eng.dma_start(causal[:, :], causal_d).then_inc(const_in, 16)
            eng.dma_start(ind[:, :, :], ind_d).then_inc(const_in, 16)
            eng.dma_start(newmask[:, :], newmask_d).then_inc(const_in, 16)
            eng.dma_start(wgate[:, :, :, :], wgate_d).then_inc(const_in, 16)
            eng.dma_start(wring[:, 1, :], w_src[1]).then_inc(w_in[1], 16)

            page_regs = [eng.alloc_register(f"page{b4}") for b4 in range(4)]

            def stream(s, slot, landed, table, freed, uses):
                eng.load(page_regs, steps[0:1, bass.ds(s * 4, 4)])
                page = [eng.snap(r, min_val=0, max_val=NPOOL - 1) for r in page_regs]
                if freed is not None:
                    eng.wait_ge(freed, uses)
                for b4 in range(4):
                    eng.dma_start(slot[:, b4, :], table[bass.ds(page[b4], 1), :, :].rearrange("a p c -> p (a c)")).then_inc(landed, 16)

            def keys(s, slot, freed, uses):
                stream(s, kv[:, slot], kv_in[slot], ck_d, freed, uses)

            def values(s, slot, freed, uses):
                stream(s, v_slot[slot], v_in[slot], cv_d, freed, uses)

            eng.wait_ge(steps_in, 16)
            keys(0, 2, None, 0)
            keys(1, 0, kx_tr, 16)
            keys(2, 1, kx_tr, 16)
            with eng.Fori(0, 9) as i:
                for j in range(3):
                    keys(i * 3 + (3 + j), (j + 2) % 3, k_mm, i * 3 + (j + 1))
            for s in range(3, V_SLOTS):
                values(s, s, gemm_mm, E_V)
            for s in (30, 31):
                keys(s, (s + 2) % 3, k_mm, s - 2)
            for s in range(3):
                values(s, s, k_mm, KSTEPS - 2 + s)
            with eng.Fori(0, 5) as i:
                for j in range(V_SLOTS):
                    values(i * V_SLOTS + (V_SLOTS + j), j, v_mm, i * V_SLOTS + (j + 1))
            for s in (30, 31):
                values(s, s % V_SLOTS, v_mm, s - V_SLOTS + 1)
            eng.wait_ge(v_mm, KSTEPS - 2)
            eng.dma_start(wring[:, 0, :], w_src[7]).then_inc(w_in[0], 16)
            eng.wait_ge(gemm_mm, E_WO + 12)
            for s in range(2):
                eng.dma_start(w_raw[:, s, :], w_mlp_d[s]).then_inc(piece_in[s], 16)
            with eng.Fori(0, PIECES // 2 - 1) as i:
                for s in range(2):
                    eng.wait_ge(w_lo_rd, i * 2 + (s + 1))
                    eng.dma_start(w_raw[:, s, :], w_mlp_d[bass.ds(i * 2 + (2 + s), 1), :, :].rearrange("a p c -> p (a c)")).then_inc(piece_in[s], 16)
            for k in range(KT):
                if k in POOL_TILES:
                    eng.wait_ge(y_pool, POOL_TILES.index(k) + 1)
                else:
                    eng.wait_ge(y_rd, k + 1 - sum(p < k for p in POOL_TILES))
                eng.dma_start(yT_d[:, k, :], xT[:, k, :]).then_inc(stored, 16)
            eng.wait_ge(state_stored, 16 * 5)
            eng.wait_ge(stored, 16 * KT)

        ci_rows = ci_d.rearrange("n (s r) d -> (n s) (r d)", r=16)

        @block.gpsimd
        def _(eng):
            steps = [0]

            def link(ins):
                steps[0] += 1
                ins.then_inc(pool_step, 1)
                eng.wait_ge(pool_step, steps[0])

            def gather(dst, rows, index, landed):
                eng.indirect_dma_start(dst, None, rows, bass.IndirectOffsetOnAxis(ap=index, axis=0)).then_inc(landed, 16)

            nc.gpsimd.memset(regQ[:, :], 0.0)
            nc.gpsimd.memset(pTp_at[:, 0:512], 0.0)
            nc.gpsimd.memset(qbd[:, :, :, :], 0.0)
            nc.gpsimd.memset(xl[:, :, 0:3], 0.0).then_inc(zero_rd, 1)
            eng.wait_ge(rows_rd, 1)
            for b in range(4):
                gather(kidx_in_sb[:, b, :], ci_rows, row_i[:, b:b + 1], kidx_in)

            def rope(t, out, parts=P):
                r, w = raw[0:parts, t % 2, :], swp[0:parts, t % 2, :]
                eng.wait_ge(gemm_ev, 2 * t + 2)
                nc.gpsimd.tensor_tensor(r, r, cosT[0:parts, :], ALU.mult)
                link(nc.gpsimd.tensor_tensor(w, w, sinT[0:parts, :], ALU.mult))
                nc.gpsimd.tensor_tensor(out, r, w, ALU.add).then_inc(rope_out, 1)

            eng.wait_ge(const_in, 16 * N_CONST)
            for t in range(CT):
                rope(t, raw[:, t % 2, :])
            rope(4, kiT[0:HD, :], HD)
            eng.wait_ge(kx_tr, 8)
            for b in range(4):
                gather(kidx_in_sb[:, b, :], ci_rows, row_i[:, 4 + b:5 + b], kidx_in)
            for t in range(5, 9):
                rope(t, raw[:, t % 2, :])
            for m in range(CT):
                rope(9 + m, kT[:, m, :])
            eng.wait_ge(rope_out, 13)
            eng.dma_start(kT_d, kT).then_inc(state_stored, 16)
            eng.dma_start(kiT_d, kiT[0:HD, :]).then_inc(state_stored, 16)
            for c in range(CT):
                eng.wait_ge(taps_rd, c + 1)
                link(nc.gpsimd.tensor_tensor(xc, xc, gi, ALU.add))
                link(nc.gpsimd.tensor_tensor(xc, xc, ga, ALU.add))
                nc.gpsimd.tensor_tensor(xc, xc, dd, ALU.add).then_inc(xc_rd, 1)
                nc.gpsimd.tensor_copy(pack[:, c, 0:3], xl[:, c, SEQ:SEQ + 3])
                nc.gpsimd.tensor_copy(pack[:, c, 3:27].rearrange("p (b t) -> p b t", t=3),
                                      xl[:, c, 3 + SEQ:XW].rearrange("p (b w) -> p b w", w=3 + DEC_SEQ)[:, :, DEC_SEQ:DEC_SEQ + 3])
                eng.wait_ge(lg_ev, 4 * c + 4)
                eng.wait_ge(xc_rd, c + 1)
                nc.gpsimd.tensor_tensor(gi, gi, xc, ALU.mult)
                eng.wait_ge(tanh_rd, c + 1)
                link(nc.gpsimd.tensor_scalar(dd, dd, 1.0, None, ALU.add))
                nc.gpsimd.tensor_tensor(dd, dd, ga, ALU.mult).then_inc(dd_rd, 1)
                eng.wait_ge(dd_rd, c + 1)
                a0 = aa[:, SEQ:NT].rearrange("p (b t) -> p b t", t=DEC_SEQ)[:, :, 0]
                u0 = gi[:, SEQ:NT].rearrange("p (b t) -> p b t", t=DEC_SEQ)[:, :, 0]
                link(nc.gpsimd.tensor_tensor(ga[:, 0:DEC_BATCH], a0, par[:, H0 + 8 * c:H0 + 8 * c + 8], ALU.mult))
                link(nc.gpsimd.memset(a0, 0.0))
                eng.wait_ge(root_rd, c + 1)
                link(nc.gpsimd.tensor_tensor(gi, gi, dd, ALU.mult))
                nc.gpsimd.tensor_tensor(u0, u0, ga[:, 0:DEC_BATCH], ALU.add).then_inc(u_rd, 1)
            eng.wait_ge(gemm_ev, E_WO)
            eng.dma_start(v_d[0:SEQ, :].rearrange("(j p) c -> p j c", p=P), v[:, 0:4, :]).then_inc(state_stored, 16)
            eng.dma_start(v_d[SEQ:NT, :], v[0:NS, 4, :]).then_inc(state_stored, 16)
            for c in range(CT):
                eng.wait_ge(scan_rd, c + 1)
                nc.gpsimd.tensor_tensor(mixT[:, c, :], mixT[:, c, :], xl[:, c, 0:NT], ALU.mult)
                nc.gpsimd.tensor_copy(pack[:, c, 27:28], xl[:, c, SEQ - 1:SEQ])
                nc.gpsimd.tensor_copy(pack[:, c, 28:36], xl[:, c, SEQ:NT].rearrange("p (b t) -> p b t", t=DEC_SEQ)[:, :, DEC_SEQ - 1]).then_inc(pk_rd, 1)
            eng.wait_ge(pk_rd, 4)
            eng.dma_start(lru_d, pack[:, :, :]).then_inc(state_stored, 16)
            for u in range(ATT_UNITS):
                eng.wait_ge(pa_r, u + 1)
                if u >= 4:
                    eng.wait_ge(pa_t, u - 3)
                nc.gpsimd.tensor_scalar(diag[:, u % 4, :], ident[:, :], stat[:, u % 4, 3:4], None, ALU.mult).then_inc(pa_n, 1)
                if u == ATT_UNITS - 4:
                    eng.wait_ge(st_tr, 10)
                    eng.dma_start(regX[:, :], xT_d).then_inc(x_again, 16)

            def residual(k, branch, c, norm):
                eng.wait_ge(rstd_rd, NORM[norm])
                link(nc.gpsimd.tensor_tensor(branch[:, k, c], branch[:, k, c], rstd[:, c], ALU.mult))
                return nc.gpsimd.tensor_tensor(xT[:, k, c], xT[:, k, c], branch[:, k, c], ALU.add)

            eng.wait_ge(x_again, 16)
            for hf, c in enumerate(half_cols):
                for k in POOL_TILES:
                    residual(k, oT, c, f"mix{hf}").then_inc(x1_pool, 1)
                for k in POOL_RESTS:
                    eng.wait_ge(hn_hi_rd, hf * KT + k + 1)
                    nc.gpsimd.tensor_tensor(hn_lo[:, k, c], normed[:, k % 4, c], hn_hi[:, k, c].bitcast(F32), ALU.subtract).then_inc(hn_lo_pool, 1)
                if hf == 0:
                    for n in range(2):
                        eng.wait_ge(w_hi_rd, n + 1)
                        nc.gpsimd.tensor_tensor(w_lo[n][:, :], w_raw[:, n, :], w_hi[n][:, :].bitcast(F32), ALU.subtract).then_inc(w_lo_rd, 1)
            for s in range(2):
                eng.wait_ge(h_ev, s + 3)
                nc.gpsimd.tensor_tensor(square_t[:, s, :], relu_t[:, s, :], relu_t[:, s, :], ALU.mult).then_inc(h_sq, 1)
            with eng.Fori(0, (FT - 2) // 2) as i:
                for s in range(2):
                    eng.wait_ge(h_ev, i * 4 + (2 * s + 6))
                    eng.wait_ge(h_lo_rd, i * 2 + (s + 1))
                    nc.gpsimd.tensor_tensor(square_t[:, s, :], relu_t[:, s, :], relu_t[:, s, :], ALU.mult).then_inc(h_sq, 1)
            for k in POOL_TILES:
                eng.wait_ge(f_sq, 2 * k + 2)
                link(nc.gpsimd.tensor_scalar(fT[:, k, :], fT[:, k, :], par[:, G_POST_FFN + k:G_POST_FFN + k + 1], None, ALU.mult))
            for k in POOL_TILES:
                residual(k, fT, slice(0, NT), "mlp").then_inc(y_pool, 1)

        @block.scalar
        def _(eng):
            steps = [0]

            def link(ins):
                steps[0] += 1
                ins.then_inc(act_step, 1)
                eng.wait_ge(act_step, steps[0])

            def gemm_out(e):
                eng.wait_ge(gemm_mm, e + 1)
                return bank[e % 4]

            eng.dma_start(par[:, :], par_d).then_inc(par_in, 16)
            for k in range(0, KT, 2):
                eng.wait_ge(x_in[k // 2], 16)
                nc.scalar.activation(hnT[:, k, :], xT[:, k, :], ACT.Square).then_inc(sq_even, 1)

            def root_mean_square(norm):
                eng.wait_ge(ssq_mm, NORM[norm] + 1)
                eng.wait_ge(averager_rd, 1)
                for b, c in zip(NORMS[NORM[norm]][1], half_cols):
                    if b is not None:
                        nc.scalar.activation(rstd[:, c], bank[b][:, 0:HALF], ACT.Sqrt, bias=eps[:, 0:1]).then_inc(rms_rd, 1)

            root_mean_square("in")
            eng.wait_ge(lam_rd, 1)
            nc.scalar.activation(sp[:, 4 * CT:5 * CT], sp[:, 2 * CT:3 * CT], ACT.Exp).then_inc(explam_rd, 1)

            def rotary_tile(t, e, parts=P):
                if 2 <= t <= 5:
                    eng.wait_ge(q_placed, t - 1)
                elif 7 <= t <= 10:
                    eng.wait_ge(q_placed, t - 2)
                elif t in (6, 11, 12):
                    eng.wait_ge(rope_out, t - 1)
                elif t == 0:
                    eng.wait_ge(hn_rd, 2 * KT)
                for hf in range(2):
                    src = gemm_out(e + hf)
                    c = slice(hf * HALF, (hf + 1) * HALF)
                    nc.scalar.copy(raw[0:parts, t % 2, c], src[0:parts, 0:HALF])
                    for q in range(parts // 32):
                        last = nc.scalar.copy(swp[32 * q:32 * q + 32, t % 2, c], src[32 * (q ^ 1):32 * (q ^ 1) + 32, 0:HALF])
                    if parts == HD:
                        last = nc.scalar.copy(kw[HD:HD + NH, c], src[HD:HD + NH, 0:HALF])
                    last.then_inc(gemm_ev, 1)

            def load_block(n):
                slot = BLOCK_SLOT[n]
                eng.dma_start(wring[:, slot, :], w_src[n]).then_inc(w_in[slot], 16)

            def place_queries(t, m, compact):
                eng.wait_ge(rope_out, t + 1)
                nc.scalar.copy(qz[0:HD, 2 * m, :], raw[0:HD, t % 2, 0:SEQ])
                nc.scalar.copy(qz[HD:P, 2 * m + 1, :], raw[HD:P, t % 2, 0:SEQ])
                nc.scalar.copy(compact[:, m, :], raw[:, t % 2, SEQ:NT]).then_inc(q_placed, 1)

            eng.wait_ge(zero_rd, 1)
            for t in range(5):
                if t < CT:
                    rotary_tile(t, 2 * t)
                else:
                    rotary_tile(t, E_KW, HD)
                if t >= 1:
                    place_queries(t - 1, t - 1, qi_s)
            load_block(2)
            eng.wait_ge(rope_out, 5)
            nc.scalar.copy(kw[0:HD, :], kiT[0:HD, :])
            nc.scalar.copy(kiT[HD:P, :], kiT[0:HD, :]).then_inc(ki_dup, 1)
            eng.wait_ge(q_placed, CT)
            for e in range(2):
                for hh in range(2):
                    for m in range(CT):
                        dst = qis[HD * e:HD * e + HD, :, e, (2 * m + hh) * DEC_SEQ:(2 * m + hh + 1) * DEC_SEQ]
                        last = nc.scalar.copy(dst, qi_s[HD * hh:HD * hh + HD, m, :].rearrange("p (b t) -> p b t", t=DEC_SEQ))
            last.then_inc(qis_rd, 1)
            for u in range(24):
                nk = P * (u // NH + 2)
                eng.wait_ge(pi_mm, u + 1)
                if u >= 2:
                    eng.wait_ge(pi_acc, u - 1)
                nc.scalar.activation(sm[:, u % 2, 0:nk], bank[6 + u % 2][:, 0:nk], ACT.Relu, scale=IDX_SCALE).then_inc(pi_ev, 1)
            for g in range(GRP):
                for u in range(8):
                    eng.wait_ge(kx_tr, 8 * g + u + 1)
                    if g == 1 and u == 0:
                        eng.wait_ge(kd_mm, 5)
                    nc.scalar.copy(kidxT[:, u // 2, (u % 2) * 512:(u % 2) * 512 + 512], bank[4 + u % 2][:, :]).then_inc(kx_ev, 1)
                for d in range(5):
                    eng.wait_ge(kd_mm, 5 * g + d + 1)
                    b_ = bank[6 + (5 * g + d) % 2]
                    if d < 4:
                        e, ch = d // 2, d % 2
                        dst = R[:, g, 0:PAST].rearrange("p (j e k) -> p e j k", e=2, k=P)[:, e, 4 * ch:4 * ch + 4, :]
                        src = b_[:, :].rearrange("p (j k) -> p j k", k=P)
                    else:
                        dst, src = R[:, g, PAST:NKEY], b_[:, 0:NS]
                    nc.scalar.activation(dst, src, ACT.Relu, scale=IDX_SCALE).then_inc(kd_ev, 1)

            for c in range(5):
                eng.wait_ge(ks_mm, c + 1)
                if c < 4:
                    dst = scs[:, 0:PAST].rearrange("q (p r) -> q r p", r=16)[:, 4 * c:4 * c + 4, :]
                    ins = nc.scalar.copy(dst, bank[4 + c % 2][0:NS, :].rearrange("q (r p) -> q r p", r=4))
                else:
                    ins = nc.scalar.copy(scs[:, PAST:NKEY], bank[4][0:NS, 0:NS])
                ins.then_inc(ks_ev, 1)

            for m in range(CT + 1):
                if m < CT:
                    rotary_tile(5 + m, E_Q + 2 * m)
                if m == CT - 1:
                    load_block(3)
                if m >= 1:
                    place_queries(4 + m, m - 1, q_s)
            eng.wait_ge(q_placed, 2 * CT)
            for m in range(CT):
                for hh in range(2):
                    dst = qbd[HD * hh:HD * hh + HD, :, m, (2 * m + hh) * DEC_SEQ:(2 * m + hh + 1) * DEC_SEQ]
                    last = nc.scalar.copy(dst, q_s[HD * hh:HD * hh + HD, m, :].rearrange("p (b t) -> p b t", t=DEC_SEQ))
            last.then_inc(qbd_rd, 1)

            def lru_taps(c):
                if c > 0:
                    eng.wait_ge(scan_rd, c)
                else:
                    eng.wait_ge(rope_out, 13)
                for j, out in enumerate((xc, gi, ga, dd)):
                    w = par[:, CONV_W0 + 4 * j + c:CONV_W0 + 4 * j + c + 1]
                    bias = par[:, CONV_B + c:CONV_B + c + 1] if j == 0 else 0.0
                    prompt = xl[:, c, j:j + SEQ]
                    sample = xl[:, c, 3 + SEQ:XW].rearrange("p (b w) -> p b w", w=3 + DEC_SEQ)[:, :, j:j + DEC_SEQ]
                    if j == 0:
                        eng.wait_ge(gemm_ev, E_XL + 2 * c + 2)
                    nc.scalar.activation(out[:, 0:SEQ], prompt, ACT.Identity, bias=bias, scale=w)
                    ins = nc.scalar.activation(out[:, SEQ:NT].rearrange("p (b t) -> p b t", t=DEC_SEQ), sample, ACT.Identity, bias=bias, scale=w)
                ins.then_inc(taps_rd, 1)

            def lru_gates(c, u):
                gate, hf = u // 2, u % 2
                eng.wait_ge(lg_mm, 4 * c + u + 1)
                bias = par[:, (B_A, B_I)[gate] + c:(B_A, B_I)[gate] + c + 1]
                nc.scalar.activation((ga, gi)[gate][:, hf * HALF:(hf + 1) * HALF], bank[6 + u % 2][:, 0:HALF],
                                     ACT.Sigmoid, bias=bias).then_inc(lg_ev, 1)

            def lru_decay(c):
                if c == 0:
                    eng.wait_ge(sp_rd, 1)
                eng.wait_ge(lg_ev, 4 * c + 4)
                link(nc.scalar.activation(aa, ga, ACT.Exp, scale=sp[:, c:c + 1]))
                nc.scalar.activation(dd, aa, ACT.Square)
                nc.scalar.activation(ga, ga, ACT.Tanh, scale=sp[:, c:c + 1]).then_inc(tanh_rd, 1)

            def lru_root(c):
                eng.wait_ge(dd_rd, c + 1)
                nc.scalar.activation(dd, dd, ACT.Sqrt, scale=-1.0).then_inc(root_rd, 1)

            def unit_end(unit):
                c, stage = unit // 3, unit % 3
                if unit >= 0 and stage == 1:
                    lru_gates(c, 0)
                    lru_gates(c, 1)
                for i in range(2):
                    sample_scores(8 + 2 * unit + i)
                if unit >= 0 and stage == 0:
                    lru_taps(c)
                elif unit >= 0 and stage == 1:
                    lru_gates(c, 2)
                    lru_gates(c, 3)
                    lru_decay(c)
                elif unit >= 0:
                    lru_root(c)

            def sample_scores(s):
                eng.wait_ge(k_mm, s + 1)
                nc.scalar.mul(S[:, s // NPG, (s % NPG) * P:(s % NPG + 1) * P], bank[4 + s % 2][:, 0:P], SCALE).then_inc(k_ev, 1)

            for m in range(CT):
                rotary_tile(9 + m, E_K + 2 * m)
                sample_scores(2 * m)
                sample_scores(2 * m + 1)
            load_block(4)
            for m in range(CT):
                for hf in range(2):
                    e = E_XL + 2 * m + hf
                    src = gemm_out(e)
                    if hf == 0:
                        nc.scalar.copy(xl[:, m, 3:3 + HALF], src[:, 0:HALF]).then_inc(gemm_ev, 1)
                    else:
                        n = SEQ - HALF
                        nc.scalar.copy(xl[:, m, 3 + HALF:3 + SEQ], src[:, 0:n])
                        dst = xl[:, m, 3 + SEQ:XW].rearrange("p (b w) -> p b w", w=3 + DEC_SEQ)[:, :, 3:3 + DEC_SEQ]
                        nc.scalar.copy(dst, src[:, n:n + NS].rearrange("p (b t) -> p b t", t=DEC_SEQ)).then_inc(gemm_ev, 1)
                unit_end(m)
            load_block(5)
            for m in range(CT):
                for hf in range(2):
                    src = gemm_out(E_GATE + 2 * m + hf)
                    if m == 0 and hf == 0:
                        eng.wait_ge(ks_mm, 5)
                    nc.scalar.activation(mixT[:, m, hf * HALF:(hf + 1) * HALF], src[:, 0:HALF], ACT.Gelu_apprx_tanh).then_inc(gemm_ev, 1)
                unit_end(4 + m)
            for j in range(5):
                src = gemm_out(E_V + j)
                n = P if j < 4 else NS
                nc.scalar.copy(v[0:n, j, :], src[0:n, :]).then_inc(gemm_ev, 1)
                if j < 4:
                    unit_end(8 + j)
            eng.wait_ge(gemm_mm, E_WO)
            load_block(6)
            for g in range(GRP):
                eng.wait_ge(kn_mm, g + 1)
                nc.scalar.mul(S[:, g, PAST:NKEY], bank[4 + g][:, 0:NS], SCALE).then_inc(kn_ev, 1)

            for g in range(GRP):
                eng.wait_ge(smax_rd, g + 1)
                nc.scalar.activation(S[:, g, :], S[:, g, :], ACT.Exp, bias=sstat[:, g, 6:7], accum_out=sstat[:, g, 7:8]).then_inc(se_rd, 1)

            def sample_transposed(n):
                g, q = n // 5, n % 5
                b_ = bank[2 + (n % 2 if g == 0 else 1)]
                eng.wait_ge(st_tr, n + 1)
                if q < 4:
                    ins = nc.scalar.copy(pT[:, g, 4 * q:4 * q + 4, :], b_[:, :].rearrange("p (r c) -> p r c", r=4))
                else:
                    ins = nc.scalar.copy(pT[0:NS, g, 16, :], b_[0:NS, 0:P])
                ins.then_inc(st_ev, 1)

            def exponentials(u):
                nk = P * (u // NH + 1)
                eng.wait_ge(pa_m, u + 1)
                nc.scalar.activation(probs[u % 4][:, 0:nk], probs[u % 4][:, 0:nk], ACT.Exp, bias=stat[:, u % 4, 1:2],
                                     accum_out=stat[:, u % 4, 2:3]).then_inc(pa_e, 1)

            def transposed_out(u):
                nk = P * (u // NH + 1)
                eng.wait_ge(pa_t, u + 1)
                if u == 0:
                    eng.wait_ge(kd_mm, 10)
                nc.scalar.copy(probsT[u % 4][:, 0:nk], bank[6 + u % 2][:, 0:nk]).then_inc(pa_te, 1)

            for u in range(ATT_UNITS + 2):
                if u < ATT_UNITS:
                    exponentials(u)
                if u < 10:
                    sample_transposed(u)
                if u >= 2:
                    transposed_out(u - 2)

            for g in range(GRP):
                eng.wait_ge(so_tr, g + 1)
                for m in range(CT):
                    for hh in range(2):
                        h = 2 * m + hh
                        src = bank[6 + g][HD * hh:HD * hh + HD, m * P:(m + 1) * P].rearrange("p (b h t) -> p b h t", b=4, h=NH)[:, :, h, :]
                        dst = mixT[HD * hh:HD * hh + HD, 4 + m, SEQ + 16 * g:SEQ + 16 * g + 16].rearrange("p (b t) -> p b t", b=4)
                        last = nc.scalar.copy(dst, src)
                last.then_inc(so_ev, 1)

            def mixer_out(hf, m):
                src = gemm_out(E_WO + KT * hf + m)
                c = half_cols[hf]
                nc.scalar.activation(oT[:, m, c], src[:, 0:HALF], ACT.Identity, scale=par[:, G_POST_MIX + m:G_POST_MIX + m + 1])
                nc.scalar.activation(sqT[:, m, c], src[:, 0:HALF], ACT.Square).then_inc(gemm_ev, 1)

            def residual_squares(hf, tiles_):
                for k in tiles_:
                    if k in POOL_TILES:
                        eng.wait_ge(x1_pool, hf * len(POOL_TILES) + POOL_TILES.index(k) + 1)
                    else:
                        eng.wait_ge(x1_rd, hf * (KT - len(POOL_TILES)) + k + 1 - sum(p < k for p in POOL_TILES))
                    nc.scalar.activation(sqT[:, k, half_cols[hf]], xT[:, k, half_cols[hf]], ACT.Square).then_inc(sq_rd, 1)

            def round_input(hf, tiles_):
                for k in tiles_:
                    eng.wait_ge(hn_f, hf * KT + k + 1)
                    nc.scalar.copy(hn_hi[:, k, half_cols[hf]], normed[:, k % 4, half_cols[hf]]).then_inc(hn_hi_rd, 1)

            def round_piece(n, parity, freed, uses):
                eng.wait_ge(freed, uses)
                eng.wait_ge(piece_in[parity], (n - parity) * 8 + 16)
                nc.scalar.copy(w_hi[parity][:, :], w_raw[:, parity, :]).then_inc(w_hi_rd, 1)

            for m in range(KT):
                mixer_out(0, m)
            mixer_out(1, 0)
            root_mean_square("mix0")
            mixer_out(1, 1)
            residual_squares(0, range(0, 4))
            mixer_out(1, 2)
            residual_squares(0, range(4, KT))
            mixer_out(1, 3)
            mixer_out(1, 4)
            root_mean_square("x0")
            mixer_out(1, 5)
            for n in range(2):
                round_piece(n, n, gemm_mm, E_WO + 12)
            round_input(0, range(0, 4))
            mixer_out(1, 6)
            round_input(0, range(4, KT))
            mixer_out(1, 7)
            root_mean_square("mix1")
            residual_squares(1, range(KT))
            root_mean_square("x1")
            round_input(1, range(KT))

            def rectify(j, parity):
                for hf in range(2):
                    u = j * 2 + hf
                    if hf == 0:
                        eng.wait_ge(h_sq, j - 1)
                    eng.wait_ge(h_mm, u + 1)
                    nc.scalar.activation(relu_t[:, parity, hf * HALF:(hf + 1) * HALF], bank[(2 * parity + hf) % 4][:, 0:HALF], ACT.Relu).then_inc(h_ev, 1)

            def round_hidden(j, half, parity):
                eng.wait_ge(h_sq, j + 1)
                nc.scalar.copy(h_hi[:, bass.ds((j - half * HT) * NT, NT)], square_t[:, parity, :]).then_inc(h_hi_rd, 1)

            def weighted(v, parity, hf):
                eng.wait_ge(f_mm, v + 1)
                return bank[(2 * parity + hf) % 4][:, 0:HALF]

            eng.wait_ge(state_stored, 16 * 5)
            for half in range(2):
                j0, n0, v0 = half * HT, half * PIECES // 2, half * 2 * KT
                if half == 1:
                    round_piece(n0 + 1, 1, f_mm, v0)
                if half == 0:
                    for hf in range(2):
                        for j in range(2):
                            eng.wait_ge(h_mm, 2 * hf + j + 1)
                            nc.scalar.activation(relu_t[:, j, half_cols[hf]], bank[2 * j + hf][:, 0:HALF], ACT.Relu).then_inc(h_ev, 1)
                            if hf == 1 and j == 0:
                                round_piece(2, 0, h_mm, 3)
                else:
                    rectify(j0, 0)
                    round_piece(n0 + 2, 0, h_mm, 2 * j0 + 2)
                    rectify(j0 + 1, 1)
                round_hidden(j0, half, 0)
                with eng.Fori(0, HT // 2 - 1) as i:
                    for s in range(2):
                        j = i * 2 + (j0 + 2 + s)
                        round_piece(i * 2 + (n0 + 3 + s), (1 + s) % 2, h_mm, i * 4 + (2 * j0 + 4 + 2 * s))
                        rectify(j, s)
                        round_hidden(i * 2 + (j0 + 1 + s), half, (1 + s) % 2)
                round_hidden(j0 + HT - 1, half, 1)
                round_piece(n0 + HT + 1, 1, h_mm, 2 * (j0 + HT))
                round_piece(n0 + HT + 2, 0, half_mm, KT * half + 1)

                def output(m, parity, last=False):
                    if half == 0:
                        for hf in range(2):
                            src = weighted(m * 2 + (v0 + hf), parity, hf)
                            nc.scalar.copy(regM[:, bass.ds(m * NT + hf * HALF, HALF)], src).then_inc(f_ev, 1)
                    else:
                        for hf in range(2):
                            eng.wait_ge(f_add, m * 2 + (hf + 1))
                            c = m * NT + hf * HALF
                            nc.scalar.activation(regQ[:, bass.ds(c, HALF)], regM[:, bass.ds(c, HALF)], ACT.Square).then_inc(f_sq, 1)

                output(0, 0)
                with eng.Fori(0, (KT - 2) // 2) as i:
                    for s in range(2):
                        m = i * 2 + (1 + s)
                        round_piece(i * 4 + (n0 + HT + 3 + 2 * s), 1, f_mm, i * 4 + (v0 + 2 + 2 * s))
                        round_piece(i * 4 + (n0 + HT + 4 + 2 * s), 0, half_mm, i * 2 + (KT * half + 2 + s))
                        output(m, (1 + s) % 2)
                round_piece(n0 + HT + 2 * KT - 1, 1, f_mm, v0 + 2 * KT - 2)
                if half == 0:
                    round_piece(n0 + HT + 2 * KT, 0, half_mm, KT)
                output(KT - 1, 1)
            root_mean_square("mlp")

        @block.vector
        def _(eng):
            steps = [0]
            vec = nc.vector

            def link(ins):
                steps[0] += 1
                ins.then_inc(dve_step, 1)
                eng.wait_ge(dve_step, steps[0])

            vec.memset(eps[:, :], EPS)
            vec.memset(averager[:, :], 1.0 / D_MODEL).then_inc(averager_rd, 1)
            for k in range(1, KT, 2):
                eng.wait_ge(x_in[k // 2], 16)
                link(vec.tensor_tensor(hnT[:, k, :], xT[:, k, :], xT[:, k, :], ALU.mult))
                eng.wait_ge(sq_even, k // 2 + 1)
                vec.tensor_tensor(hnT[:, k, :], hnT[:, k, :], hnT[:, k - 1, :], ALU.add).then_inc(sq_pair, 1)

            def inverse_rms(norm):
                roots = roots_before(norm)
                for b, c in zip(NORMS[NORM[norm]][1], half_cols):
                    if b is not None:
                        roots += 1
                        eng.wait_ge(rms_rd, roots)
                        ins = vec.reciprocal(rstd[:, c], rstd[:, c])
                ins.then_inc(rstd_rd, 1)
                eng.wait_ge(rstd_rd, NORM[norm])

            eng.wait_ge(par_in, 16)
            for hf, c in enumerate(half_cols):
                eng.wait_ge(rms_rd, hf + 1)
                vec.reciprocal(rstd[:, c], rstd[:, c]).then_inc(first_rstd, 1)
                eng.wait_ge(first_rstd, hf + 1)
                for k in range(KT):
                    vec.scalar_tensor_tensor(out=hnT[:, k, c], in0=xT[:, k, c], scalar=par[:, G_PRE_MIX + k:G_PRE_MIX + k + 1],
                                             in1=rstd[:, c], op0=ALU.mult, op1=ALU.mult).then_inc(hn_rd, 1)

            eng.wait_ge(const_in, 16 * N_CONST)
            vec.tensor_scalar(row_i[:, :], pt_own[:, :], float(PAGE // 16), keyoff[:, 0:1], ALU.mult, ALU.add).then_inc(rows_rd, 1)
            for c in range(CT):
                dst = xl[:, c, 3 + SEQ:XW].rearrange("p (b w) -> p b w", w=3 + DEC_SEQ)[:, :, 0:3]
                src = par[:, CONV0 + 24 * c:CONV0 + 24 * c + 24].rearrange("p (b w) -> p b w", w=3)
                vec.tensor_copy(dst, src)

            lam, z = par[:, LAM:LAM + CT], sp[:, CT:2 * CT]
            link(vec.tensor_scalar(z, lam, -1.0, None, ALU.mult))
            link(vec.tensor_tensor(sp[:, 2 * CT:3 * CT], lam, z, ALU.min))
            vec.tensor_scalar(sp[:, 3 * CT:4 * CT], z, 0.0, None, ALU.max).then_inc(lam_rd, 1)
            eng.wait_ge(explam_rd, 1)
            ez, s1, s2, acc = (sp[:, i * CT:(i + 1) * CT] for i in (4, 5, 6, 7))
            link(vec.tensor_scalar(s1, ez, 2.0, None, ALU.add))
            link(vec.reciprocal(s1, s1))
            link(vec.tensor_tensor(s1, s1, ez, ALU.mult))
            link(vec.tensor_tensor(s2, s1, s1, ALU.mult))
            link(vec.tensor_scalar(acc, s2, 1.0 / 17, None, ALU.mult))
            for odd in range(15, 1, -2):
                link(vec.scalar_tensor_tensor(out=acc, in0=acc, scalar=1.0 / odd, in1=s2, op0=ALU.add, op1=ALU.mult))
            link(vec.scalar_tensor_tensor(out=acc, in0=acc, scalar=1.0, in1=s1, op0=ALU.add, op1=ALU.mult))
            link(vec.scalar_tensor_tensor(out=acc, in0=acc, scalar=2.0, in1=sp[:, 3 * CT:4 * CT], op0=ALU.mult, op1=ALU.add))
            vec.tensor_scalar(sp[:, 0:CT], acc, -RG_C, None, ALU.mult).then_inc(sp_rd, 1)


            vec.tensor_copy(ind_r[:, :, :], ind[:, :, :])
            eng.wait_ge(wi_tr, 1)
            vec.tensor_copy(kwrow[:, 0:4, :], bank[6][:, 0:288].rearrange("p (j c) -> p j c", j=4))
            vec.tensor_copy(kwrow[0:NS, 4, :], bank[6][0:NS, 288:360]).then_inc(wi_rd, 1)
            eng.wait_ge(wi_rd, 1)
            for g in range(GRP):
                wi = kwrow[0:NS, 4, HD:HD + NH].unsqueeze(1).unsqueeze(3).to_broadcast([NS, 4, NH, DEC_SEQ])
                ins = vec.tensor_tensor(wT[:, g, :].rearrange("p (b h t) -> p b h t", b=4, h=NH),
                                        ind[:, g, :].rearrange("p (b h t) -> p b h t", b=4, h=NH), wi, ALU.mult)
            ins.then_inc(wT_rd, 1)
            eng.wait_ge(wT_tr, 1)
            vec.tensor_copy(wm[:, :, :], bank[7][:, 0:GRP * NS].rearrange("p (g c) -> p g c", g=GRP)).then_inc(wm_rd, 1)
            for u in range(24):
                n, h = u // NH + 1, u % NH
                nk = P * (n + 1)
                acc = scp[:, SCP_AT[n]:SCP_AT[n] + nk]
                w = kwrow[:, n, HD + h:HD + h + 1]
                eng.wait_ge(pi_ev, u + 1)
                if h == 0:
                    ins = vec.tensor_scalar(acc, sm[:, u % 2, 0:nk], w, None, ALU.mult)
                else:
                    ins = vec.scalar_tensor_tensor(out=acc, in0=sm[:, u % 2, 0:nk], scalar=w, in1=acc, op0=ALU.mult, op1=ALU.add)
                ins.then_inc(pi_acc, 1)
                eng.wait_ge(pi_acc, u + 1)
            for n in range(1, QB):
                last = scp[:, SCP_AT[n] + n * P:SCP_AT[n] + (n + 1) * P]
                link(vec.tensor_tensor(last, last, causal[:, :], ALU.add))
            link(vec.tensor_copy(work_p, scp[:, :]))
            wp = {n: work_p[:, SCP_AT[n]:SCP_AT[n] + P * (n + 1)] for n in range(1, QB)}
            for i in range(TOPK_P // 8):
                for n in range(1, QB):
                    vec.max(m8[:, n - 1, :], wp[n]).then_inc(tk_p, 1)
                for n in range(1, QB):
                    eng.wait_ge(tk_p, 6 * i + n)
                    vec.match_replace(wp[n], m8[:, n - 1, :], wp[n], TAKEN).then_inc(tk_p, 1)
                eng.wait_ge(tk_p, 6 * i + 6)
            link(vec.tensor_tensor(work_p, work_p, scp[:, :], ALU.not_equal))
            link(vec.tensor_scalar(scp[:, :], work_p, -OUT_OF_REACH, OUT_OF_REACH, ALU.mult, ALU.add))
            eng.wait_ge(ks_ev, 5)
            link(vec.tensor_tensor(scs[:, PAST:NKEY], scs[:, PAST:NKEY], newmask[:, :], ALU.add))
            link(vec.tensor_copy(work_s, scs))

            def scan(c):
                eng.wait_ge(u_rd, c + 1)
                vec.tensor_tensor_scan(xl[:, c, 0:NT], aa, gi, 0.0, ALU.mult, ALU.add).then_inc(scan_rd, 1)

            for i in range(TOPK_S // 8):
                vec.max(m8[0:NS, 0, :], work_s).then_inc(tk_s, 1)
                eng.wait_ge(tk_s, 2 * i + 1)
                vec.match_replace(work_s, m8[0:NS, 0, :], work_s, TAKEN).then_inc(tk_s, 1)
                eng.wait_ge(tk_s, 2 * i + 2)
                if i in SCAN_ROUNDS:
                    scan(SCAN_ROUNDS.index(i))
            link(vec.tensor_tensor(work_s, work_s, scs, ALU.not_equal))
            vec.tensor_scalar(smask[:, :], work_s, -OUT_OF_REACH, OUT_OF_REACH, ALU.mult, ALU.add).then_inc(smask_rd, 1)
            scan(CT - 1)

            for g in range(GRP):
                for c in range(5):
                    n = 5 * g + c
                    cols = slice(c * 512, min((c + 1) * 512, NKEY))
                    w = cols.stop - cols.start
                    eng.wait_ge(sm_mm, n + 1)
                    eng.wait_ge(kn_ev, g + 1)
                    vec.tensor_tensor_reduce(out=S[:, g, cols], in0=S[:, g, cols], in1=bank[2 + n % 2][:, 0:w], scale=1.0, scalar=TAKEN,
                                             op0=ALU.add, op1=ALU.max, accum_out=sstat[:, g, c:c + 1]).then_inc(sm_ev, 1)
                eng.wait_ge(sm_ev, 5 * g + 5)
                link(vec.tensor_reduce(sstat[:, g, 5:6], sstat[:, g, 0:5], AX_X, ALU.max))
                vec.tensor_scalar(sstat[:, g, 6:7], sstat[:, g, 5:6], -1.0, None, ALU.mult).then_inc(smax_rd, 1)
            def masked(u):
                n, h = u // NH, u % NH
                nk = P * (n + 1)
                mask = causal[:, :] if n == 0 else scp[:, SCP_AT[n]:SCP_AT[n] + nk]
                eng.wait_ge(pa_s, u + 1)
                if u >= 4:
                    eng.wait_ge(pa_t, u - 3)
                link(vec.tensor_tensor_reduce(out=probs[u % 4][:, 0:nk], in0=bank[4 + u % 2][:, 0:nk], in1=mask, scale=SCALE, scalar=TAKEN,
                                              op0=ALU.add, op1=ALU.max, accum_out=stat[:, u % 4, 0:1]))
                vec.tensor_scalar(stat[:, u % 4, 1:2], stat[:, u % 4, 0:1], -1.0, None, ALU.mult).then_inc(pa_m, 1)

            def row_sum(u):
                eng.wait_ge(pa_e, u + 1)
                vec.reciprocal(stat[:, u % 4, 3:4], stat[:, u % 4, 2:3]).then_inc(pa_r, 1)

            def pair_out(w):
                eng.wait_ge(pa_o, w + 1)
                n, m = w // CT, w % CT
                vec.tensor_copy(mixT[:, 4 + m, n * P:(n + 1) * P], bank[w % 2][:, 0:P]).then_inc(pa_oe, 1)

            for u in range(ATT_UNITS + 5):
                if u < ATT_UNITS:
                    masked(u)
                if 1 <= u <= ATT_UNITS:
                    row_sum(u - 1)
                if u >= 6 and u % 2 == 0:
                    pair_out((u - 6) // 2)

            for g in range(GRP):
                eng.wait_ge(se_rd, g + 1)
                link(vec.reciprocal(sstat[:, g, 0:1], sstat[:, g, 7:8]))
            for g in range(GRP):
                eng.wait_ge(v_mm, 16 * (g + 1))
                vec.tensor_scalar(so[:, g, :], bank[2 + g][:, :], sstat[:, g, 0:1], None, ALU.mult).then_inc(so_rd, 1)

            eng.wait_ge(x_again, 16)

            def rest_of_piece(n, parity):
                eng.wait_ge(w_hi_rd, n + 1)
                vec.tensor_tensor(w_lo[parity][:, :], w_raw[:, parity, :], w_hi[parity][:, :].bitcast(F32), ALU.subtract).then_inc(w_lo_rd, 1)

            def rest_of_input(hf, k):
                if k not in POOL_RESTS:
                    c = half_cols[hf]
                    eng.wait_ge(hn_hi_rd, hf * KT + k + 1)
                    vec.tensor_tensor(hn_lo[:, k, c], normed[:, k % 4, c], hn_hi[:, k, c].bitcast(F32), ALU.subtract).then_inc(hn_lo_rd, 1)

            def sum_of_squares(hf, landed, counts, first=1, last=KT):
                c = half_cols[hf]
                for k in range(first, last):
                    eng.wait_ge(landed, counts + k + 1)
                    ins = vec.tensor_tensor(sqT[:, 0, c], sqT[:, 0, c], sqT[:, k, c], ALU.add)
                    if k < KT - 1:
                        link(ins)
                if last == KT:
                    ins.then_inc(sum_rd, 1)

            own_tiles, own_rests = KT - len(POOL_TILES), KT - len(POOL_RESTS)
            for hf, c in enumerate(half_cols):
                sum_of_squares(hf, gemm_ev, E_WO + hf * KT, first=5 if hf else 1)
                inverse_rms(f"mix{hf}")
                for k in range(KT):
                    if k not in POOL_TILES:
                        link(vec.tensor_tensor(oT[:, k, c], oT[:, k, c], rstd[:, c], ALU.mult))
                        vec.tensor_tensor(xT[:, k, c], xT[:, k, c], oT[:, k, c], ALU.add).then_inc(x1_rd, 1)
                if hf == 0:
                    sum_of_squares(0, sq_rd, 0)
                    sum_of_squares(1, gemm_ev, E_WO + KT, last=5)
                inverse_rms(f"x{hf}")
                eng.wait_ge(x1_pool, (hf + 1) * len(POOL_TILES))
                eng.wait_ge(x1_rd, (hf + 1) * own_tiles)
                for k in range(KT):
                    if k >= 4 and k - 4 in POOL_RESTS:
                        eng.wait_ge(hn_lo_pool, hf * len(POOL_RESTS) + POOL_RESTS.index(k - 4) + 1)
                    elif k >= 4:
                        eng.wait_ge(hn_lo_rd, hf * own_rests + k - 3 - sum(p < k - 4 for p in POOL_RESTS))
                    vec.scalar_tensor_tensor(out=normed[:, k % 4, c], in0=xT[:, k, c], scalar=par[:, G_PRE_FFN + k:G_PRE_FFN + k + 1],
                                             in1=rstd[:, c], op0=ALU.mult, op1=ALU.mult).then_inc(hn_f, 1)
                    if k >= 2:
                        rest_of_input(hf, k - 2)
                rest_of_input(hf, KT - 2)
                rest_of_input(hf, KT - 1)

            def rest_of_hidden(j, half, parity):
                at = bass.ds((j - half * HT) * NT, NT)
                eng.wait_ge(h_hi_rd, j + 1)
                vec.tensor_tensor(h_lo[:, at], square_t[:, parity, :], h_hi[:, at].bitcast(F32), ALU.subtract).then_inc(h_lo_rd, 1)

            for half in range(2):
                j0, n0, v0 = half * HT, half * PIECES // 2, half * 2 * KT
                if half == 1:
                    rest_of_piece(n0 + 1, 1)
                rest_of_piece(n0 + 2, 0)
                rest_of_hidden(j0, half, 0)
                with eng.Fori(0, HT // 2 - 1) as i:
                    for s in range(2):
                        rest_of_piece(i * 2 + (n0 + 3 + s), (1 + s) % 2)
                        rest_of_hidden(i * 2 + (j0 + 1 + s), half, (1 + s) % 2)
                rest_of_hidden(j0 + HT - 1, half, 1)
                rest_of_piece(n0 + HT + 1, 1)
                rest_of_piece(n0 + HT + 2, 0)

                def add_output(m, parity):
                    if half == 1:
                        for hf in range(2):
                            out = regM[:, bass.ds(m * NT + hf * HALF, HALF)]
                            eng.wait_ge(f_mm, m * 2 + (v0 + hf + 1))
                            vec.tensor_tensor(out, out, bank[(2 * parity + hf) % 4][:, 0:HALF], ALU.add).then_inc(f_add, 1)

                def add_squares(m):
                    eng.wait_ge(f_sq, m * 2 + 2)
                    return vec.tensor_tensor(regQ[:, 0:NT], regQ[:, 0:NT], regQ[:, bass.ds(m * NT, NT)], ALU.add)

                add_output(0, 0)
                with eng.Fori(0, (KT - 2) // 2) as i:
                    for s in range(2):
                        rest_of_piece(i * 4 + (n0 + HT + 3 + 2 * s), 1)
                        rest_of_piece(i * 4 + (n0 + HT + 4 + 2 * s), 0)
                        add_output(i * 2 + (1 + s), (1 + s) % 2)
                        if half == 1:
                            add_squares(i * 2 + (1 + s)).then_inc(sq_sum, 1)
                            eng.wait_ge(sq_sum, i * 2 + (1 + s))
                rest_of_piece(n0 + HT + 2 * KT - 1, 1)
                if half == 0:
                    rest_of_piece(n0 + HT + 2 * KT, 0)
                add_output(KT - 1, 1)
            add_squares(KT - 1).then_inc(sum_rd, 1)
            inverse_rms("mlp")
            for k in range(KT):
                if k not in POOL_TILES:
                    link(vec.scalar_tensor_tensor(out=fT[:, k, :], in0=fT[:, k, :], scalar=par[:, G_POST_FFN + k:G_POST_FFN + k + 1],
                                                  in1=rstd, op0=ALU.mult, op1=ALU.mult))
                    vec.tensor_tensor(xT[:, k, :], xT[:, k, :], fT[:, k, :], ALU.add).then_inc(y_rd, 1)

        @block.tensor
        def _(eng):
            pe = nc.tensor

            def mean_square(norm, squares, k, first=0):
                for b, c in zip(NORMS[NORM[norm]][1], half_cols):
                    if b is not None:
                        ins = pe.matmul(bank[b][:, 0:HALF], averager[:, :], squares[:, k, c], start=(k == first), stop=(k == KT - 1))
                if k == KT - 1:
                    ins.then_inc(ssq_mm, 1)

            def slot_free(e):
                if e >= 4:
                    eng.wait_ge(gemm_ev, e - 3)

            def product(e, hf, lhs, rhs, parts=P, ready=None):
                slot_free(e)
                for k in range(KT):
                    if ready:
                        ready(k)
                    ins = pe.matmul(bank[e % 4][0:parts, 0:HALF], lhs(k), rhs[:, k, hf * HALF:(hf + 1) * HALF],
                                    start=(k == 0), stop=(k == KT - 1))
                ins.then_inc(gemm_mm, 1)

            def tile_product(e, w, m, rhs):
                for hf in range(2):
                    product(e + hf, hf, lambda k: w[:, k, m * P:(m + 1) * P], rhs)

            def weights(n):
                slot = BLOCK_SLOT[n]
                eng.wait_ge(w_in[slot], 16 * BLOCK_SLOT[:n + 1].count(slot))
                return wslot[slot]

            eng.wait_ge(averager_rd, 1)
            for i in range(KT // 2):
                eng.wait_ge(sq_pair, i + 1)
                mean_square("in", hnT, 2 * i + 1, first=1)
            w = weights(0)
            for m in range(CT):
                if m == 0:
                    for hf in range(2):
                        product(E_QI + hf, hf, lambda k: w[:, k, 0:P], hnT, ready=lambda k: eng.wait_ge(hn_rd, hf * KT + k + 1))
                else:
                    tile_product(E_QI + 2 * m, w, m, hnT)
            eng.wait_ge(kw_in, 16)
            for hf in range(2):
                product(E_KW + hf, hf, lambda k: wkw[:, k, :], hnT, 72)
            w = weights(1)
            tile_product(E_Q, w, 0, hnT)
            eng.wait_ge(ki_dup, 1)
            eng.wait_ge(const_in, 16 * N_CONST)
            for j in range(5):
                n = P if j < 4 else NS
                ins = pe.transpose(bank[6][0:n, 72 * j:72 * j + 72], kw[0:72, j * P:j * P + n], ident[0:72, 0:72])
            ins.then_inc(wi_tr, 1)
            eng.wait_ge(wT_rd, 1)
            for g in range(GRP):
                ins = pe.transpose(bank[7][:, g * NS:(g + 1) * NS], wT[:, g, :], ident[0:NS, 0:NS])
            ins.then_inc(wT_tr, 1)
            eng.wait_ge(zero_rd, 1)
            eng.wait_ge(q_placed, CT)
            for u in range(24):
                n, h = u // NH + 1, u % NH
                nk = P * (n + 1)
                if u >= 2:
                    eng.wait_ge(pi_ev, u - 1)
                elif u == 1:
                    eng.wait_ge(wm_rd, 1)
                pe.matmul(bank[6 + u % 2][:, 0:nk], qz[:, h, n * P:(n + 1) * P], kiT[:, 0:nk], start=True, stop=True).then_inc(pi_mm, 1)
            eng.wait_ge(qis_rd, 1)
            for g in range(GRP):
                if g == 1:
                    tile_product(E_Q + 2, w, 1, hnT)
                eng.wait_ge(kidx_in, 64 * (g + 1))
                for u in range(8):
                    n = 8 * g + u
                    if n >= 2:
                        eng.wait_ge(kx_ev, n - 1)
                    for j in range(4):
                        ins = pe.transpose(bank[4 + u % 2][:, j * P:(j + 1) * P],
                                           kidx_in_sb[:, u // 2, ((u % 2) * 4 + j) * P:((u % 2) * 4 + j + 1) * P], ident[:, :])
                    ins.then_inc(kx_tr, 1)
                eng.wait_ge(kx_ev, 8 * g + 8)
                for d in range(5):
                    n = 5 * g + d
                    if n >= 2:
                        eng.wait_ge(kd_ev, n - 1)
                    else:
                        eng.wait_ge(pi_ev, 24)
                    for b4 in range(4):
                        e, ch = (d // 2, d % 2) if d < 4 else (0, 0)
                        rhs = kidxT[:, b4, ch * 512:ch * 512 + 512] if d < 4 else kiT[:, SEQ:NT]
                        w_ = 512 if d < 4 else NS
                        ins = pe.matmul(bank[6 + n % 2][32 * b4:32 * b4 + 32, 0:w_], qis[:, 4 * g + b4, e, :], rhs, start=True, stop=True)
                    ins.then_inc(kd_mm, 1)
            eng.wait_ge(kd_ev, 10)
            eng.wait_ge(wm_rd, 1)
            for c in range(5):
                cols = slice(c * 512, min((c + 1) * 512, NKEY))
                if c >= 2:
                    eng.wait_ge(ks_ev, c - 1)
                for g in range(GRP):
                    ins = pe.matmul(bank[4 + c % 2][0:NS, 0:cols.stop - cols.start], wm[:, g, :], R[:, g, cols],
                                    start=(g == 0), stop=(g == GRP - 1))
                ins.then_inc(ks_mm, 1)

            for m in range(2, CT):
                tile_product(E_Q + 2 * m, w, m, hnT)

            def key_scores(s):
                slot = (s + 2) % 3
                eng.wait_ge(kv_in[slot], 64 * (s // 3 + 1))
                if s >= 2:
                    eng.wait_ge(k_ev, s - 1)
                elif s == 0:
                    eng.wait_ge(qbd_rd, 1)
                    eng.wait_ge(ks_ev, 5)
                for m in range(CT):
                    for b4 in range(4):
                        ins = pe.matmul(bank[4 + s % 2][32 * b4:32 * b4 + 32, 0:P], qbd[:, 4 * (s // NPG) + b4, m, :],
                                        kv[:, slot, b4, m * P:(m + 1) * P], start=(m == 0), stop=(m == CT - 1))
                ins.then_inc(k_mm, 1)

            def lru_gate(c, u):
                n = 4 * c + u
                if u == 0:
                    eng.wait_ge(xc_rd, c + 1)
                if n >= 2:
                    eng.wait_ge(lg_ev, n - 1)
                hf = u % 2
                pe.matmul(bank[6 + n % 2][:, 0:HALF], wgate[:, u // 2, c, :], xc[:, hf * HALF:(hf + 1) * HALF],
                          start=True, stop=True).then_inc(lg_mm, 1)

            def unit_end(unit):
                gates = unit >= 0 and unit % 3 == 1
                if gates:
                    lru_gate(unit // 3, 0)
                    lru_gate(unit // 3, 1)
                for i in range(2):
                    key_scores(8 + 2 * unit + i)
                if gates:
                    lru_gate(unit // 3, 2)
                    lru_gate(unit // 3, 3)

            for n, e0 in ((2, E_K), (3, E_XL), (4, E_GATE)):
                w = weights(n)
                for m in range(CT):
                    tile_product(e0 + 2 * m, w, m, hnT)
                    unit_end(4 * (n - 3) + m)
            w = weights(5)
            for j in range(5):
                n = P if j < 4 else NS
                e = E_V + j
                slot_free(e)
                for k in range(KT):
                    ins = pe.matmul(bank[e % 4][0:n, :], hnT[:, k, j * P:j * P + n], w[:, k, :], start=(k == 0), stop=(k == KT - 1))
                ins.then_inc(gemm_mm, 1)
                if j < 4:
                    unit_end(8 + j)
            eng.wait_ge(rope_out, 13)
            for g in range(GRP):
                eng.wait_ge(k_ev, KSTEPS)
                for m in range(CT):
                    for b4 in range(4):
                        ins = pe.matmul(bank[4 + g][32 * b4:32 * b4 + 32, 0:NS], qbd[:, 4 * g + b4, m, :], kT[:, m, SEQ:NT],
                                        start=(m == 0), stop=(m == CT - 1))
                ins.then_inc(kn_mm, 1)
            eng.wait_ge(smask_rd, 1)
            eng.wait_ge(gemm_ev, E_WO)
            for g in range(GRP):
                for c in range(5):
                    n = 5 * g + c
                    cols = slice(c * 512, min((c + 1) * 512, NKEY))
                    if n >= 2:
                        eng.wait_ge(sm_ev, n - 1)
                    pe.matmul(bank[2 + n % 2][:, 0:cols.stop - cols.start], ind_r[:, g, :], smask[:, cols], start=True, stop=True).then_inc(sm_mm, 1)
            def sample_transposes(n):
                g, q = n // 5, n % 5
                b_ = bank[2 + (n % 2 if g == 0 else 1)]
                if q == 0:
                    eng.wait_ge(sm_ev, 10)
                    eng.wait_ge(se_rd, g + 1)
                if n >= 2:
                    eng.wait_ge(st_ev, n - 1 if n <= 5 else n)
                if q < 4:
                    for r in range(4 * q, 4 * q + 4):
                        ins = pe.transpose(b_[:, (r % 4) * P:(r % 4 + 1) * P], S[:, g, r * P:(r + 1) * P], ident[:, :])
                else:
                    ins = pe.transpose(b_[0:NS, 0:P], S[:, g, PAST:NKEY], ident[:, :])
                ins.then_inc(st_tr, 1)

            def value_products(s):
                g, r = s // NPG, s % NPG
                eng.wait_ge(v_in[s % V_SLOTS], 64 * (s // V_SLOTS + 1))
                if r == 0:
                    eng.wait_ge(st_ev, 5 * g + 5)
                for b4 in range(4):
                    ins = pe.matmul(bank[2 + g][32 * b4:32 * b4 + 32, :], pT[:, g, r, 32 * b4:32 * b4 + 32], v_slot[s % V_SLOTS][:, b4, :],
                                    start=(r == 0), stop=False)
                if r == NPG - 1:
                    for b4 in range(4):
                        ins = pe.matmul(bank[2 + g][32 * b4:32 * b4 + 32, :], pT[0:NS, g, 16, 32 * b4:32 * b4 + 32], v[0:NS, 4, :],
                                        start=False, stop=True)
                ins.then_inc(v_mm, 1)

            def att_scores(u):
                n, h = u // NH, u % NH
                if u >= 2:
                    eng.wait_ge(pa_m, u - 1)
                else:
                    eng.wait_ge(kn_ev, GRP)
                pe.matmul(bank[4 + u % 2][:, 0:P * (n + 1)], qz[:, h, n * P:(n + 1) * P], kT[:, h // 2, 0:P * (n + 1)],
                          start=True, stop=True).then_inc(pa_s, 1)

            def att_transposes(u):
                n = u // NH
                eng.wait_ge(pa_n, u + 1)
                if u >= 2:
                    eng.wait_ge(pa_te, u - 1)
                else:
                    eng.wait_ge(lg_ev, 16)
                for j in range(n + 1):
                    ins = pe.matmul(bank[6 + u % 2][:, j * P:(j + 1) * P], probs[u % 4][:, j * P:(j + 1) * P], diag[:, u % 4, :],
                                    start=True, stop=True)
                ins.then_inc(pa_t, 1)

            def att_values(w_):
                n, m = w_ // CT, w_ % CT
                eng.wait_ge(pa_te, 2 * w_ + 2)
                if w_ >= 2:
                    eng.wait_ge(pa_oe, w_ - 1)
                else:
                    eng.wait_ge(gemm_ev, E_WO)
                for j in range(n + 1):
                    for hh in range(2):
                        ins = pe.matmul(bank[w_ % 2][HD * hh:HD * hh + HD, 0:P], v[:, j, (2 * m + hh) * HD:(2 * m + hh + 1) * HD],
                                        probsT[(2 * w_ + hh) % 4][:, j * P:(j + 1) * P], start=(j == 0), stop=(j == n))
                ins.then_inc(pa_o, 1)

            for u in range(KSTEPS + 5):
                if u < ATT_UNITS:
                    att_scores(u)
                if u < 10:
                    sample_transposes(u)
                if 2 <= u < ATT_UNITS + 2:
                    att_transposes(u - 2)
                if 4 <= u < ATT_UNITS + 3 and u % 2 == 0:
                    att_values(u // 2 - 2)
                if u >= 5:
                    value_products(u - 5)

            for g in range(GRP):
                eng.wait_ge(so_rd, g + 1)
                if g == 0:
                    eng.wait_ge(pa_te, ATT_UNITS)
                for m in range(CT):
                    ins = pe.transpose(bank[6 + g][:, m * P:(m + 1) * P], so[:, g, m * P:(m + 1) * P], ident[:, :])
                ins.then_inc(so_tr, 1)

            eng.wait_ge(so_ev, GRP)
            eng.wait_ge(pa_oe, ATT_UNITS // 2)
            eng.wait_ge(pk_rd, CT)
            eng.wait_ge(st_ev, 10)
            def mean_of_sum(norm, sums):
                eng.wait_ge(sum_rd, sums)
                for b, c in zip(NORMS[NORM[norm]][1], half_cols):
                    if b is not None:
                        ins = pe.matmul(bank[b][:, 0:HALF], averager[:, :], sqT[:, 0, c], start=True, stop=True)
                ins.then_inc(ssq_mm, 1)

            for hf in range(2):
                for m in range(KT):
                    w = weights(6 + m // CT)
                    product(E_WO + KT * hf + m, hf, lambda k: w[:, k, (m % CT) * P:(m % CT + 1) * P], mixT)
                    if hf == 1 and m == 0:
                        mean_of_sum("mix0", 1)
                    if hf == 1 and m == 4:
                        mean_of_sum("x0", 2)
            mean_of_sum("mix1", 3)
            def three_passes(out, w, rhs_hi, rhs_lo, first, last):
                passes = ((w_hi, rhs_hi), (w_hi, rhs_lo), (w_lo, rhs_hi))
                for k in range(KT):
                    for i, (lhs, rhs) in enumerate(passes):
                        ins = pe.matmul(out, lhs[w][:, k * P:(k + 1) * P], rhs(k), start=(first and k == 0 and i == 0),
                                        stop=(last and k == KT - 1 and i == 2))
                return ins

            def hidden_tile(j, n, parity, wait=True):
                eng.wait_ge(w_lo_rd, n + 1)
                for hf in range(2):
                    if wait:
                        eng.wait_ge(h_ev, j * 2 + (hf - 3))
                    c = slice(hf * HALF, (hf + 1) * HALF)
                    three_passes(bank[2 * parity + hf][:, 0:HALF], parity, lambda k: hn_hi[:, k, c], lambda k: hn_lo[:, k, c],
                                 True, True).then_inc(h_mm, 1)

            def output_tile(m, n, half, parity, wait=True, hidden=None):
                for piece in range(2):
                    eng.wait_ge(w_lo_rd, n + (piece + 1))
                    if hidden is not None and piece == 1:
                        eng.wait_ge(h_lo_rd, hidden)
                    for hf in range(2):
                        if wait and piece == 0:
                            eng.wait_ge((f_ev, f_add)[half], m * 2 + (hf - 3))

                        def part(h):
                            return lambda k: h[:, (piece * KT + k) * NT + hf * HALF:(piece * KT + k) * NT + (hf + 1) * HALF]

                        ins = three_passes(bank[2 * parity + hf][:, 0:HALF], piece, part(h_hi), part(h_lo), piece == 0, piece == 1)
                        if piece == 1:
                            ins.then_inc(f_mm, 1)
                    if piece == 0:
                        ins.then_inc(half_mm, 1)

            for half in range(2):
                j0, n0 = half * HT, half * PIECES // 2
                if half == 1:
                    for s in range(2):
                        eng.wait_ge(f_ev, 2 * KT - 2 + 2 * s)
                        hidden_tile(j0 + s, n0 + s, s, False)
                else:
                    eng.wait_ge(gemm_ev, E_MIX)
                    for hf, c in enumerate(half_cols):
                        for j in range(2):
                            if hf == 0 and j == 1:
                                for k in range(KT):
                                    eng.wait_ge(sq_rd, KT + k + 1)
                                    mean_square("x1", sqT, k)
                            eng.wait_ge(w_lo_rd, j + 1)
                            for k in range(KT):
                                if j == 0 and k in POOL_RESTS:
                                    eng.wait_ge(hn_lo_pool, hf * len(POOL_RESTS) + POOL_RESTS.index(k) + 1)
                                elif j == 0:
                                    eng.wait_ge(hn_lo_rd, hf * (KT - len(POOL_RESTS)) + k + 1 - sum(p < k for p in POOL_RESTS))
                                for i, (lhs, rhs) in enumerate(((w_hi, hn_hi), (w_hi, hn_lo), (w_lo, hn_hi))):
                                    ins = pe.matmul(bank[2 * j + hf][:, 0:HALF], lhs[j][:, k * P:(k + 1) * P], rhs[:, k, c],
                                                    start=(k == 0 and i == 0), stop=(k == KT - 1 and i == 2))
                            ins.then_inc(h_mm, 1)
                with eng.Fori(0, HT // 2 - 1) as i:
                    for s in range(2):
                        hidden_tile(i * 2 + (j0 + 2 + s), i * 2 + (n0 + 2 + s), s)
                for s in range(2):
                    eng.wait_ge(h_ev, 2 * (j0 + HT - 1 + s))
                    eng.wait_ge(h_lo_rd, j0 + KT)
                    output_tile(s, n0 + HT + 2 * s, half, s, False, j0 + HT)
                with eng.Fori(0, KT // 2 - 1) as i:
                    for s in range(2):
                        output_tile(i * 2 + (2 + s), i * 4 + (n0 + HT + 4 + 2 * s), half, s)
            mean_of_sum("mlp", 4)


def kernel(x_prompt, x_sample, cache_k, cache_v, cache_kidx, state_h, state_conv, page_table, g_pre_mix, w_in, conv_w,
           conv_b, w_a, b_a, w_i, b_i, lam, w_out, g_post_mix, g_pre_ffn, w_ff1, w_ff2, g_post_ffn):
    import numpy as np
    import concourse.bacc as bacc
    from concourse.bass_utils import run_bass_kernel_spmd as run

    f4 = np.float32
    a = {k: np.asarray(x) for k, x in dict(
        x_prompt=x_prompt, x_sample=x_sample, ck=cache_k, cv=cache_v, ci=cache_kidx, sh=state_h, sc=state_conv,
        w_in=w_in, w_out=w_out, w1=w_ff1, w2=w_ff2, conv_w=conv_w, w_a=w_a, w_i=w_i).items()}

    tokens = np.concatenate([a["x_prompt"].reshape(SEQ, D_MODEL), a["x_sample"].reshape(NS, D_MODEL)])
    xT = tokens.T.reshape(KT, P, NT).transpose(1, 0, 2).reshape(P, KT * NT)

    def by_channel(x, *rest):
        return np.asarray(x).reshape(-1, P).T

    par = np.concatenate(
        [by_channel(g) for g in (g_pre_mix, g_post_mix, g_pre_ffn, g_post_ffn, conv_w, conv_b, b_a, b_i, lam)]
        + [a["sh"].reshape(DEC_BATCH, CT, P).transpose(2, 1, 0).reshape(P, -1),
           a["sc"].reshape(DEC_BATCH, 3, CT, P).transpose(3, 2, 0, 1).reshape(P, -1)], axis=1)

    def blocks(w, cols):
        k, n = w.shape
        return w.reshape(k // P, P, n // cols, cols).transpose(2, 1, 0, 3).reshape(n // cols, P, -1)

    wi = a["w_in"][0]
    part = {n: wi[:, 512 * i:512 * (i + 1)] for i, n in enumerate(["xl", "gate", "q", "k", "v", "qi"])}
    w_in_blocks = np.concatenate([blocks(part[n], 512) for n in ("qi", "q", "k", "xl", "gate", "v")])
    w1 = blocks(a["w1"][0], P).reshape(2, HT, P, PIECE)
    w2 = a["w2"][0].reshape(2, 2, KT, P, KT, P).transpose(0, 4, 1, 3, 2, 5).reshape(2, 2 * KT, P, PIECE)
    w_mlp = np.concatenate([w1, w2], axis=1).reshape(PIECES, P, PIECE)
    w_kw = wi[:, 3072:3144].reshape(KT, P, 72).transpose(1, 0, 2)
    wgate = np.zeros((P, 2, CT, P), f4)
    for n, w in enumerate((a["w_a"][0], a["w_i"][0])):
        for j in range(8):
            o = HD * (j % 2)
            wgate[o:o + HD, n, j // 2, o:o + HD] = w[j]
    ck = a["ck"][0].reshape(NPOOL, PAGE, CT, P).transpose(0, 3, 2, 1).reshape(NPOOL, P, CT * PAGE)

    half = HD // 2
    freq = f4(10000.0) ** (-np.arange(half, dtype=f4) / f4(half))
    pos = np.concatenate([np.arange(SEQ), np.tile(PAST + np.arange(DEC_SEQ), DEC_BATCH)]).astype(f4)
    ang = (pos[None, :] * freq[:, None]).astype(f4)
    cos, sin = np.cos(ang), np.sin(ang)
    rope = np.concatenate([np.tile(cos, (4, 1)), np.tile(np.concatenate([-sin, sin]), (2, 1))], axis=1).astype(f4)
    q = np.arange(P)
    causal = np.where(q[None, :] > q[:, None], OUT_OF_REACH, 0.0).astype(f4)
    qb, qt = np.arange(NS) // DEC_SEQ, np.arange(NS) % DEC_SEQ
    rb, rt = np.arange(P) // 32, np.arange(P) % DEC_SEQ
    ind = np.stack([(qb[:, None] == rb[None, :] + 4 * g) & (qt[:, None] == rt[None, :]) for g in range(GRP)], axis=1).astype(f4)
    newmask = np.where((qb[:, None] == qb[None, :]) & (qt[None, :] <= qt[:, None]), 0.0, OUT_OF_REACH).astype(f4)
    keyoff = (q[:, None] % 8).astype(f4)

    steps = np.asarray(page_table).reshape(GRP, 4, NPG).transpose(0, 2, 1).reshape(1, KSTEPS * 4)

    arrays = {
        "xT": xT, "par": par, "w_in": w_in_blocks, "w_kw": w_kw, "w_out": blocks(a["w_out"][0], 512),
        "w_mlp": w_mlp, "wgate": wgate,
        "ck": ck, "cv": a["cv"][0].reshape(NPOOL, PAGE, WIDTH), "ci": a["ci"][0], "steps": steps, "ptT": np.asarray(page_table).T,
        "ident": np.eye(P, dtype=f4), "rope": rope, "causal": causal, "ind": ind, "newmask": newmask, "keyoff": keyoff,
    }
    arrays = {f"in_{k}": np.ascontiguousarray(x) for k, x in arrays.items()}
    nc = bacc.Bacc("TRN2", target_bir_lowering=False, num_devices=1)
    args = [nc.dram_tensor(k, x.shape, mybir.dt.from_np(x.dtype), kind="ExternalInput").ap() for k, x in arrays.items()]
    outs = [(P, KT, NT), (P, CT, NT), (NT, WIDTH), (HD, NT), (P, CT, 36)]
    for i, shape in enumerate(outs):
        args.append(nc.dram_tensor(f"out_{i}", shape, F32, kind="ExternalOutput").ap())
    build(nc, *args)
    r = run(nc, [arrays], core_ids=[0]).results[0]
    yT, kT, v, kiT, lru = (r[f"out_{i}"] for i in range(len(outs)))

    y = yT.transpose(2, 1, 0).reshape(NT, D_MODEL)
    k = kT.transpose(2, 1, 0).reshape(NT, WIDTH)
    ki = kiT.T
    st = lru.transpose(2, 1, 0).reshape(36, WIDTH)
    return (y[:SEQ].reshape(1, SEQ, D_MODEL), y[SEQ:].reshape(DEC_BATCH, DEC_SEQ, D_MODEL),
            k[:SEQ].reshape(1, 1, SEQ, NH, HD), v[:SEQ].reshape(1, 1, SEQ, NH, HD), ki[:SEQ].reshape(1, 1, SEQ, HD),
            st[27].reshape(1, 1, WIDTH), st[0:3].reshape(1, 1, 3, WIDTH),
            k[SEQ:].reshape(1, DEC_BATCH, DEC_SEQ, NH, HD), v[SEQ:].reshape(1, DEC_BATCH, DEC_SEQ, NH, HD),
            ki[SEQ:].reshape(1, DEC_BATCH, DEC_SEQ, HD),
            st[28:36].reshape(1, DEC_BATCH, WIDTH), st[3:27].reshape(1, DEC_BATCH, 3, WIDTH))
```
